# Optimizing a Trainium2 kernel written in Bass

```python
import math
import jax, jax.numpy as jnp
from jax import lax
import numpy as np

D_MODEL = 1024
BATCH = 1
SEQ = 512
DEPTH = 1

CHUNK = 64
QBLOCK = 128
MIX_WIDTH = D_MODEL
DIFF_HEADS = 4
DIFF_DH = 64
DIFF_VD = 2 * DIFF_DH
FOX_HEADS = 8
FOX_DH = 64
ROPE_THETA = 500000.0
ROPE_DIM = DIFF_DH // 4
D_FF = ((8 * D_MODEL // 3 + 255) // 256) * 256
EPS = 1e-5
NEG = -1e30

DIFF_QK_W = DIFF_HEADS * 2 * DIFF_DH
DIFF_V_W = DIFF_HEADS * DIFF_VD
FOX_W = FOX_HEADS * FOX_DH
PROJ_W = 2 * DIFF_QK_W + DIFF_V_W + 3 * FOX_W + FOX_HEADS
SPLITS = (DIFF_QK_W,
          2 * DIFF_QK_W,
          2 * DIFF_QK_W + DIFF_V_W,
          2 * DIFF_QK_W + DIFF_V_W + FOX_W,
          2 * DIFF_QK_W + DIFF_V_W + 2 * FOX_W,
          2 * DIFF_QK_W + DIFF_V_W + 3 * FOX_W)


def rmsnorm(x, g):
    xf = x.astype(jnp.float32)
    y = xf * lax.rsqrt(jnp.mean(xf * xf, axis=-1, keepdims=True) + EPS)
    return (y * g.astype(jnp.float32)).astype(x.dtype)

def rope_partial(t, cos, sin):
    half = ROPE_DIM // 2
    shp = (1, t.shape[1]) + (1,) * (t.ndim - 3) + (half,)
    c = cos.reshape(shp).astype(t.dtype)
    s = sin.reshape(shp).astype(t.dtype)
    t1 = t[..., :half]
    t2 = t[..., half:ROPE_DIM]
    return jnp.concatenate([t1 * c - t2 * s, t2 * c + t1 * s, t[..., ROPE_DIM:]], axis=-1)

def to_blocks(t, nb):
    b, _, h, d = t.shape
    return t.reshape(b, nb, QBLOCK, h, d).transpose(1, 0, 3, 2, 4)

def from_blocks(t):
    nb, b, h, q, d = t.shape
    return t.transpose(1, 0, 3, 2, 4).reshape(b, nb * q, h * d)

def first_inputs(seed: int = 0) -> dict:
    key = jax.random.key(seed)
    ks = jax.random.split(key, 16)
    f32 = jnp.float32
    nrm = lambda k, shp, s: jax.random.normal(k, shp, f32) * s
    return {
        "x": jax.random.normal(ks[0], (BATCH, SEQ, D_MODEL), f32),
        "norm1_g": 1.0 + nrm(ks[1], (DEPTH, D_MODEL), 0.02),
        "w_in": nrm(ks[2], (DEPTH, D_MODEL, PROJ_W), D_MODEL ** -0.5),
        "b_f": 3.0 + nrm(ks[3], (DEPTH, FOX_HEADS), 0.5),
        "lam_q1": nrm(ks[4], (DEPTH, DIFF_DH), 0.1),
        "lam_k1": nrm(ks[5], (DEPTH, DIFF_DH), 0.1),
        "lam_q2": nrm(ks[6], (DEPTH, DIFF_DH), 0.1),
        "lam_k2": nrm(ks[7], (DEPTH, DIFF_DH), 0.1),
        "subln_g": 1.0 + nrm(ks[8], (DEPTH, DIFF_VD), 0.02),
        "w_out": nrm(ks[9], (DEPTH, MIX_WIDTH, D_MODEL), MIX_WIDTH ** -0.5),
        "norm2_g": 1.0 + nrm(ks[10], (DEPTH, D_MODEL), 0.02),
        "w_gate": nrm(ks[11], (DEPTH, D_MODEL, D_FF), D_MODEL ** -0.5),
        "w_up": nrm(ks[12], (DEPTH, D_MODEL, D_FF), D_MODEL ** -0.5),
        "w_down": nrm(ks[13], (DEPTH, D_FF, D_MODEL), D_FF ** -0.5),
        "normf_g": 1.0 + nrm(ks[14], (D_MODEL,), 0.02),
    }

def first_block(x, norm1_g, w_in, b_f, lam_q1, lam_k1, lam_q2, lam_k2, subln_g, w_out,
              norm2_g, w_gate, w_up, w_down, normf_g):
    f32 = jnp.float32
    B, S, _ = x.shape
    nb = S // QBLOCK
    pos = jnp.arange(S, dtype=jnp.int32)
    inv_freq = ROPE_THETA ** (-jnp.arange(0, ROPE_DIM, 2, dtype=f32) / ROPE_DIM)
    ang = pos.astype(f32)[:, None] * inv_freq[None, :]
    cos, sin = jnp.cos(ang), jnp.sin(ang)
    k_chunk = pos // CHUNK
    scale_d = DIFF_DH ** -0.5
    scale_f = FOX_DH ** -0.5

    for l in range(DEPTH):
        lam_init = 0.8 - 0.6 * math.exp(-0.3 * l)
        h = rmsnorm(x, norm1_g[l])
        proj = jnp.einsum('bsd,de->bse', h, w_in[l])
        dq, dk, dv, fq, fk, fv, fg = jnp.split(proj, SPLITS, axis=-1)

        dq = rope_partial(dq.reshape(B, S, DIFF_HEADS, 2, DIFF_DH), cos, sin)
        dk = rope_partial(dk.reshape(B, S, DIFF_HEADS, 2, DIFF_DH), cos, sin)
        dv_t = dv.reshape(B, S, DIFF_HEADS, DIFF_VD).transpose(0, 2, 1, 3)
        k1 = dk[:, :, :, 0].transpose(0, 2, 1, 3)
        k2 = dk[:, :, :, 1].transpose(0, 2, 1, 3)
        lam = (jnp.exp(jnp.sum(lam_q1[l].astype(f32) * lam_k1[l].astype(f32)))
               - jnp.exp(jnp.sum(lam_q2[l].astype(f32) * lam_k2[l].astype(f32)))
               + lam_init)

        fq = fq.reshape(B, S, FOX_HEADS, FOX_DH)
        fk_t = fk.reshape(B, S, FOX_HEADS, FOX_DH).transpose(0, 2, 1, 3)
        fv_t = fv.reshape(B, S, FOX_HEADS, FOX_DH).transpose(0, 2, 1, 3)
        log_f = jax.nn.log_sigmoid((fg + b_f[l]).astype(f32))
        cum = jnp.cumsum(log_f, axis=1).transpose(0, 2, 1)
        cum_blocks = cum.reshape(B, FOX_HEADS, nb, QBLOCK).transpose(2, 0, 1, 3)

        def block(args):
            i, q1b, q2b, qfb, cqb = args
            qpos = i * QBLOCK + jnp.arange(QBLOCK, dtype=jnp.int32)
            chunk_mask = k_chunk[None, :] <= (qpos // CHUNK)[:, None]
            causal = pos[None, :] <= qpos[:, None]
            s1 = jnp.einsum('bhqd,bhkd->bhqk', q1b, k1, preferred_element_type=f32) * scale_d
            s2 = jnp.einsum('bhqd,bhkd->bhqk', q2b, k2, preferred_element_type=f32) * scale_d
            p = (jax.nn.softmax(jnp.where(chunk_mask, s1, NEG), axis=-1)
                 - lam * jax.nn.softmax(jnp.where(chunk_mask, s2, NEG), axis=-1))
            od = jnp.einsum('bhqk,bhkd->bhqd', p.astype(dv_t.dtype), dv_t)
            sf = (jnp.einsum('bhqd,bhkd->bhqk', qfb, fk_t, preferred_element_type=f32) * scale_f
                  + cqb[:, :, :, None] - cum[:, :, None, :])
            pf = jax.nn.softmax(jnp.where(causal, sf, NEG), axis=-1)
            of = jnp.einsum('bhqk,bhkd->bhqd', pf.astype(fv_t.dtype), fv_t)
            return od, of

        od_b, of_b = lax.map(block, (jnp.arange(nb, dtype=jnp.int32),
                                     to_blocks(dq[:, :, :, 0], nb),
                                     to_blocks(dq[:, :, :, 1], nb),
                                     to_blocks(fq, nb),
                                     cum_blocks))
        od_b = rmsnorm(od_b, subln_g[l]) * (1.0 - lam_init)
        mix = jnp.concatenate([from_blocks(od_b), from_blocks(of_b)], axis=-1)
        x = x + jnp.einsum('bse,ed->bsd', mix, w_out[l])

        h2 = rmsnorm(x, norm2_g[l])
        g = jnp.einsum('bsd,df->bsf', h2, w_gate[l])
        u = jnp.einsum('bsd,df->bsf', h2, w_up[l])
        x = x + jnp.einsum('bsf,fd->bsd', jax.nn.silu(g) * u, w_down[l])

    return rmsnorm(x, normf_g)


DEPTH_2 = 2

N_A = DEPTH_2 // 2
N_B = DEPTH_2 - N_A
CONV_W = 3
D_FF_2 = 4 * D_MODEL
N_HEADS = 8
QK_NOPE = 128
QK_ROPE = 64
V_HEAD = 128
Q_LORA = 384
KV_LORA = 256
ROPE_THETA_2 = 10000.0
Q_BLOCK = 128
NORM_EPS = 1e-6


def rmsnorm_2(x, g):
    xf = x.astype(jnp.float32)
    y = xf * lax.rsqrt(jnp.mean(xf * xf, axis=-1, keepdims=True) + NORM_EPS)
    return (y * g.astype(jnp.float32)).astype(x.dtype)

def modulate(h, shift, scale):
    return h * (1 + scale[:, None, :]) + shift[:, None, :]

def rope_tables(seq_len, dim, dtype):
    inv_freq = 1.0 / (ROPE_THETA_2 ** (jnp.arange(0, dim, 2, dtype=jnp.float32) / dim))
    ang = jnp.arange(seq_len, dtype=jnp.float32)[:, None] * inv_freq[None, :]
    return jnp.cos(ang).astype(dtype), jnp.sin(ang).astype(dtype)

def apply_rope(x, cos, sin):
    half = x.shape[-1] // 2
    x1, x2 = x[..., :half], x[..., half:]
    return jnp.concatenate([x1 * cos - x2 * sin, x2 * cos + x1 * sin], axis=-1)

def short_conv_mixer(h, w_in, w_conv, b_conv, w_out):
    bcx = h @ w_in
    b_gate, c_gate, xh = jnp.split(bcx, 3, axis=-1)
    u = c_gate * xh
    conv = lax.conv_general_dilated(
        u, w_conv[:, None, :], window_strides=(1,), padding=[(CONV_W - 1, 0)],
        dimension_numbers=("NWC", "WIO", "NWC"), feature_group_count=D_MODEL) + b_conv
    return (b_gate * conv) @ w_out

def squared_relu_mlp(h, w_up, w_down):
    return jnp.square(jax.nn.relu(h @ w_up)) @ w_down

def shared_kv(x, c_act, kv_ada_w, kv_ada_b, kv_norm_g, kv_a_w, kv_a_norm_g, kv_b_w, cos, sin):
    B, S, _ = x.shape
    shift, scale = jnp.split(c_act @ kv_ada_w + kv_ada_b, 2, axis=-1)
    hkv = modulate(rmsnorm_2(x, kv_norm_g), shift, scale)
    kv_a = hkv @ kv_a_w
    c_kv = rmsnorm_2(kv_a[..., :KV_LORA], kv_a_norm_g)
    k_pe = apply_rope(kv_a[..., KV_LORA:], cos, sin)
    kv = (c_kv @ kv_b_w).reshape(B, S, N_HEADS, QK_NOPE + V_HEAD)
    return kv[..., :QK_NOPE], kv[..., QK_NOPE:], k_pe

def mla_mixer(h, q_a_w, q_a_norm_g, q_b_w, o_w, k_nope, v, k_pe, cos, sin):
    B, S, _ = h.shape
    q = (rmsnorm_2(h @ q_a_w, q_a_norm_g) @ q_b_w).reshape(B, S, N_HEADS, QK_NOPE + QK_ROPE)
    sm_scale = 1.0 / math.sqrt(QK_NOPE + QK_ROPE)
    q_nope = q[..., :QK_NOPE] * sm_scale
    q_pe = apply_rope(q[..., QK_NOPE:], cos[:, None, :], sin[:, None, :]) * sm_scale
    outs = []
    for i in range(S // Q_BLOCK):
        q0, k_end = i * Q_BLOCK, (i + 1) * Q_BLOCK
        qn = q_nope[:, q0:k_end]
        qp = q_pe[:, q0:k_end]
        s = (jnp.einsum("bqhd,bkhd->bhqk", qn, k_nope[:, :k_end])
             + jnp.einsum("bqhr,bkr->bhqk", qp, k_pe[:, :k_end])).astype(jnp.float32)
        q_chunk = np.arange(q0, k_end) // CHUNK
        k_chunk = np.arange(k_end) // CHUNK
        mask = k_chunk[None, :] <= q_chunk[:, None]
        s = jnp.where(mask[None, None], s, jnp.finfo(jnp.float32).min)
        p = jax.nn.softmax(s, axis=-1).astype(v.dtype)
        outs.append(jnp.einsum("bhqk,bkhd->bqhd", p, v[:, :k_end]))
    o = jnp.concatenate(outs, axis=1).reshape(B, S, N_HEADS * V_HEAD)
    return o @ o_w

def second_inputs(seed: int = 0) -> dict:
    key = jax.random.key(seed)
    ks = jax.random.split(key, 24)
    D = D_MODEL
    f32 = jnp.float32

    def w(k, shape, fan_in):
        return jax.random.normal(k, shape, f32) * (fan_in ** -0.5)

    def gain(k, shape):
        return 1.0 + 0.05 * jax.random.normal(k, shape, f32)

    return {
        "x": jax.random.normal(ks[0], (BATCH, SEQ, D), f32),
        "c": jax.random.normal(ks[1], (BATCH, D), f32),
        "ada_w": w(ks[2], (DEPTH_2, D, 6 * D), D) * 0.5,
        "ada_b": 0.02 * jax.random.normal(ks[3], (DEPTH_2, 6 * D), f32),
        "norm_g": gain(ks[4], (DEPTH_2, 4, D)),
        "conv_in_w": w(ks[5], (N_A, D, 3 * D), D),
        "conv_w": w(ks[6], (N_A, CONV_W, D), CONV_W),
        "conv_b": 0.02 * jax.random.normal(ks[7], (N_A, D), f32),
        "conv_out_w": w(ks[8], (N_A, D, D), D),
        "kv_ada_w": w(ks[9], (D, 2 * D), D) * 0.5,
        "kv_ada_b": 0.02 * jax.random.normal(ks[10], (2 * D,), f32),
        "kv_norm_g": gain(ks[11], (D,)),
        "kv_a_w": w(ks[12], (D, KV_LORA + QK_ROPE), D),
        "kv_a_norm_g": gain(ks[13], (KV_LORA,)),
        "kv_b_w": w(ks[14], (KV_LORA, N_HEADS * (QK_NOPE + V_HEAD)), KV_LORA),
        "q_a_w": w(ks[15], (N_B, D, Q_LORA), D),
        "q_a_norm_g": gain(ks[16], (N_B, Q_LORA)),
        "q_b_w": w(ks[17], (N_B, Q_LORA, N_HEADS * (QK_NOPE + QK_ROPE)), Q_LORA),
        "attn_o_w": w(ks[18], (N_B, N_HEADS * V_HEAD, D), N_HEADS * V_HEAD),
        "mlp_up_w": w(ks[19], (DEPTH_2, D, D_FF_2), D),
        "mlp_down_w": w(ks[20], (DEPTH_2, D_FF_2, D), D_FF_2),
    }

def second_block(x, c, ada_w, ada_b, norm_g, conv_in_w, conv_w, conv_b, conv_out_w,
              kv_ada_w, kv_ada_b, kv_norm_g, kv_a_w, kv_a_norm_g, kv_b_w,
              q_a_w, q_a_norm_g, q_b_w, attn_o_w, mlp_up_w, mlp_down_w):
    S = x.shape[1]
    c_act = jax.nn.silu(c)
    cos, sin = rope_tables(S, QK_ROPE, x.dtype)
    k_nope = v = k_pe = None
    for l in range(DEPTH_2):
        mod = c_act @ ada_w[l] + ada_b[l]
        sh_m, sc_m, g_m, sh_f, sc_f, g_f = jnp.split(mod, 6, axis=-1)
        h = modulate(rmsnorm_2(x, norm_g[l, 0]), sh_m, sc_m)
        if l < N_A:
            y = short_conv_mixer(h, conv_in_w[l], conv_w[l], conv_b[l], conv_out_w[l])
        else:
            if l == N_A:
                k_nope, v, k_pe = shared_kv(x, c_act, kv_ada_w, kv_ada_b, kv_norm_g,
                                            kv_a_w, kv_a_norm_g, kv_b_w, cos, sin)
            j = l - N_A
            y = mla_mixer(h, q_a_w[j], q_a_norm_g[j], q_b_w[j], attn_o_w[j],
                          k_nope, v, k_pe, cos, sin)
        x = x + g_m[:, None, :] * rmsnorm_2(y, norm_g[l, 1])
        h = modulate(rmsnorm_2(x, norm_g[l, 2]), sh_f, sc_f)
        y = squared_relu_mlp(h, mlp_up_w[l], mlp_down_w[l])
        x = x + g_f[:, None, :] * rmsnorm_2(y, norm_g[l, 3])
    return x


def setup_inputs(seed=0):
    out = dict(first_inputs(seed))
    for name, value in second_inputs(seed + 1).items():
        if name != "x":
            out[name + "_2"] = value
    return out


def reference(
    x, norm1_g, w_in, b_f, lam_q1, lam_k1, lam_q2, lam_k2, subln_g, w_out, norm2_g, w_gate,
    w_up, w_down, normf_g, c_2, ada_w_2, ada_b_2, norm_g_2, conv_in_w_2, conv_w_2, conv_b_2,
    conv_out_w_2, kv_ada_w_2, kv_ada_b_2, kv_norm_g_2, kv_a_w_2, kv_a_norm_g_2, kv_b_w_2,
    q_a_w_2, q_a_norm_g_2, q_b_w_2, attn_o_w_2, mlp_up_w_2, mlp_down_w_2,
):
    x = first_block(
        x, norm1_g, w_in, b_f, lam_q1, lam_k1, lam_q2, lam_k2, subln_g, w_out, norm2_g, w_gate,
        w_up, w_down, normf_g,
    )
    return second_block(
        x, c_2, ada_w_2, ada_b_2, norm_g_2, conv_in_w_2, conv_w_2, conv_b_2, conv_out_w_2,
        kv_ada_w_2, kv_ada_b_2, kv_norm_g_2, kv_a_w_2, kv_a_norm_g_2, kv_b_w_2, q_a_w_2,
        q_a_norm_g_2, q_b_w_2, attn_o_w_2, mlp_up_w_2, mlp_down_w_2,
    )


_drawn_inputs = setup_inputs


def setup_inputs(seed=0):
    import zlib

    import numpy as np

    out = dict(_drawn_inputs(seed))
    spreads = {}
    factors = {'lam_k1': 3.067,
     'lam_q2': 3.25,
     'subln_g': 4.577,
     'norm2_g': 4.202,
     'normf_g': 2.688,
     'conv_b_2': 23.231,
     'kv_ada_b_2': 4.329,
     'kv_norm_g_2': 5.38,
     'kv_a_norm_g_2': 4.043,
     'q_a_norm_g_2': 8.0}
    for name, (base, spread) in spreads.items():
        noise = np.random.default_rng([zlib.crc32(name.encode()), seed]).standard_normal(out[name].shape)
        drawn = base * np.exp(spread * noise) if base else spread * noise
        out[name] = __import__('jax').numpy.asarray(drawn.astype(out[name].dtype))
    for name, factor in factors.items():
        out[name] = (out[name] * factor).astype(out[name].dtype)
    return out
```

```python
from contextlib import ExitStack

import numpy as np

import concourse.bass as bass
from concourse import mybir

F32 = mybir.dt.float32
F32R = mybir.dt.float32r
ALU = mybir.AluOpType
ACT = mybir.ActivationFunctionType
AX_X = mybir.AxisListType.X

P = 128
S = 512
D = 1024
DT = D // P
QB = S // P
D_FF = 2816
EPS1, EPS2 = 1e-5, 1e-6
NEG = -1e30
LAM_INIT = 0.2

RAW = 4
SPLIT = 4
AHEAD = 3
BANKS = 4
PT_BANK, O_BANK, AUX_BANK = 4, 6, 7
ADA_COLS = 512
ADA_GROUPS = (6 + 2 + 6) * D // ADA_COLS
ADA_SLOTS = 4
MOD_PER_GROUP = ADA_COLS // P

COLS = {}
_at = 0
for _name, _n in (("norm1", 8), ("norm2", 8), ("normf", 8), ("norm_g2", 64), ("kv_norm", 8), ("kv_a_norm", 2),
                  ("q_a_norm", 3), ("subln", 1), ("conv_w", 24), ("conv_b", 8), ("ada_b", 112), ("c", 8),
                  ("b_f", 8), ("lam", 256)):
    COLS[_name] = _at
    _at += _n
PARAMS = _at
CONST = {}
_at = 0
for _name, _n in (("ident", 128), ("tri", 512), ("chunk_mask", 128), ("causal_mask", 128),
                  ("rot", 128), ("cos", 512), ("sin", 512)):
    CONST[_name] = _at
    _at += _n
CONSTS = _at
ROPE_AT = CONST["rot"]
ROPE_COLS = CONSTS - ROPE_AT


def make_plan():
    counts = dict(n=0, o=0, gate=0, tap=0, sqv=0, ss=0, val=0, hi=0, rhs=0, xup=0, sqa=0, aux=0, rstd=0,
                  mod=0)
    plan = []

    def add(kind, inc=None, **about):
        plan.append(dict(kind=kind, at=dict(counts), **about))
        for k, v in (inc or {}).items():
            counts[k] += v

    def gemm(evac, nblk, rhs, r0, nk=8, nout=1, rhs_at=0, **about):
        inc = dict(n=nblk, o=nblk * nout)
        if evac == "acc" and about.get("sq"):
            inc.update(sqv=nblk, ss=1 + nblk)
        if evac == "gateup":
            inc.update(gate=nblk // 2, hi=nblk // 2, rhs=nblk // 2)
        if evac == "relu2":
            inc.update(gate=nblk, hi=nblk, rhs=nblk)
        if evac == "conv":
            inc.update(gate=nblk // 3, tap=1 + nblk, hi=nblk // 3, rhs=nblk // 3)
        add("gemm", inc, evac=evac, nblk=nblk, rhs=rhs, r0=r0, nk=nk, nout=nout, rhs_at=rhs_at, **about)

    def sumsq(src, at, nch, mean):
        add("sumsq", dict(sqa=nch, aux=nch), src=src, src_at=at, nch=nch, mean=mean)

    def total():
        add("total", dict(aux=1))

    def rstd(eps):
        add("rstd", dict(rstd=1), eps=eps)

    def norm(dst, src="x", src_at=0, nch=8, dst_at=0, gain=None, shift=None):
        r0 = counts["rhs"]
        add("norm", dict(val=nch, hi=nch, rhs=nch), dst=dst, src=src, src_at=src_at, nch=nch, dst_at=dst_at,
            gain=gain, shift=shift)
        return r0

    def update(gain, last=False):
        add("update", dict(val=8, xup=8, **({} if last else dict(sqa=8, aux=8))), gain=gain, last=last)

    def modulation(groups):
        for _ in range(groups):
            add("mod", dict(mod=1))

    sumsq("x", 0, 8, 1024)
    rstd(EPS1)
    h = norm("h", gain="norm1")
    gemm("store", 17, "h", h, dst="proj", dst_at=0)
    add("rope1")
    add("forget1")
    modulation(1)
    gemm("store", 8, "h", h, dst="scratch", dst_at=0)
    add("vtrans")
    add("forget2")
    modulation(2)
    mix = counts["rhs"]
    add("attn", dict(hi=4, rhs=4), name="diff")
    add("forget3")
    add("attn", dict(hi=4, rhs=4), name="fox")
    modulation(1)
    gemm("acc", 8, "h", mix, dst="x", first=False, sq=True)
    total()
    rstd(EPS1)
    h = norm("h", gain="norm2")
    for g, nk in enumerate((8, 8, 6)):
        hid = counts["rhs"]
        gemm("gateup", 2 * nk, "h", h)
        modulation(1)
        gemm("acc", 8, "hid", hid, nk=nk, dst="x", first=False, sq=g == 2)
        modulation(1)
    modulation(2)
    add("modcols0")
    total()
    rstd(EPS1)
    add("final1", dict(xup=8, sqa=8, aux=8))
    rstd(EPS2)
    h = norm("h", gain="g_m0", shift=0)
    hid = counts["rhs"]
    gemm("conv", 24, "h", h)
    modulation(2)
    gemm("acc", 8, "hid", hid, dst="y", first=True, sq=True)
    modulation(2)
    total()
    rstd(EPS2)
    update("r_m0")
    rstd(EPS2)
    h = norm("h", gain="g_f0", shift=24)

    def mlp(h):
        for g in range(4):
            hid = counts["rhs"]
            gemm("relu2", 8, "h", h)
            if counts["mod"] < ADA_GROUPS:
                modulation(2)
            gemm("acc", 8, "hid", hid, dst="y", first=g == 0, sq=g == 3)
            if counts["mod"] < ADA_GROUPS:
                modulation(1)

    mlp(h)
    add("modcols1")
    total()
    rstd(EPS2)
    update("r_f0")
    rstd(EPS2)
    hkv = norm("hid", gain="g_kv", shift=48)
    h = norm("h", gain="g_m1", shift=64)
    gemm("store", 3, "hid", hkv, dst="kv_a", dst_at=0)
    gemm("store", 3, "h", h, dst="scratch", dst_at=0)
    sumsq("scratch", 3, 2, 256)
    rstd(EPS2)
    c_kv = norm("h", src="scratch", src_at=3, nch=2, dst_at=3, gain="kv_a_norm")
    sumsq("scratch", 0, 3, 384)
    rstd(EPS2)
    q_a = norm("h", src="scratch", src_at=0, nch=3, dst_at=0, gain="q_a_norm")
    gemm("store", 2, "h", c_kv, nk=2, nout=4, rhs_at=3, dst="proj", dst_at=0)
    gemm("store", 2, "h", c_kv, nk=2, nout=4, rhs_at=3, dst="scratch", dst_at=0)
    add("vtrans")
    gemm("store", 6, "h", q_a, nk=3, nout=2, dst="proj", dst_at=8)
    add("rope2")
    mix = counts["rhs"]
    add("attn", dict(hi=8, rhs=8), name="mla")
    gemm("acc", 8, "h", mix, dst="y", first=True, sq=True)
    total()
    rstd(EPS2)
    update("r_m1")
    rstd(EPS2)
    h = norm("h", gain="g_f1", shift=88)
    mlp(h)
    total()
    rstd(EPS2)
    update("r_f1", last=True)
    assert counts["mod"] == ADA_GROUPS, counts["mod"]
    return plan, counts


PLAN, TOTALS = make_plan()
NB = TOTALS["n"]
LAST_GEMM = max(i for i, s in enumerate(PLAN) if s["kind"] == "gemm")

ATTN = dict(
    diff=dict(heads=4, mats=2, scale=64 ** -0.5, per_tile=1, tiles=4),
    fox=dict(heads=8, mats=1, scale=64 ** -0.5, per_tile=2, tiles=4),
    mla=dict(heads=8, mats=1, scale=192 ** -0.5, per_tile=1, tiles=8),
)


class Step:

    def __init__(self, stage, b, j, turn, body):
        self.b, self.j = b, j
        self.n = stage["at"]["n"] + b
        self.n0 = stage["at"]["n"] + j
        self.turn, self.body = turn, body
        self.o = stage["at"]["o"] + b * stage["nout"]
        self.o0 = stage["at"]["o"] + j * stage["nout"]

    def rounds(self, ahead, ring):
        return (self.n0 + ahead) // ring + 1 + self.turn * (self.body // ring)

    def of(self, per):
        return self.j // per + self.turn * (self.body // per)


def steps(eng, stage, do, last=False):
    nblk = stage["nblk"]
    body = 12 if stage["evac"] == "conv" else 4
    turns = nblk // body
    first = 1 if stage["at"]["n"] == 0 else 0
    for b in range(first * body):
        do(Step(stage, b, b, 0, body))
    if last:
        turns -= 1
    if turns >= 2:
        with eng.Fori(first, turns) as i:
            for j in range(body):
                do(Step(stage, body * i + j, j, i, body))
        done = turns * body
    else:
        done = 0
    for b in range(done, nblk):
        do(Step(stage, b, b, 0, body))


def tile_of(t, i):
    if isinstance(i, int):
        return t[:, i, :]
    return t[:, bass.ds(i, 1), :].rearrange("p a n -> p (a n)")


def col_of(t, i):
    if isinstance(i, int):
        return t[:, i:i + 1]
    return t[:, bass.ds(i, 1)]


def build(nc, xT, wstream, ada, params, consts, rope2, outT):
    ctx = ExitStack()
    with ctx:
        place = [nc.sbuf_base if not callable(nc.sbuf_base) else nc.sbuf_base()]
        place[0] = (place[0] + 63) // 64 * 64

        def at(name, shape, dtype, where):
            return nc.alloc_sbuf_tensor_at(name, shape, dtype, offset=where)

        def sb(name, shape, dtype=F32):
            where = place[0]
            place[0] += (int(np.prod(shape[1:])) * 4 + 63) // 64 * 64
            return at(name, shape, dtype, where)

        x = sb("x", [P, DT, S])
        y_at = place[0]
        y = sb("y", [P, DT, S])
        vtok = at("vtok", [P, DT, QB, P], F32, y_at)
        h_hi = sb("h_hi", [P, DT, S], F32R)
        h_lo = sb("h_lo", [P, DT, S], F32R)
        proj_at = place[0]
        proj = sb("proj", [P, 21, S])
        hid_hi = at("hid_hi", [P, DT, S], F32R, proj_at)
        hid_lo = at("hid_lo", [P, DT, S], F32R, proj_at + DT * S * 4)
        w_raw = sb("w_raw", [P, RAW, D])
        w_hi = sb("w_hi", [P, SPLIT, D], F32R)
        w_lo = sb("w_lo", [P, SPLIT, D], F32R)
        conv_u = at("conv_u", [P, S + 2], F32, place[0])
        scratch = sb("scratch", [P, 10, S])
        ss = sb("ss", [P, S])
        rstd = sb("rstd", [P, S])
        ada_raw = sb("ada_raw", [P, ADA_SLOTS, ADA_COLS])
        ada_acc = sb("ada_acc", [P, 2, ADA_COLS])
        par = sb("par", [P, PARAMS])
        con = sb("con", [P, CONSTS])
        mean = {n: sb(f"mean{n}", [P, P]) for n in (1024, 256, 384, 128)}
        ones_col = sb("ones_col", [P, 1])
        eps = {e: sb(f"eps{n}", [P, 1]) for n, e in enumerate((EPS1, EPS2))}
        c_act = sb("c_act", [P, 8])
        mod = sb("mod", [P, ADA_GROUPS * MOD_PER_GROUP])
        gains = sb("gains", [P, 8, DT])
        subln_gain = sb("subln_gain", [P, 1])
        lam_prod = sb("lam_prod", [P, 2, 64])
        lam_sum = sb("lam_sum", [P, 2])
        lam_exp = sb("lam_exp", [P, 2])
        neg_lam = sb("neg_lam", [P, 1])
        lam_diff = sb("lam_diff", [P, 1])
        fgate = sb("fgate", [P, QB, 8])
        fgate_a = sb("fgate_a", [P, QB, 8])
        fgate_b = sb("fgate_b", [P, QB, 8])
        log_f = sb("log_f", [P, QB, 8])
        cum_tok = sb("cum_tok", [P, QB, 8])
        neg_cum = proj[0:8, 17, :]
        row_max = sb("row_max", [P, 4])
        neg_max = sb("neg_max", [P, 4])
        row_sum = sb("row_sum", [P, 4])
        row_inv = sb("row_inv", [P, 4])
        lam_inv = sb("lam_inv", [P, 2])

        psum = ctx.enter_context(nc.psum_tensor("psum", [P, 8, S], F32))

        def sem(name):
            return ctx.enter_context(nc.semaphore(name))

        raw_loaded = [sem(f"raw_loaded{i}") for i in range(RAW)]
        whi_done = sem("whi_done")
        wlo_done = sem("wlo_done")
        out_done = sem("out_done")
        bank_free = sem("bank_free")
        gate_done = sem("gate_done")
        tap_done = sem("tap_done")
        sqv_done = sem("sqv_done")
        ss_done = sem("ss_done")
        val_done = sem("val_done")
        hi_done = sem("hi_done")
        rhs_ready = sem("rhs_ready")
        x_done = sem("x_done")
        sqa_done = sem("sqa_done")
        aux_done = sem("aux_done")
        std_done = sem("std_done")
        rstd_done = sem("rstd_done")
        ada_loaded = [sem(f"ada_loaded{i}") for i in range(2)]
        ada_scaled = sem("ada_scaled")
        ada_used = sem("ada_used")
        acc_free = sem("acc_free")
        mod_done = sem("mod_done")
        gains_done = sem("gains_done")
        c_done = sem("c_done")
        act_settled = sem("act_settled")
        dve_settled = sem("dve_settled")
        x_loaded = sem("x_loaded")
        par_loaded = sem("par_loaded")
        con_loaded = sem("con_loaded")
        rope_loaded = sem("rope_loaded")
        const_done = sem("const_done")
        small_done = sem("small_done")
        lam_done = sem("lam_done")
        out_stored = sem("out_stored")
        rot_done = sem("rot_done")
        rope_mul = sem("rope_mul")
        rope_done = sem("rope_done")
        vt_done = sem("vt_done")
        v_done = sem("v_done")
        fg_turned = sem("fg_turned")
        fg_step = sem("fg_step")
        fg_exp = sem("fg_exp")
        logf_done = sem("logf_done")
        cum_psum = sem("cum_psum")
        cum_done = sem("cum_done")
        nck_psum = sem("nck_psum")
        nck_done = sem("nck_done")
        names = ("scores", "masked", "maxed", "negmax", "exp", "inv", "prob", "turned", "pt", "pv", "o_copied",
                 "o_sq", "o_ss", "o_free", "o_rstd", "o_val", "biased", "lam")
        att = {a: {n: sem(f"{a}_{n}") for n in names} for a in ATTN}

        def col(name, i=0, n=1):
            return par[:, COLS[name] + i:COLS[name] + i + n]

        def cst(name, n, i=0, rows=P):
            return con[0:rows, CONST[name] + i:CONST[name] + i + n]

        ident = cst("ident", 128)
        GAIN = dict(g_m0=0, r_m0=1, g_f0=2, r_f0=3, g_kv=4, g_m1=5, r_m1=6, g_f1=7)
        r_f1 = sb("r_f1", [P, DT])

        def gain_of(name, c):
            if name == "r_f1":
                return r_f1[:, c:c + 1]
            if name in GAIN:
                return gains[:, GAIN[name], c:c + 1]
            return col(name, c)

        def operand(name):
            return dict(h=(h_hi, h_lo), hid=(hid_hi, hid_lo))[name]

        def stored(name, i):
            if name == "kv_a":
                return scratch[:, 3 + i, :] if i < 2 else proj[:, 20, :]
            return tile_of(dict(proj=proj, scratch=scratch, x=x, y=y)[name], i)

        block = ctx.enter_context(nc.Block())

        @block.sync
        def _(sp):
            for c in range(DT):
                sp.dma_start(x[:, c, :], xT[c]).then_inc(x_loaded, 16)
                if c == 0:
                    sp.dma_start(par[:, :], params).then_inc(par_loaded, 16)
                    sp.dma_start(con[:, :], consts).then_inc(con_loaded, 16)
            for n in range(RAW):
                sp.dma_start(w_raw[:, n, :], wstream[n]).then_inc(raw_loaded[n], 16)

            def load(n, slot):
                sp.wait_ge(wlo_done, n + 1 - RAW)
                src = wstream[n] if isinstance(n, int) else wstream[bass.ds(n, 1)].rearrange("a p m -> (a p) m")
                sp.dma_start(w_raw[:, slot, :], src).then_inc(raw_loaded[slot], 16)

            with sp.Fori(1, NB // RAW) as i:
                for j in range(RAW):
                    load(RAW * i + j, j)
            for n in range(NB // RAW * RAW, NB):
                load(n, n % RAW)
            for s in PLAN:
                if s["kind"] == "update" and s["last"]:
                    for c in range(DT):
                        sp.wait_ge(x_done, s["at"]["xup"] + c + 1)
                        sp.dma_start(outT[c], x[:, c, :]).then_inc(out_stored, 16)
            sp.wait_ge(out_stored, 16 * DT)

        @block.gpsimd
        def _(pool):
            def load(v, half):
                src = ada[v] if isinstance(v, int) else ada[bass.ds(v, 1)].rearrange("a p m -> (a p) m")
                pool.dma_start(ada_raw[:, 2 * half:2 * half + 2, :].rearrange("p a n -> p (a n)"), src)\
                    .then_inc(ada_loaded[half], 16)

            load(0, 0)
            load(1, 1)
            pool.wait_ge(c_done, 1)

            def two_groups(i, last):
                for v in range(DT):
                    g, acc = v // 4, ada_acc[:, v // 4, :]
                    if v % 4 == 0:
                        pool.wait_ge(acc_free, 2 * i + g + 1)
                    pool.wait_ge(ada_loaded[v % 2], 16 * (4 * i + v // 2 + 1))
                    for u in range(2 * v, 2 * v + 2):
                        k = u % DT
                        row = ada_raw[:, u % ADA_SLOTS, :]
                        c_k = c_act[:, k:k + 1].broadcast_to([P, ADA_COLS])
                        if k == 0:
                            pool.tensor_tensor(acc, row, c_k, ALU.mult).then_inc(ada_used, 1)
                        else:
                            pool.tensor_tensor(row, row, c_k, ALU.mult).then_inc(ada_scaled, 1)
                            pool.wait_ge(ada_scaled, (DT - 1) * (2 * i + g) + k)
                            pool.wait_ge(ada_used, 2 * DT * i + u)
                            pool.tensor_tensor(acc, acc, row, ALU.add).then_inc(ada_used, 1)
                    if not (last and v >= DT - 2):
                        pool.wait_ge(ada_used, 2 * DT * i + 2 * v + 2)
                        pool.wait_ge(c_done, 1)
                        load(DT * i + (v + 2), v % 2)

            with pool.Fori(0, ADA_GROUPS // 2 - 1) as i:
                two_groups(i, False)
            two_groups(ADA_GROUPS // 2 - 1, True)

        @block.scalar
        def _(act):
            act.wait_ge(const_done, 7)
            act.wait_ge(par_loaded, 16)
            act.activation(c_act[:, :], col("c", 0, 8), ACT.Silu).then_inc(c_done, 1)

            def split_hi(m_rounds, slot, out_wait):
                if out_wait is not None:
                    act.wait_ge(out_done, out_wait)
                act.wait_ge(raw_loaded[slot], 16 * m_rounds)
                act.activation(w_hi[:, slot, :], w_raw[:, slot, :], ACT.Copy).then_inc(whi_done, 1)

            def gemm(s, last):
                at_ = s["at"]
                evac = s["evac"]
                hi_out = operand("hid")[0]

                def step(t):
                    if not (last and isinstance(t.n, int) and t.n + AHEAD >= NB):
                        split_hi(t.rounds(AHEAD, RAW), (t.n0 + AHEAD) % SPLIT,
                                 None if isinstance(t.o, int) and t.o == 0 else t.o)
                    bank = psum[:, t.o0 % BANKS, :]
                    if evac == "gateup" and t.j % 2 == 0:
                        f = t.of(2)
                        act.wait_ge(out_done, t.o + 1)
                        act.wait_ge(bank_free, BANKS + t.o - 2)
                        act.activation(scratch[:, 2 + t.j // 2 % 2, :], bank, ACT.Silu).then_inc(gate_done, 1)
                    if evac == "gateup" and t.j % 2 == 1:
                        act.wait_ge(bank_free, BANKS + t.o + 1)
                        act.activation(tile_of(hi_out, t.of(2)), scratch[:, 8, :], ACT.Copy).then_inc(hi_done, 1)
                    if evac == "relu2":
                        act.wait_ge(out_done, t.o + 1)
                        act.wait_ge(bank_free, BANKS + t.o - 1)
                        act.activation(scratch[:, 2 + t.j % 2, :], bank, ACT.Relu).then_inc(gate_done, 1)
                        act.wait_ge(bank_free, BANKS + t.o + 1)
                        act.activation(tile_of(hi_out, t.b), scratch[:, 8, :], ACT.Copy).then_inc(hi_done, 1)
                    if evac == "conv" and t.j % 3 == 0:
                        act.wait_ge(out_done, t.o + 1)
                        act.wait_ge(bank_free, BANKS + t.o - 1)
                        act.activation(scratch[:, 2, :], bank, ACT.Copy).then_inc(gate_done, 1)
                    if evac == "conv" and t.j % 3 == 2:
                        act.wait_ge(bank_free, BANKS + t.o + 1)
                        act.activation(tile_of(hi_out, t.of(3)), scratch[:, 8, :], ACT.Copy).then_inc(hi_done, 1)

                steps(act, s, step, last)

            def squares(s, src, src_at, nch, x_from=None):
                for c in range(nch):
                    if x_from is not None:
                        act.wait_ge(x_done, x_from + c + 1)
                    if c >= 2:
                        act.wait_ge(aux_done, s["at"]["aux"] + c - 1)
                    act.activation(scratch[:, 5 + c % 2, :], stored(src, src_at + c), ACT.Square)\
                       .then_inc(sqa_done, 1)

            def norm(s):
                hi_out = operand(s["dst"])[0]
                for c in range(s["nch"]):
                    act.wait_ge(val_done, s["at"]["val"] + c + 1)
                    val = scratch[:, 7 + c % 3, :]
                    if s["shift"] is None:
                        act.activation(hi_out[:, s["dst_at"] + c, :], val, ACT.Copy).then_inc(hi_done, 1)
                    else:
                        act.activation(hi_out[:, s["dst_at"] + c, :], val, ACT.Identity,
                                       bias=mod[:, s["shift"] + c:s["shift"] + c + 1]).then_inc(hi_done, 1)

            def attention(s):
                a, e = ATTN[s["name"]], att[s["name"]]
                M, units = a["mats"], a["heads"] * QB
                upt = a["per_tile"] * QB

                def exps(i):
                    W = (i % QB + 1) * P
                    act.wait_ge(e["negmax"], M * (i + 1))
                    for m in range(M):
                        src = psum[:, 2 * (i % 2) + m, 0:W]
                        if s["name"] == "fox":
                            src = scratch[:, 8 + i % 2, 0:W]
                        c = 2 * (i % 2) + m
                        act.activation(scratch[:, 2 * (i % 2) + m, 0:W], src, ACT.Exp, bias=neg_max[:, c:c + 1],
                                       scale=a["scale"], accum_out=row_sum[:, c:c + 1]).then_inc(e["exp"], 1)

                def take_turned(i):
                    W = (i % QB + 1) * P
                    act.wait_ge(e["turned"], i + 1)
                    if i >= 2:
                        act.wait_ge(e["pv"], i - 1)
                    act.activation(scratch[:, 6 + i % 2, 0:W], psum[:, PT_BANK + i % 2, 0:W], ACT.Copy)\
                       .then_inc(e["pt"], 1)

                def finish(t):
                    act.wait_ge(e["pv"], upt * (t + 1))
                    O = psum[:, O_BANK, :]
                    if s["name"] != "diff":
                        c = t + (4 if s["name"] == "fox" else 0)
                        act.activation(h_hi[:, c, :], O, ACT.Copy).then_inc(hi_done, 1)
                    else:
                        if t >= 1:
                            act.wait_ge(e["o_val"], t)
                        act.activation(scratch[:, 8, :], O, ACT.Copy).then_inc(e["o_copied"], 1)
                        act.activation(scratch[:, 9, :], O, ACT.Square).then_inc(e["o_sq"], 1)

                def finish_diff(t):
                    act.wait_ge(e["o_ss"], t + 1)
                    act.activation(rstd[:, :], psum[:, AUX_BANK, :], ACT.Sqrt, bias=eps[EPS1][:, :])\
                       .then_inc(e["o_free"], 1)
                    act.wait_ge(e["o_val"], t + 1)
                    act.activation(h_hi[:, t, :], ss[:, :], ACT.Copy).then_inc(hi_done, 1)

                for i in range(units + 4):
                    if i >= 3 and (i - 3) % upt == upt - 1:
                        finish((i - 3) // upt)
                    if i < units:
                        exps(i)
                    if 1 <= i <= units:
                        take_turned(i - 1)
                    if s["name"] == "diff" and i >= 4 and (i - 4) % upt == upt - 1:
                        finish_diff((i - 4) // upt)

            for m in range(AHEAD):
                split_hi(1, m, None)
            act.wait_ge(small_done, 1)
            act.activation(lam_exp[:, :], lam_sum[:, :], ACT.Exp).then_inc(lam_done, 1)
            act.wait_ge(x_loaded, 16 * DT)
            for idx, s in enumerate(PLAN):
                kind = s["kind"]
                act.drain().then_inc(act_settled, 1)
                act.wait_ge(act_settled, idx + 1)
                if kind == "gemm":
                    gemm(s, idx == LAST_GEMM)
                elif kind == "sumsq":
                    if s["src"] != "x":
                        act.wait_ge(bank_free, BANKS + s["at"]["o"])
                    squares(s, s["src"], s["src_at"], s["nch"])
                elif kind == "rstd":
                    act.wait_ge(aux_done, s["at"]["aux"])
                    act.activation(rstd[:, :], psum[:, AUX_BANK, :], ACT.Sqrt, bias=eps[s["eps"]][:, :])\
                       .then_inc(std_done, 1)
                elif kind == "norm":
                    norm(s)
                elif kind in ("final1", "update") and not s.get("last"):
                    squares(s, "x", 0, 8, x_from=s["at"]["xup"])
                elif kind == "vtrans":
                    base = 0 if s["at"]["n"] < 40 else 8
                    for v in range(DT):
                        act.wait_ge(vt_done, base + v + 1)
                        act.activation(vtok[:, v, :, :].rearrange("p a n -> p (a n)"), psum[:, PT_BANK + v % 2, :],
                                       ACT.Copy).then_inc(v_done, 1)
                elif kind == "forget1":
                    act.wait_ge(fg_step, 1)
                    act.activation(fgate_a[:, :, :], fgate[:, :, :], ACT.Abs).then_inc(fg_exp, 1)
                    act.wait_ge(fg_exp, 1)
                    act.activation(fgate_b[:, :, :], fgate_a[:, :, :], ACT.Exp, scale=-1.0).then_inc(fg_exp, 1)
                    act.wait_ge(fg_exp, 2)
                    act.activation(fgate_a[:, :, :], fgate_b[:, :, :], ACT.Ln, bias=1.0).then_inc(fg_exp, 1)
                elif kind == "forget2":
                    act.wait_ge(rope_done, 8)
                    act.dma_start(con[:, ROPE_AT:CONSTS], rope2).then_inc(rope_loaded, 16)
                elif kind == "forget3":
                    for h in range(8):
                        act.wait_ge(nck_psum, h + 1)
                        act.activation(proj[:, h, :], psum[:, PT_BANK + h % 2, :], ACT.Copy).then_inc(nck_done, 1)
                elif kind == "attn":
                    attention(s)

        @block.vector
        def _(dve):
            for n, m in mean.items():
                dve.memset(m[:, :], 1.0 / n).then_inc(const_done, 1)
            dve.memset(ones_col[:, :], 1.0).then_inc(const_done, 1)
            for e, t in eps.items():
                dve.memset(t[:, :], e).then_inc(const_done, 1)
            dve.sem_inc(bank_free, BANKS)
            dve.sem_inc(acc_free, 2)

            def split_lo(m, slot):
                dve.wait_ge(whi_done, m + 1)
                dve.tensor_tensor(w_lo[:, slot, :], w_raw[:, slot, :], w_hi[:, slot, :].bitcast(F32),
                                  ALU.subtract).then_inc(wlo_done, 1)

            for m in range(AHEAD):
                split_lo(m, m)
            dve.wait_ge(par_loaded, 16)
            lam = col("lam", 0, 256).rearrange("p (a b n) -> p a b n", a=2, b=2)
            dve.tensor_tensor(lam_prod[:, :, :], lam[:, :, 0, :], lam[:, :, 1, :], ALU.mult).then_inc(gains_done, 1)
            dve.wait_ge(gains_done, 1)
            dve.tensor_reduce(lam_sum[:, :], lam_prod[:, :, :], AX_X, ALU.add).then_inc(small_done, 1)
            dve.tensor_scalar(subln_gain[:, :], col("subln"), 1.0 - LAM_INIT, None, ALU.mult).then_inc(gains_done, 1)
            dve.wait_ge(lam_done, 1)
            dve.tensor_tensor(lam_diff[:, :], lam_exp[:, 1:2], lam_exp[:, 0:1], ALU.subtract).then_inc(gains_done, 1)
            dve.wait_ge(gains_done, 3)
            dve.tensor_scalar(neg_lam[:, :], lam_diff[:, :], -LAM_INIT, None, ALU.add).then_inc(gains_done, 1)
            dve.wait_ge(x_loaded, 16 * DT)

            def gemm(s, last):
                at_ = s["at"]
                evac = s["evac"]
                lo_out, hi_out = operand("hid")[1], operand("hid")[0]
                if evac == "acc" and s["sq"]:
                    dve.memset(ss[:, :], 0.0).then_inc(ss_done, 1)

                if evac == "conv":
                    dve.memset(conv_u[:, 0:2], 0.0).then_inc(tap_done, 1)
                    dve.wait_ge(tap_done, 1)

                def lo_of(f):
                    dve.wait_ge(hi_done, at_["hi"] + f + 1)
                    dve.tensor_tensor(tile_of(lo_out, f), scratch[:, 8, :], tile_of(hi_out, f).bitcast(F32),
                                      ALU.subtract).then_inc(rhs_ready, 1)

                def step(t):
                    if not (last and isinstance(t.n, int) and t.n + AHEAD >= NB):
                        split_lo(t.n + AHEAD, (t.n0 + AHEAD) % SPLIT)
                    bank = psum[:, t.o0 % BANKS, :]
                    val = scratch[:, 8, :]
                    if evac == "store":
                        for q in range(s["nout"]):
                            dve.wait_ge(out_done, t.o + q + 1)
                            dve.tensor_copy(stored(s["dst"], s["dst_at"] + t.b * s["nout"] + q),
                                            psum[:, (t.o0 + q) % BANKS, :]).then_inc(bank_free, 1)
                    elif evac == "acc":
                        dst = stored(s["dst"], t.b)
                        dve.wait_ge(out_done, t.o + 1)
                        if s["first"]:
                            dve.tensor_copy(dst, bank).then_inc(bank_free, 1)
                        else:
                            dve.tensor_tensor(dst, dst, bank, ALU.add).then_inc(bank_free, 1)
                        if s["sq"]:
                            dve.wait_ge(bank_free, BANKS + t.o + 1)
                            dve.wait_ge(ss_done, at_["ss"] + t.b + 1)
                            dve.tensor_tensor(scratch[:, 4, :], dst, dst, ALU.mult).then_inc(sqv_done, 1)
                            dve.wait_ge(sqv_done, at_["sqv"] + t.b + 1)
                            dve.tensor_tensor(ss[:, :], ss[:, :], scratch[:, 4, :], ALU.add).then_inc(ss_done, 1)
                    elif evac == "gateup":
                        f = t.of(2)
                        if t.j % 2 == 0:
                            dve.wait_ge(gate_done, at_["gate"] + f + 1)
                            dve.sem_inc(bank_free, 1)
                        else:
                            dve.wait_ge(out_done, t.o + 1)
                            dve.wait_ge(rhs_ready, at_["rhs"] + f)
                            dve.tensor_tensor(val, scratch[:, 2 + t.j // 2 % 2, :], bank, ALU.mult)\
                               .then_inc(bank_free, 1)
                            lo_of(f)
                    elif evac == "relu2":
                        dve.wait_ge(gate_done, at_["gate"] + t.b + 1)
                        dve.wait_ge(rhs_ready, at_["rhs"] + t.b)
                        dve.tensor_tensor(val, scratch[:, 2 + t.j % 2, :], bank, ALU.mult).then_inc(bank_free, 1)
                        lo_of(t.b)
                    elif evac == "conv":
                        f = t.of(3)
                        if t.j % 3 == 0:
                            dve.wait_ge(gate_done, at_["gate"] + f + 1)
                            dve.sem_inc(bank_free, 1)
                        elif t.j % 3 == 1:
                            dve.wait_ge(out_done, t.o + 1)
                            dve.wait_ge(tap_done, at_["tap"] + 1 + 3 * f)
                            dve.tensor_tensor(conv_u[:, 2:S + 2], scratch[:, 2, :], bank, ALU.mult)\
                               .then_inc(bank_free, 1)
                            dve.wait_ge(bank_free, BANKS + t.o + 1)
                            w0 = COLS["conv_w"]
                            tap = at_["tap"] + 1 + 3 * f
                            dve.wait_ge(rhs_ready, at_["rhs"] + f)
                            dve.tensor_scalar(val, conv_u[:, 0:S], col_of(par, w0 + f), col_of(par, COLS["conv_b"] + f),
                                              ALU.mult, ALU.add).then_inc(tap_done, 1)
                            for k in (1, 2):
                                dve.wait_ge(tap_done, tap + k)
                                dve.scalar_tensor_tensor(out=val, in0=conv_u[:, k:S + k],
                                                         scalar=col_of(par, w0 + 8 * k + f), in1=val,
                                                         op0=ALU.mult, op1=ALU.add).then_inc(tap_done, 1)
                        else:
                            dve.wait_ge(out_done, t.o + 1)
                            dve.wait_ge(tap_done, at_["tap"] + 3 * f + 4)
                            dve.tensor_tensor(val, val, bank, ALU.mult).then_inc(bank_free, 1)
                            lo_of(f)

                steps(dve, s, step, last)

            def norm(s):
                hi_out, lo_out = operand(s["dst"])
                at_ = s["at"]

                def value(c):
                    if c >= 3:
                        dve.wait_ge(rhs_ready, at_["rhs"] + c - 2)
                    dve.scalar_tensor_tensor(out=scratch[:, 7 + c % 3, :], in0=stored(s["src"], s["src_at"] + c),
                                             scalar=gain_of(s["gain"], c), in1=rstd[:, :], op0=ALU.mult,
                                             op1=ALU.mult).then_inc(val_done, 1)

                def low(c):
                    d = s["dst_at"] + c
                    dve.wait_ge(hi_done, at_["hi"] + c + 1)
                    val, hi = scratch[:, 7 + c % 3, :], hi_out[:, d, :].bitcast(F32)
                    if s["shift"] is None:
                        dve.tensor_tensor(lo_out[:, d, :], val, hi, ALU.subtract).then_inc(rhs_ready, 1)
                    else:
                        sh = s["shift"] + c
                        dve.scalar_tensor_tensor(out=lo_out[:, d, :], in0=val, scalar=mod[:, sh:sh + 1], in1=hi,
                                                 op0=ALU.add, op1=ALU.subtract).then_inc(rhs_ready, 1)

                for c in range(s["nch"] + 1):
                    if c < s["nch"]:
                        value(c)
                    if c >= 1:
                        low(c - 1)

            def update(s):
                for c in range(DT):
                    val = scratch[:, 8 + c % 2, :]
                    if c >= 2:
                        dve.wait_ge(x_done, s["at"]["xup"] + c - 1)
                    dve.scalar_tensor_tensor(out=val, in0=y[:, c, :], scalar=gain_of(s["gain"], c), in1=rstd[:, :],
                                             op0=ALU.mult, op1=ALU.mult).then_inc(val_done, 1)
                    dve.wait_ge(val_done, s["at"]["val"] + c + 1)
                    dve.tensor_tensor(x[:, c, :], x[:, c, :], val, ALU.add).then_inc(x_done, 1)

            def modulated(name, norm_col, scale_col, with_one, base):
                out = r_f1[:, :] if name == "r_f1" else gains[:, GAIN[name], :]
                g = par[:, norm_col:norm_col + 8]
                dve.scalar_tensor_tensor(out=out, in0=mod[:, scale_col:scale_col + 8], scalar=1.0 if with_one else 0.0,
                                         in1=g, op0=ALU.add, op1=ALU.mult).then_inc(gains_done, 1)

            def rope(tiles, base):
                for r, tile in enumerate(tiles):
                    t = proj[:, tile, :]
                    tmp = scratch[:, 8 + r % 2, :]
                    dve.wait_ge(rot_done, base + r + 1)
                    if r >= 2:
                        dve.wait_ge(rope_done, base + r - 1)
                    dve.tensor_tensor(tmp, psum[:, PT_BANK + r % 2, :], cst("sin", 512), ALU.mult)\
                       .then_inc(rope_mul, 1)
                    dve.tensor_tensor(t, t, cst("cos", 512), ALU.mult).then_inc(rope_mul, 1)
                    dve.wait_ge(rope_mul, 2 * (base + r + 1))
                    dve.tensor_tensor(t, t, tmp, ALU.add).then_inc(rope_done, 1)

            def attention(s):
                name = s["name"]
                a, e = ATTN[name], att[name]
                M, units = a["mats"], a["heads"] * QB
                upt = a["per_tile"] * QB
                mask = cst("causal_mask" if name == "fox" else "chunk_mask", 128)

                def maxima(i):
                    W = (i % QB + 1) * P
                    dve.wait_ge(e["scores"], i + 1)
                    if name == "fox":
                        h = i // QB
                        z = scratch[:, 8 + i % 2, :]
                        dve.scalar_tensor_tensor(out=z[:, 0:W], in0=psum[:, 2 * (i % 2), 0:W],
                                                 scalar=cum_tok[:, i % QB, h:h + 1], in1=proj[:, h, 0:W],
                                                 op0=ALU.add, op1=ALU.add).then_inc(e["biased"], 1)
                        dve.wait_ge(e["biased"], i + 1)
                        rows = [z]
                    else:
                        rows = [psum[:, 2 * (i % 2) + m, :] for m in range(M)]
                    for m in range(M):
                        dve.tensor_tensor(rows[m][:, W - P:W], rows[m][:, W - P:W], mask, ALU.add)\
                           .then_inc(e["masked"], 1)
                    if i >= 2:
                        dve.wait_ge(e["negmax"], M * (i - 1))
                    for m in range(M):
                        c = 2 * (i % 2) + m
                        dve.wait_ge(e["masked"], M * i + m + 1)
                        dve.tensor_reduce(row_max[:, c:c + 1], rows[m][:, 0:W], AX_X, ALU.max).then_inc(e["maxed"], 1)
                    for m in range(M):
                        c = 2 * (i % 2) + m
                        dve.wait_ge(e["maxed"], M * i + m + 1)
                        dve.tensor_scalar(neg_max[:, c:c + 1], row_max[:, c:c + 1], -a["scale"], None, ALU.mult)\
                           .then_inc(e["negmax"], 1)

                def probs(i):
                    W = (i % QB + 1) * P
                    c = 2 * (i % 2)
                    dve.wait_ge(e["exp"], M * (i + 1))
                    if i >= 2:
                        dve.wait_ge(e["turned"], i - 1)
                        dve.wait_ge(e["prob"], M * (i - 1))
                    p = scratch[:, 4 + i % 2, 0:W]
                    dve.reciprocal(row_inv[:, c:c + M], row_sum[:, c:c + M]).then_inc(e["inv"], 1)
                    dve.wait_ge(e["inv"], i + 1)
                    if M == 2:
                        dve.tensor_tensor(lam_inv[:, i % 2:i % 2 + 1], row_inv[:, c + 1:c + 2], neg_lam[:, :],
                                          ALU.mult).then_inc(e["lam"], 1)
                    dve.tensor_scalar(p, scratch[:, 2 * (i % 2), 0:W], row_inv[:, c:c + 1], None, ALU.mult)\
                       .then_inc(e["prob"], 1)
                    if M == 2:
                        dve.wait_ge(e["prob"], 2 * i + 1)
                        dve.wait_ge(e["lam"], i + 1)
                        dve.scalar_tensor_tensor(out=p, in0=scratch[:, 2 * (i % 2) + 1, 0:W],
                                                 scalar=lam_inv[:, i % 2:i % 2 + 1], in1=p, op0=ALU.mult,
                                                 op1=ALU.add).then_inc(e["prob"], 1)

                def finish(t):
                    c = t + (4 if name == "fox" else 0)
                    dve.wait_ge(hi_done, s["at"]["hi"] + t + 1)
                    dve.tensor_tensor(h_lo[:, c, :], psum[:, O_BANK, :], h_hi[:, c, :].bitcast(F32),
                                      ALU.subtract).then_inc(rhs_ready, 1)

                def finish_diff(t):
                    dve.wait_ge(e["o_free"], t + 1)
                    dve.reciprocal(rstd[:, :], rstd[:, :]).then_inc(e["o_rstd"], 1)
                    dve.wait_ge(e["o_rstd"], t + 1)
                    dve.wait_ge(rhs_ready, s["at"]["rhs"] + t)
                    dve.scalar_tensor_tensor(out=ss[:, :], in0=scratch[:, 8, :], scalar=subln_gain[:, 0:1],
                                             in1=rstd[:, :], op0=ALU.mult, op1=ALU.mult).then_inc(e["o_val"], 1)
                    dve.wait_ge(hi_done, s["at"]["hi"] + t + 1)
                    dve.tensor_tensor(h_lo[:, t, :], ss[:, :], h_hi[:, t, :].bitcast(F32),
                                      ALU.subtract).then_inc(rhs_ready, 1)

                for i in range(units + 4):
                    if name != "diff" and i >= 3 and (i - 3) % upt == upt - 1:
                        finish((i - 3) // upt)
                    if i < units:
                        maxima(i)
                    if 1 <= i <= units:
                        probs(i - 1)
                    if name == "diff" and i >= 4 and (i - 4) % upt == upt - 1:
                        finish_diff((i - 4) // upt)

            def rstd_of(s):
                dve.wait_ge(std_done, s["at"]["rstd"] + 1)
                dve.reciprocal(rstd[:, :], rstd[:, :]).then_inc(rstd_done, 1)
                dve.wait_ge(rstd_done, s["at"]["rstd"] + 1)

            dve.wait_ge(gains_done, 4)
            dve.wait_ge(con_loaded, 16)
            NG2 = COLS["norm_g2"]
            for idx, s in enumerate(PLAN):
                kind = s["kind"]
                dve.drain().then_inc(dve_settled, 1)
                dve.wait_ge(dve_settled, idx + 1)
                if kind == "gemm":
                    gemm(s, idx == LAST_GEMM)
                elif kind == "rstd":
                    rstd_of(s)
                elif kind == "norm":
                    norm(s)
                elif kind == "update":
                    update(s)
                elif kind == "final1":
                    for c in range(DT):
                        dve.scalar_tensor_tensor(out=x[:, c, :], in0=x[:, c, :], scalar=col("normf", c),
                                                 in1=rstd[:, :], op0=ALU.mult, op1=ALU.mult).then_inc(x_done, 1)
                    dve.wait_ge(x_done, s["at"]["xup"] + 8)
                elif kind == "mod":
                    g = s["at"]["mod"]
                    dve.wait_ge(acc_free, g + 3)
                    m0 = MOD_PER_GROUP * g
                    dve.tensor_tensor(mod[:, m0:m0 + MOD_PER_GROUP],
                                      psum[:, O_BANK, (g % 4) * MOD_PER_GROUP:(g % 4 + 1) * MOD_PER_GROUP],
                                      col("ada_b", m0, MOD_PER_GROUP), ALU.add).then_inc(mod_done, 1)
                elif kind == "modcols0":
                    dve.wait_ge(mod_done, 12)
                    modulated("g_m0", NG2 + 0, 8, True, 4)
                    modulated("r_m0", NG2 + 8, 16, False, 5)
                    modulated("g_f0", NG2 + 16, 32, True, 6)
                    modulated("r_f0", NG2 + 24, 40, False, 7)
                    dve.wait_ge(gains_done, 8)
                elif kind == "modcols1":
                    dve.wait_ge(mod_done, 28)
                    modulated("g_kv", COLS["kv_norm"], 56, True, 8)
                    modulated("g_m1", NG2 + 32, 72, True, 9)
                    modulated("r_m1", NG2 + 40, 80, False, 10)
                    modulated("g_f1", NG2 + 48, 96, True, 11)
                    modulated("r_f1", NG2 + 56, 104, False, 12)
                    dve.wait_ge(gains_done, 13)
                elif kind == "rope1":
                    rope(range(8), 0)
                elif kind == "rope2":
                    dve.wait_ge(rope_loaded, 16)
                    rope(range(16, 21), 8)
                elif kind == "forget1":
                    dve.wait_ge(fg_turned, 1)
                    turned = psum[:, AUX_BANK, :].rearrange("p (a n) -> p a n", a=QB)
                    for q in range(QB):
                        z = dve.tensor_tensor(fgate[:, q, :], turned[:, q, P - 8:P], col("b_f", 0, 8), ALU.add)
                    z.then_inc(fg_step, 1)
                    dve.wait_ge(fg_exp, 3)
                    dve.scalar_tensor_tensor(out=log_f[:, :, :], in0=fgate[:, :, :], scalar=0.0,
                                             in1=fgate_a[:, :, :], op0=ALU.min, op1=ALU.subtract)\
                       .then_inc(logf_done, 1)
                elif kind == "forget2":
                    dve.wait_ge(cum_psum, 1)
                    dve.tensor_scalar(neg_cum, psum[0:8, AUX_BANK, :], -8.0, None, ALU.mult)\
                       .then_inc(cum_done, 1)
                    dve.wait_ge(cum_psum, 2)
                    dve.tensor_scalar(cum_tok[:, :, :].rearrange("p a n -> p (a n)"), psum[:, O_BANK, 0:8 * QB],
                                      8.0, None, ALU.mult).then_inc(cum_done, 1)
                elif kind == "forget3":
                    dve.wait_ge(nck_done, 8)
                    dve.wait_ge(cum_done, 2)
                elif kind == "vtrans":
                    pass
                elif kind == "attn":
                    attention(s)

        @block.tensor
        def _(pe):
            pe.wait_ge(const_done, 7)

            def gemm(s, last):
                hi, lo = operand(s["rhs"])
                nk, ra = s["nk"], s["rhs_at"]

                def step(t):
                    slot = t.n0 % SPLIT
                    pe.wait_ge(wlo_done, t.n + 1)
                    for q in range(s["nout"]):
                        bank = psum[:, (t.o0 + q) % BANKS, :]
                        pe.wait_ge(bank_free, t.o + q + 1)
                        for k in range(nk):
                            if t.j == 0 and q == 0:
                                pe.wait_ge(rhs_ready, s["r0"] + k + 1)
                            w = slice((q * nk + k) * P, (q * nk + k + 1) * P)
                            pe.matmul(bank, w_hi[:, slot, w], hi[:, ra + k, :], start=k == 0, stop=False)
                            pe.matmul(bank, w_hi[:, slot, w], lo[:, ra + k, :], start=False, stop=False)
                            mm = pe.matmul(bank, w_lo[:, slot, w], hi[:, ra + k, :], start=False,
                                           stop=k == nk - 1)
                        mm.then_inc(out_done, 1)

                steps(pe, s, step, last)

            def sum_squares(s, nch, n):
                pe.wait_ge(rstd_done, s["at"]["rstd"])
                for c in range(nch):
                    pe.wait_ge(sqa_done, s["at"]["sqa"] + c + 1)
                    pe.matmul(psum[:, AUX_BANK, :], mean[n][:, :], scratch[:, 5 + c % 2, :], start=c == 0,
                              stop=c == nch - 1).then_inc(aux_done, 1)

            def rope(tiles, base, stored_by):
                pe.wait_ge(bank_free, BANKS + stored_by)
                pe.wait_ge(con_loaded, 16)
                for r, tile in enumerate(tiles):
                    if r >= 2:
                        pe.wait_ge(rope_done, base + r - 1)
                    pe.matmul(psum[:, PT_BANK + r % 2, :], cst("rot", 128), proj[:, tile, :], start=True,
                              stop=True).then_inc(rot_done, 1)

            def attention(s):
                name = s["name"]
                a, e = ATTN[name], att[name]
                M, units = a["mats"], a["heads"] * QB
                upt = a["per_tile"] * QB

                def scores(i):
                    h, q = divmod(i, QB)
                    W = (q + 1) * P
                    rows = slice(q * P, (q + 1) * P)
                    if i >= 2:
                        pe.wait_ge(e["exp"], M * (i - 1))
                    for m in range(M):
                        out = psum[:, 2 * (i % 2) + m, 0:W]
                        if name == "diff":
                            half = slice(64 * m, 64 * m + 64)
                            mm = pe.matmul(out, proj[half, h, rows], proj[half, 4 + h, 0:W], start=True, stop=True)
                        elif name == "fox":
                            half = slice(64 * (h % 2), 64 * (h % 2) + 64)
                            mm = pe.matmul(out, proj[half, 8 + h // 2, rows], proj[half, 12 + h // 2, 0:W],
                                           start=True, stop=True)
                        else:
                            half = slice(64 * (h % 2), 64 * (h % 2) + 64)
                            pe.matmul(out, proj[:, 8 + h, rows], proj[:, h, 0:W], start=True, stop=False)
                            mm = pe.matmul(out, proj[half, 16 + h // 2, rows], proj[half, 20, 0:W], start=False,
                                           stop=True)
                    mm.then_inc(e["scores"], 1)

                def turn(i):
                    q = i % QB
                    pe.wait_ge(e["prob"], M * (i + 1))
                    if i >= 2:
                        pe.wait_ge(e["pt"], i - 1)
                    for kb in range(q + 1):
                        mm = pe.transpose(psum[:, PT_BANK + i % 2, kb * P:(kb + 1) * P],
                                          scratch[:, 4 + i % 2, kb * P:(kb + 1) * P], ident)
                    mm.then_inc(e["turned"], 1)

                def values(i):
                    h, q = divmod(i, QB)
                    pe.wait_ge(e["pt"], i + 1)
                    t = i // upt
                    if i % upt == 0 and t >= 1:
                        if name == "diff":
                            pe.wait_ge(e["o_sq"], t)
                        else:
                            pe.wait_ge(rhs_ready, s["at"]["rhs"] + t)
                    for kb in range(q + 1):
                        if name == "fox":
                            c = 64 * (h % 2)
                            v, rows = vtok[:, 4 + h // 2, kb, c:c + 64], slice(c, c + 64)
                        else:
                            v, rows = vtok[:, h, kb, :], slice(0, P)
                        mm = pe.matmul(psum[rows, O_BANK, q * P:(q + 1) * P], v,
                                       scratch[:, 6 + i % 2, kb * P:(kb + 1) * P], start=kb == 0, stop=kb == q)
                    mm.then_inc(e["pv"], 1)

                def head_square(t):
                    pe.wait_ge(e["o_sq"], t + 1)
                    if t >= 1:
                        pe.wait_ge(e["o_free"], t)
                    pe.matmul(psum[:, AUX_BANK, :], mean[128][:, :], scratch[:, 9, :], start=True,
                              stop=True).then_inc(e["o_ss"], 1)

                for i in range(units + 4):
                    if name == "diff" and i >= 4 and (i - 4) % upt == upt - 1:
                        head_square((i - 4) // upt)
                    if i < units:
                        scores(i)
                    if 1 <= i <= units:
                        turn(i - 1)
                    if 2 <= i <= units + 1:
                        values(i - 2)

            for idx, s in enumerate(PLAN):
                kind = s["kind"]
                if kind == "gemm":
                    gemm(s, idx == LAST_GEMM)
                elif kind == "sumsq":
                    sum_squares(s, s["nch"], s["mean"])
                elif kind in ("final1", "update") and not s.get("last"):
                    sum_squares(s, 8, 1024)
                elif kind == "total":
                    pe.wait_ge(rstd_done, s["at"]["rstd"])
                    pe.wait_ge(ss_done, s["at"]["ss"])
                    pe.matmul(psum[:, AUX_BANK, :], mean[1024][:, :], ss[:, :], start=True, stop=True)\
                      .then_inc(aux_done, 1)
                elif kind == "mod":
                    g = s["at"]["mod"]
                    if PLAN[idx - 1]["kind"] == "forget2":
                        pe.wait_ge(cum_done, 2)
                    if PLAN[idx - 1]["kind"] == "attn":
                        pe.wait_ge(rhs_ready, s["at"]["rhs"])
                    pe.wait_ge(ada_used, DT * (g + 1))
                    if g >= 1:
                        pe.wait_ge(mod_done, g)
                    for m in range(MOD_PER_GROUP):
                        c = (g % 4) * MOD_PER_GROUP + m
                        mm = pe.matmul(psum[:, O_BANK, c:c + 1], ada_acc[:, g % 2, m * P:(m + 1) * P],
                                       ones_col[:, :], start=True, stop=True)
                    mm.then_inc(acc_free, 1)
                elif kind == "rope1":
                    rope(range(8), 0, s["at"]["o"])
                elif kind == "rope2":
                    pe.wait_ge(rope_loaded, 16)
                    pe.wait_ge(v_done, 16)
                    rope(range(16, 21), 8, s["at"]["o"])
                elif kind == "vtrans":
                    base = 0 if s["at"]["n"] < 40 else 8
                    pe.wait_ge(bank_free, BANKS + s["at"]["o"])
                    if base == 0:
                        pe.wait_ge(rope_done, 8)
                    for v in range(DT):
                        if v >= 2:
                            pe.wait_ge(v_done, base + v - 1)
                        for kb in range(QB):
                            mm = pe.transpose(psum[:, PT_BANK + v % 2, kb * P:(kb + 1) * P],
                                              scratch[:, v, kb * P:(kb + 1) * P], ident)
                        mm.then_inc(vt_done, 1)
                elif kind == "forget1":
                    for kb in range(QB):
                        mm = pe.transpose(psum[:, AUX_BANK, kb * P:(kb + 1) * P], proj[:, 16, kb * P:(kb + 1) * P],
                                          ident)
                    mm.then_inc(fg_turned, 1)
                elif kind == "forget2":
                    pe.wait_ge(logf_done, 1)
                    for kb in range(QB):
                        mm = pe.matmul(psum[0:8, AUX_BANK, kb * P:S], log_f[:, kb, :], cst("tri", S - kb * P),
                                       start=kb == 0, stop=kb == QB - 1)
                    mm.then_inc(cum_psum, 1)
                    pe.wait_ge(mod_done, s["at"]["mod"])
                    for q in range(QB):
                        for kb in range(q + 1):
                            mm = pe.matmul(psum[:, O_BANK, 8 * q:8 * q + 8], cst("tri", P, (q - kb) * P),
                                           log_f[:, kb, :], start=kb == 0, stop=kb == q)
                    mm.then_inc(cum_psum, 1)
                elif kind == "forget3":
                    pe.wait_ge(cum_done, 2)
                    for h in range(8):
                        if h >= 2:
                            pe.wait_ge(nck_done, h - 1)
                        pe.matmul(psum[:, PT_BANK + h % 2, :], con[0:8, h:h + 1].broadcast_to([8, P]),
                                  neg_cum, start=True, stop=True).then_inc(nck_psum, 1)
                elif kind == "attn":
                    pe.wait_ge(v_done, 8 if s["name"] != "mla" else 16)
                    pe.wait_ge(rope_done, 8 if s["name"] != "mla" else 13)
                    pe.wait_ge(mod_done, s["at"]["mod"])
                    pe.wait_ge(cum_done, 2)
                    if s["name"] == "fox":
                        pe.wait_ge(nck_done, 8)
                        pe.wait_ge(rhs_ready, s["at"]["rhs"])
                    attention(s)


def lay_out(inp):
    f = {k: np.asarray(v) for k, v in inp.items()}
    blocks = []

    def tiles(w):
        K, M = w.shape
        return w.reshape(K // P, P, M // P, P).transpose(2, 1, 0, 3).reshape(M // P, P, K)

    def push(t, per=1):
        n = t.shape[0] // per
        t = t.reshape(n, per, P, -1).transpose(0, 2, 1, 3).reshape(n, P, -1)
        full = np.zeros((n, P, D), np.float32)
        full[:, :, :t.shape[2]] = t
        blocks.append(full)

    w = f["w_in"][0]
    push(tiles(w[:, 0:1024]))
    push(tiles(w[:, 1536:2560]))
    push(tiles(w[:, w.shape[1] - P:]))
    push(tiles(w[:, 1024:1536]))
    push(tiles(w[:, 2560:3072]))
    push(tiles(f["w_out"][0]))
    gate, up = tiles(f["w_gate"][0]), tiles(f["w_up"][0])
    for c, nk in ((0, 8), (8, 8), (16, 6)):
        push(np.stack([gate[c:c + nk], up[c:c + nk]], 1).reshape(2 * nk, P, D))
        push(tiles(f["w_down"][0][c * P:(c + nk) * P]))
    b, c, xh = (tiles(f["conv_in_w_2"][0][:, i * D:(i + 1) * D]) for i in range(3))
    push(np.stack([c, xh, b], 1).reshape(24, P, D))
    push(tiles(f["conv_out_w_2"][0]))

    def mlp(l):
        for g in range(4):
            push(tiles(f["mlp_up_w_2"][l][:, g * D:(g + 1) * D]))
            push(tiles(f["mlp_down_w_2"][l][g * D:(g + 1) * D]))

    mlp(0)
    w = f["kv_a_w_2"]
    push(tiles(w[:, 0:256]))
    push(tiles(np.concatenate([w[:, 256:320], w[:, 256:320]], 1)))
    push(tiles(f["q_a_w_2"][0]))
    w = f["kv_b_w_2"].reshape(256, 8, 2, P)
    push(tiles(w[:, :, 0].reshape(256, D)), 4)
    push(tiles(w[:, :, 1].reshape(256, D)), 4)
    w = f["q_b_w_2"][0].reshape(384, 8, 192)
    push(tiles(np.concatenate([w[:, :, 0:P].reshape(384, D), w[:, :, P:].reshape(384, 512)], 1)), 2)
    push(tiles(f["attn_o_w_2"][0]))
    mlp(1)
    wstream = np.concatenate(blocks, 0)
    assert wstream.shape[0] == NB, (wstream.shape, NB)

    ada = np.concatenate([f["ada_w_2"][0], f["kv_ada_w_2"], f["ada_w_2"][1]], 1)
    ada = ada.reshape(DT, P, ADA_GROUPS, ADA_COLS)
    ada = ada.transpose(2, 0, 1, 3).reshape(ADA_GROUPS * DT // 2, 2, P, ADA_COLS).transpose(0, 2, 1, 3)
    ada = ada.reshape(ADA_GROUPS * DT // 2, P, 2 * ADA_COLS)

    def cols(v):
        return np.asarray(v).reshape(-1, P).T

    def rows(v):
        v = np.asarray(v).reshape(1, -1)
        return np.broadcast_to(v, (P, v.shape[1]))

    params = np.concatenate([
        cols(f["norm1_g"]), cols(f["norm2_g"]), cols(f["normf_g"]), cols(f["norm_g_2"]), cols(f["kv_norm_g_2"]),
        cols(f["kv_a_norm_g_2"]), cols(f["q_a_norm_g_2"]), cols(f["subln_g"]), cols(f["conv_w_2"]),
        cols(f["conv_b_2"]), cols(np.concatenate([f["ada_b_2"][0], f["kv_ada_b_2"], f["ada_b_2"][1]])),
        cols(f["c_2"]), rows(f["b_f"]), rows(np.concatenate([f["lam_q1"], f["lam_k1"], f["lam_q2"], f["lam_k2"]])),
    ], 1)
    xT = f["x"][0].T.reshape(DT, P, S)
    return xT, wstream, ada, params


def constants():
    q, k = np.arange(P)[:, None], np.arange(P)[None, :]
    ident = np.eye(P)
    tri = np.concatenate([(q <= k) * 1.0, np.ones((P, S - P))], 1)
    chunk_mask = np.where(k // 64 <= q // 64, 0.0, NEG)
    causal_mask = np.where(k <= q, 0.0, NEG)

    def rotary(dim, theta):
        half = dim // 2
        inv = np.float32(theta) ** (-np.arange(0, dim, 2, dtype=np.float32) / np.float32(dim))
        ang = np.arange(S, dtype=np.float32)[None, :] * inv.astype(np.float32)[:, None]
        cos, sin = np.ones((64, S)), np.zeros((64, S))
        rot = np.zeros((64, 64))
        for i in range(half):
            cos[i] = cos[i + half] = np.cos(ang[i])
            sin[i] = sin[i + half] = np.sin(ang[i])
            rot[i + half, i] = -1.0
            rot[i, i + half] = 1.0
        two = np.zeros((P, P))
        two[:64, :64] = two[64:, 64:] = rot
        return [two, np.tile(cos, (2, 1)), np.tile(sin, (2, 1))]

    first = np.concatenate([ident, tri, chunk_mask, causal_mask] + rotary(16, 500000.0), 1)
    return first.astype(np.float32), np.concatenate(rotary(64, 10000.0), 1).astype(np.float32)


def kernel(**inputs):
    import concourse.bacc as bacc
    from concourse.bass_utils import run_bass_kernel_spmd as run

    xT, wstream, ada, params = lay_out(inputs)
    consts, rope2 = constants()
    arrays = dict(xT=xT, wstream=wstream, ada=ada, params=params, consts=consts, rope2=rope2)
    arrays = {f"in_{k}": np.ascontiguousarray(v) for k, v in arrays.items()}
    nc = bacc.Bacc("TRN2", target_bir_lowering=False, num_devices=1)
    args = [nc.dram_tensor(k, v.shape, F32, kind="ExternalInput").ap() for k, v in arrays.items()]
    args.append(nc.dram_tensor("outT", (DT, P, S), F32, kind="ExternalOutput").ap())
    build(nc, *args)
    r = run(nc, [arrays], core_ids=[0])
    return np.asarray(r.results[0]["outT"]).reshape(D, S).T.reshape(1, S, D)
```

```python
from contextlib import ExitStack

import numpy as np

import concourse.bass as bass
from concourse import mybir

F32 = mybir.dt.float32
F32R = mybir.dt.float32r
ALU = mybir.AluOpType
ACT = mybir.ActivationFunctionType
AX_X = mybir.AxisListType.X

P = 128
S = 512
D = 1024
DT = D // P
QB = S // P
D_FF = 2816
EPS1, EPS2 = 1e-5, 1e-6
NEG = -1e30
LAM_INIT = 0.2

RAW = 4
SPLIT = 4
AHEAD = 3
BANKS = 4
PT_BANK, O_BANK, AUX_BANK = 4, 6, 7
ADA_COLS = 512
ADA_GROUPS = (6 + 2 + 6) * D // ADA_COLS
ADA_SLOTS = 4
ACCS = 3
MOD_PER_GROUP = ADA_COLS // P

COLS = {}
_at = 0
for _name, _n in (("norm1", 8), ("norm2", 8), ("normf", 8), ("norm_g2", 64), ("kv_norm", 8), ("kv_a_norm", 2),
                  ("q_a_norm", 3), ("subln", 1), ("conv_w", 24), ("conv_b", 8), ("ada_b", 112), ("c", 8),
                  ("b_f", 8), ("lam", 256)):
    COLS[_name] = _at
    _at += _n
PARAMS = _at
CONST = {}
_at = 0
for _name, _n in (("ident", 128), ("tri", 512), ("chunk_mask", 128), ("causal_mask", 128),
                  ("rot", 128), ("cos", 512), ("sin", 512)):
    CONST[_name] = _at
    _at += _n
CONSTS = _at
ROPE_AT = CONST["rot"]
ROPE_COLS = CONSTS - ROPE_AT


def make_plan():
    counts = dict(n=0, o=0, gate=0, tap=0, sqv=0, ss=0, val=0, hi=0, rhs=0, xup=0, sqa=0, aux=0, rstd=0,
                  mod=0, take=0)
    plan = []

    def add(kind, inc=None, **about):
        plan.append(dict(kind=kind, at=dict(counts), **about))
        for k, v in (inc or {}).items():
            counts[k] += v

    def gemm(evac, nblk, rhs, r0, nk=8, nout=1, rhs_at=0, **about):
        inc = dict(n=nblk, o=nblk * nout)
        if evac == "acc" and about.get("sq"):
            inc.update(sqv=nblk, ss=1 + nblk)
        if evac == "gateup":
            inc.update(gate=nblk // 2, hi=nblk // 2, rhs=nblk // 2)
        if evac == "relu2":
            inc.update(gate=nblk, hi=nblk, rhs=nblk)
        if evac == "conv":
            inc.update(gate=nblk // 3, tap=1 + nblk, hi=nblk // 3, rhs=nblk // 3)
        add("gemm", inc, evac=evac, nblk=nblk, rhs=rhs, r0=r0, nk=nk, nout=nout, rhs_at=rhs_at, **about)

    def sumsq(src, at, nch, mean):
        add("sumsq", dict(sqa=nch, aux=nch), src=src, src_at=at, nch=nch, mean=mean)

    def total():
        add("total", dict(aux=1))

    def rstd(eps):
        add("rstd", dict(rstd=1), eps=eps)

    def norm(dst, src="x", src_at=0, nch=8, dst_at=0, gain=None, shift=None):
        r0 = counts["rhs"]
        add("norm", dict(val=nch, hi=nch, rhs=nch), dst=dst, src=src, src_at=src_at, nch=nch, dst_at=dst_at,
            gain=gain, shift=shift)
        return r0

    def update(gain, last=False):
        add("update", dict(val=8, xup=8, **({} if last else dict(sqa=8, aux=8))), gain=gain, last=last)

    def modulation(groups, after=None):
        add("mod", dict(mod=groups), groups=groups, after=after)

    taken = [0]

    def take():
        add("take", dict(take=1), first=taken[0], upto=counts["mod"])
        taken[0] = counts["mod"]

    sumsq("x", 0, 8, 1024)
    rstd(EPS1)
    h = norm("h", gain="norm1")
    gemm("store", 8, "h", h, dst="proj", dst_at=0, kouter=True)
    modulation(2)
    gemm("store", 9, "h", h, dst="proj", dst_at=8)
    modulation(2)
    add("rope1")
    add("forget1")
    gemm("store", 8, "h", h, dst="scratch", dst_at=0)
    modulation(2)
    take()
    add("vtrans")
    add("forget2")
    mix = counts["rhs"]
    add("attn", dict(hi=4, rhs=4), name="diff")
    modulation(2, "attn")
    take()
    add("forget3")
    add("attn", dict(hi=4, rhs=4), name="fox")
    modulation(2, "attn")
    gemm("acc", 8, "h", mix, dst="x", first=False, sq=True)
    modulation(2)
    total()
    rstd(EPS1)
    h = norm("h", gain="norm2")
    for g, nk in enumerate((8, 8, 6)):
        hid = counts["rhs"]
        gemm("gateup", 2 * nk, "h", h, kouter=g == 0)
        modulation(3 if g < 2 else 2)
        gemm("acc", 8, "hid", hid, nk=nk, dst="x", first=False, sq=g == 2)
        if g < 2:
            modulation(2)
    take()
    add("modcols0")
    total()
    rstd(EPS1)
    add("final1", dict(xup=8, sqa=8, aux=8))
    rstd(EPS2)
    h = norm("h", gain="g_m0", shift=0)
    hid = counts["rhs"]
    gemm("conv", 24, "h", h, kouter=True)
    modulation(3)
    gemm("acc", 8, "hid", hid, dst="y", first=True, sq=True)
    modulation(1)
    total()
    rstd(EPS2)
    update("r_m0")
    rstd(EPS2)
    h = norm("h", gain="g_f0", shift=24)

    def mlp(h):
        for g in range(4):
            hid = counts["rhs"]
            gemm("relu2", 8, "h", h, kouter=g == 0)
            gemm("acc", 8, "hid", hid, dst="y", first=g == 0, sq=g == 3)

    mlp(h)
    take()
    add("modcols1")
    total()
    rstd(EPS2)
    update("r_f0")
    rstd(EPS2)
    hkv = norm("hid", gain="g_kv", shift=48)
    h = norm("h", gain="g_m1", shift=64)
    gemm("store", 3, "hid", hkv, dst="kv_a", dst_at=0)
    gemm("store", 3, "h", h, dst="scratch", dst_at=0)
    sumsq("scratch", 3, 2, 256)
    rstd(EPS2)
    c_kv = norm("h", src="scratch", src_at=3, nch=2, dst_at=3, gain="kv_a_norm")
    sumsq("scratch", 0, 3, 384)
    rstd(EPS2)
    q_a = norm("h", src="scratch", src_at=0, nch=3, dst_at=0, gain="q_a_norm")
    gemm("store", 2, "h", c_kv, nk=2, nout=4, rhs_at=3, dst="proj", dst_at=0)
    gemm("store", 2, "h", c_kv, nk=2, nout=4, rhs_at=3, dst="scratch", dst_at=0)
    add("vtrans")
    gemm("store", 6, "h", q_a, nk=3, nout=2, dst="proj", dst_at=8)
    add("rope2")
    mix = counts["rhs"]
    add("attn", dict(hi=8, rhs=8), name="mla")
    gemm("acc", 8, "h", mix, dst="y", first=True, sq=True)
    total()
    rstd(EPS2)
    update("r_m1")
    rstd(EPS2)
    h = norm("h", gain="g_f1", shift=88)
    mlp(h)
    total()
    rstd(EPS2)
    update("r_f1", last=True)
    assert counts["mod"] == ADA_GROUPS, counts["mod"]
    return plan, counts


PLAN, TOTALS = make_plan()
NB = TOTALS["n"]
LAST_GEMM = max(i for i, s in enumerate(PLAN) if s["kind"] == "gemm")

ATTN = dict(
    diff=dict(heads=4, mats=2, scale=64 ** -0.5, per_tile=1, tiles=4),
    fox=dict(heads=8, mats=1, scale=64 ** -0.5, per_tile=2, tiles=4),
    mla=dict(heads=8, mats=1, scale=192 ** -0.5, per_tile=1, tiles=8),
)


PROB_LAG, TURN_LAG, TAKE_LAG, PV_LAG = 2, 3, 4, 5


class Step:

    def __init__(self, stage, b, j, turn, body):
        self.b, self.j = b, j
        self.n = stage["at"]["n"] + b
        self.n0 = stage["at"]["n"] + j
        self.turn, self.body = turn, body
        self.o = stage["at"]["o"] + b * stage["nout"]
        self.o0 = stage["at"]["o"] + j * stage["nout"]

    def rounds(self, ahead, ring):
        return (self.n0 + ahead) // ring + 1 + self.turn * (self.body // ring)

    def of(self, per):
        return self.j // per + self.turn * (self.body // per)


def steps(eng, stage, do, last=False, done=0):
    nblk = stage["nblk"]
    body = 12 if stage["evac"] == "conv" else 4
    turns = nblk // body
    first = 1 if stage["at"]["n"] == 0 or done else 0
    if last:
        turns -= 1
    if turns - first < 2:
        first = turns = 0
    for b in range(done, first * body):
        do(Step(stage, b, b, 0, body))
    if turns:
        with eng.Fori(first, turns) as i:
            for j in range(body):
                do(Step(stage, body * i + j, j, i, body))
    for b in range(max(done, turns * body), nblk):
        do(Step(stage, b, b, 0, body))


def tile_of(t, i):
    if isinstance(i, int):
        return t[:, i, :]
    return t[:, bass.ds(i, 1), :].rearrange("p a n -> p (a n)")


def col_of(t, i):
    if isinstance(i, int):
        return t[:, i:i + 1]
    return t[:, bass.ds(i, 1)]


def build(nc, xT, wstream, ada, params, consts, rope2, outT):
    ctx = ExitStack()
    with ctx:
        place = [nc.sbuf_base if not callable(nc.sbuf_base) else nc.sbuf_base()]
        place[0] = (place[0] + 63) // 64 * 64

        def at(name, shape, dtype, where):
            return nc.alloc_sbuf_tensor_at(name, shape, dtype, offset=where)

        def sb(name, shape, dtype=F32):
            where = place[0]
            place[0] += (int(np.prod(shape[1:])) * 4 + 63) // 64 * 64
            return at(name, shape, dtype, where)

        x = sb("x", [P, DT, S])
        y_at = place[0]
        y = sb("y", [P, DT, S])
        vtok = at("vtok", [P, DT, QB, P], F32, y_at)
        h_hi = sb("h_hi", [P, DT, S], F32R)
        h_lo = sb("h_lo", [P, DT, S], F32R)
        proj_at = place[0]
        proj = sb("proj", [P, 21, S])
        hid_hi = at("hid_hi", [P, DT, S], F32R, proj_at)
        hid_lo = at("hid_lo", [P, DT, S], F32R, proj_at + DT * S * 4)
        w_raw = sb("w_raw", [P, RAW, D])
        w_hi = sb("w_hi", [P, SPLIT, D], F32R)
        w_lo = sb("w_lo", [P, SPLIT, D], F32R)
        conv_u = at("conv_u", [P, S + 2], F32, place[0])
        scratch = sb("scratch", [P, 10, S])
        ss = sb("ss", [P, S])
        rstd = sb("rstd", [P, S])
        ada_raw = sb("ada_raw", [P, ADA_SLOTS, ADA_COLS])
        ada_acc = sb("ada_acc", [P, ACCS, ADA_COLS])
        par = sb("par", [P, PARAMS])
        con = sb("con", [P, CONSTS])
        mean = {n: sb(f"mean{n}", [P, P]) for n in (1024, 256, 384, 128)}
        ones_col = sb("ones_col", [P, 1])
        eps = {e: sb(f"eps{n}", [P, 1]) for n, e in enumerate((EPS1, EPS2))}
        c_act = sb("c_act", [P, 8])
        mod = sb("mod", [P, ADA_GROUPS * MOD_PER_GROUP])
        gains = sb("gains", [P, 8, DT])
        subln_gain = sb("subln_gain", [P, 1])
        lam_prod = sb("lam_prod", [P, 2, 64])
        lam_sum = sb("lam_sum", [P, 2])
        lam_exp = sb("lam_exp", [P, 2])
        neg_lam = sb("neg_lam", [P, 1])
        lam_diff = sb("lam_diff", [P, 1])
        fgate = sb("fgate", [P, QB, 8])
        fgate_a = sb("fgate_a", [P, QB, 8])
        fgate_b = sb("fgate_b", [P, QB, 8])
        log_f = sb("log_f", [P, QB, 8])
        cum_tok = sb("cum_tok", [P, QB, 8])
        neg_cum = proj[0:8, 17, :]
        row_max = sb("row_max", [P, 8])
        neg_max = sb("neg_max", [P, 8])
        row_sum = sb("row_sum", [P, 8])
        row_inv = sb("row_inv", [P, 8])
        lam_inv = sb("lam_inv", [P, 2])

        psum = ctx.enter_context(nc.psum_tensor("psum", [P, 8, S], F32))

        def sem(name):
            return ctx.enter_context(nc.semaphore(name))

        raw_loaded = [sem(f"raw_loaded{i}") for i in range(RAW)]
        whi_done = sem("whi_done")
        wlo_done = sem("wlo_done")
        out_done = sem("out_done")
        bank_free = sem("bank_free")
        gate_done = sem("gate_done")
        tap_done = sem("tap_done")
        sqv_done = sem("sqv_done")
        ss_done = sem("ss_done")
        val_done = sem("val_done")
        hi_done = sem("hi_done")
        rhs_ready = sem("rhs_ready")
        x_done = sem("x_done")
        sqa_done = sem("sqa_done")
        aux_done = sem("aux_done")
        ln_done = sem("ln_done")
        rstd_done = sem("rstd_done")
        ada_loaded = [sem(f"ada_loaded{i}") for i in range(2)]
        ada_scaled = sem("ada_scaled")
        ada_used = sem("ada_used")
        acc_free = sem("acc_free")
        mod_done = sem("mod_done")
        gains_done = sem("gains_done")
        c_done = sem("c_done")
        act_settled = sem("act_settled")
        dve_settled = sem("dve_settled")
        x_loaded = [sem(f"x_loaded{c}") for c in range(DT)]
        par_loaded = sem("par_loaded")
        con_loaded = sem("con_loaded")
        rope_loaded = sem("rope_loaded")
        const_done = sem("const_done")
        small_done = sem("small_done")
        lam_done = sem("lam_done")
        out_stored = sem("out_stored")
        rot_done = sem("rot_done")
        rope_mul = sem("rope_mul")
        rope_done = sem("rope_done")
        vt_done = sem("vt_done")
        v_done = sem("v_done")
        fg_turned = sem("fg_turned")
        fg_step = sem("fg_step")
        fg_exp = sem("fg_exp")
        logf_done = sem("logf_done")
        cum_psum = sem("cum_psum")
        cum_done = sem("cum_done")
        nck_psum = sem("nck_psum")
        nck_done = sem("nck_done")
        names = ("scores", "masked", "maxed", "negmax", "exp", "inv", "prob", "turned", "pt", "pv", "o_copied",
                 "o_sq", "o_ss", "o_free", "o_rstd", "o_val", "biased", "lam")
        att = {a: {n: sem(f"{a}_{n}") for n in names} for a in ATTN}

        def col(name, i=0, n=1):
            return par[:, COLS[name] + i:COLS[name] + i + n]

        def cst(name, n, i=0, rows=P):
            return con[0:rows, CONST[name] + i:CONST[name] + i + n]

        ident = cst("ident", 128)
        GAIN = dict(g_m0=0, r_m0=1, g_f0=2, r_f0=3, g_kv=4, g_m1=5, r_m1=6, g_f1=7)
        r_f1 = sb("r_f1", [P, DT])

        def gain_of(name, c):
            if name == "r_f1":
                return r_f1[:, c:c + 1]
            if name in GAIN:
                return gains[:, GAIN[name], c:c + 1]
            return col(name, c)

        def operand(name):
            return dict(h=(h_hi, h_lo), hid=(hid_hi, hid_lo))[name]

        def stored(name, i):
            if name == "kv_a":
                return scratch[:, 3 + i, :] if i < 2 else proj[:, 20, :]
            return tile_of(dict(proj=proj, scratch=scratch, x=x, y=y)[name], i)

        def score_bank(name, i, m):
            return 2 * (i % 2) + m if name == "diff" else i % 4

        def exp_tile(name, i, m):
            return scratch[:, 2 * (i % 2) + m if name == "diff" else i % 6, :]

        def prob_tile(name, i):
            return scratch[:, (4, 5, 9)[i % 3], :] if name == "diff" else exp_tile(name, i, 0)

        def turned_tile(i):
            return scratch[:, 6 + i % 3, :]

        def out_bank(name, t):
            return O_BANK if name == "diff" else (O_BANK, AUX_BANK)[t % 2]

        head_out, head_sq = proj[:, 18, :], proj[:, 19, :]
        bias_tile = lambda h: (h % 2) * 4 + h // 2

        block = ctx.enter_context(nc.Block())

        @block.sync
        def _(sp):
            for c in range(DT):
                sp.dma_start(x[:, c, :], xT[c]).then_inc(x_loaded[c], 16)
                if c == 1:
                    sp.dma_start(par[:, :], params).then_inc(par_loaded, 16)
            for n in range(RAW):
                sp.dma_start(w_raw[:, n, :], wstream[n]).then_inc(raw_loaded[n], 16)
            sp.dma_start(con[:, :], consts).then_inc(con_loaded, 16)

            def load(n, slot):
                sp.wait_ge(wlo_done, n + 1 - RAW)
                src = wstream[n] if isinstance(n, int) else wstream[bass.ds(n, 1)].rearrange("a p m -> (a p) m")
                sp.dma_start(w_raw[:, slot, :], src).then_inc(raw_loaded[slot], 16)

            with sp.Fori(1, NB // RAW) as i:
                for j in range(RAW):
                    load(RAW * i + j, j)
            for n in range(NB // RAW * RAW, NB):
                load(n, n % RAW)
            for s in PLAN:
                if s["kind"] == "update" and s["last"]:
                    for c in range(DT):
                        sp.wait_ge(x_done, s["at"]["xup"] + c + 1)
                        sp.dma_start(outT[c], x[:, c, :]).then_inc(out_stored, 16)
            sp.wait_ge(out_stored, 16 * DT)

        @block.gpsimd
        def _(pool):
            def load(v, half):
                src = ada[v] if isinstance(v, int) else ada[bass.ds(v, 1)].rearrange("a p m -> (a p) m")
                pool.dma_start(ada_raw[:, 2 * half:2 * half + 2, :].rearrange("p a n -> p (a n)"), src)\
                    .then_inc(ada_loaded[half], 16)

            load(0, 0)
            load(1, 1)
            pool.wait_ge(c_done, 1)

            def groups(i, n, last):
                for v in range(4 * n):
                    g, acc = v // 4, ada_acc[:, v // 4, :]
                    if v % 4 == 0:
                        pool.wait_ge(acc_free, ACCS * i + g + 1)
                    pool.wait_ge(ada_loaded[v % 2], 16 * (2 * ACCS * i + v // 2 + 1))
                    for u in range(2 * v, 2 * v + 2):
                        k = u % DT
                        row = ada_raw[:, u % ADA_SLOTS, :]
                        c_k = c_act[:, k:k + 1].broadcast_to([P, ADA_COLS])
                        if k == 0:
                            pool.tensor_tensor(acc, row, c_k, ALU.mult).then_inc(ada_used, 1)
                        else:
                            pool.tensor_tensor(row, row, c_k, ALU.mult).then_inc(ada_scaled, 1)
                            pool.wait_ge(ada_scaled, (DT - 1) * (ACCS * i + g) + k)
                            pool.wait_ge(ada_used, ACCS * DT * i + u)
                            pool.tensor_tensor(acc, acc, row, ALU.add).then_inc(ada_used, 1)
                    if not (last and v >= 4 * n - 2):
                        pool.wait_ge(ada_used, ACCS * DT * i + 2 * v + 2)
                        pool.wait_ge(c_done, 1)
                        load(4 * ACCS * i + (v + 2), v % 2)

            with pool.Fori(0, ADA_GROUPS // ACCS) as i:
                groups(i, ACCS, False)
            assert ADA_GROUPS % ACCS == 1
            groups(ADA_GROUPS // ACCS, 1, True)

        @block.scalar
        def _(act):
            act.wait_ge(const_done, 7)
            act.wait_ge(par_loaded, 16)
            act.activation(c_act[:, :], col("c", 0, 8), ACT.Silu).then_inc(c_done, 1)

            def split_hi(m_rounds, slot, out_wait):
                if out_wait is not None:
                    act.wait_ge(out_done, out_wait)
                act.wait_ge(raw_loaded[slot], 16 * m_rounds)
                act.activation(w_hi[:, slot, :], w_raw[:, slot, :], ACT.Copy).then_inc(whi_done, 1)

            def gemm(s, last):
                at_ = s["at"]
                evac = s["evac"]
                hi_out = operand("hid")[0]

                def step(t):
                    if not (last and isinstance(t.n, int) and t.n + AHEAD >= NB):
                        split_hi(t.rounds(AHEAD, RAW), (t.n0 + AHEAD) % SPLIT,
                                 None if isinstance(t.o, int) and t.o == 0 else t.o)
                    bank = psum[:, t.o0 % BANKS, :]
                    if evac == "gateup" and t.j % 2 == 0:
                        f = t.of(2)
                        act.wait_ge(out_done, t.o + 1)
                        act.wait_ge(bank_free, BANKS + t.o - 2)
                        act.activation(scratch[:, 2 + t.j // 2 % 2, :], bank, ACT.Silu).then_inc(gate_done, 1)
                    if evac == "gateup" and t.j % 2 == 1:
                        act.wait_ge(bank_free, BANKS + t.o + 1)
                        act.activation(tile_of(hi_out, t.of(2)), scratch[:, 8, :], ACT.Copy).then_inc(hi_done, 1)
                    if evac == "relu2":
                        act.wait_ge(out_done, t.o + 1)
                        act.wait_ge(bank_free, BANKS + t.o - 1)
                        act.activation(scratch[:, 2 + t.j % 2, :], bank, ACT.Relu).then_inc(gate_done, 1)
                        act.wait_ge(bank_free, BANKS + t.o + 1)
                        act.activation(tile_of(hi_out, t.b), scratch[:, 8, :], ACT.Copy).then_inc(hi_done, 1)
                    if evac == "conv" and t.j % 3 == 0:
                        act.wait_ge(out_done, t.o + 1)
                        act.wait_ge(bank_free, BANKS + t.o - 1)
                        act.activation(scratch[:, 2, :], bank, ACT.Copy).then_inc(gate_done, 1)
                    if evac == "conv" and t.j % 3 == 2:
                        act.wait_ge(bank_free, BANKS + t.o + 1)
                        act.activation(tile_of(hi_out, t.of(3)), scratch[:, 8, :], ACT.Copy).then_inc(hi_done, 1)

                steps(act, s, step, last)

            def squares(s, src, src_at, nch, x_from=None):
                for c in range(nch):
                    if x_from is not None:
                        act.wait_ge(x_done, x_from + c + 1)
                    if c >= 2:
                        act.wait_ge(aux_done, s["at"]["aux"] + c - 1)
                    if s["at"]["sqa"] == 0:
                        act.wait_ge(x_loaded[c], 16)
                    act.activation(scratch[:, 5 + c % 2, :], stored(src, src_at + c), ACT.Square)\
                       .then_inc(sqa_done, 1)

            def norm(s):
                hi_out = operand(s["dst"])[0]
                for c in range(s["nch"]):
                    act.wait_ge(val_done, s["at"]["val"] + c + 1)
                    val = scratch[:, 7 + c % 3, :]
                    if s["shift"] is None:
                        act.activation(hi_out[:, s["dst_at"] + c, :], val, ACT.Copy).then_inc(hi_done, 1)
                    else:
                        act.activation(hi_out[:, s["dst_at"] + c, :], val, ACT.Identity,
                                       bias=mod[:, s["shift"] + c:s["shift"] + c + 1]).then_inc(hi_done, 1)

            def attention(s):
                name = s["name"]
                a, e = ATTN[name], att[name]
                M, units = a["mats"], a["heads"] * QB
                upt = a["per_tile"] * QB

                def exps(i):
                    W = (i % QB + 1) * P
                    act.wait_ge(e["negmax"], i + 1)
                    for m in range(M):
                        dst = exp_tile(name, i, m)[:, 0:W]
                        src = dst if name == "fox" else psum[:, score_bank(name, i, m), 0:W]
                        c = M * (i % 4) + m
                        act.activation(dst, src, ACT.Exp, bias=neg_max[:, c:c + 1], scale=a["scale"],
                                       accum_out=row_sum[:, c:c + 1]).then_inc(e["exp"], 1)

                def take_turned(i):
                    W = (i % QB + 1) * P
                    act.wait_ge(e["turned"], i + 1)
                    if i >= 3:
                        act.wait_ge(e["pv"], i - 2)
                    act.activation(turned_tile(i)[:, 0:W], psum[:, PT_BANK + i % 2, 0:W], ACT.Copy)\
                       .then_inc(e["pt"], 1)

                def finish(t):
                    act.wait_ge(e["pv"], upt * (t + 1))
                    O = psum[:, out_bank(name, t), :]
                    if name != "diff":
                        c = t + (4 if name == "fox" else 0)
                        act.activation(h_hi[:, c, :], O, ACT.Copy).then_inc(hi_done, 1)
                    else:
                        if t >= 1:
                            act.wait_ge(e["o_val"], t)
                        act.activation(head_out, O, ACT.Copy).then_inc(e["o_copied"], 1)
                        act.activation(head_sq, O, ACT.Square).then_inc(e["o_sq"], 1)

                def root(t):
                    act.wait_ge(e["o_ss"], t + 1)
                    act.activation(rstd[:, :], psum[:, AUX_BANK, :], ACT.Ln, bias=eps[EPS1][:, :])\
                       .then_inc(e["o_free"], 1)
                    act.wait_ge(e["o_free"], t + 1)
                    act.activation(rstd[:, :], rstd[:, :], ACT.Exp, scale=-0.5).then_inc(e["o_rstd"], 1)

                def high(t):
                    act.wait_ge(e["o_val"], t + 1)
                    act.activation(h_hi[:, t, :], ss[:, :], ACT.Copy).then_inc(hi_done, 1)

                def due(i, lag):
                    u = i - PV_LAG - lag
                    return u // upt if 0 <= u < units and u % upt == upt - 1 else None

                for i in range(units + PV_LAG + 4):
                    if due(i, 1) is not None:
                        finish(due(i, 1))
                    if name == "diff" and due(i, 2) is not None:
                        root(due(i, 2))
                    if name == "diff" and due(i, 3) is not None:
                        high(due(i, 3))
                    if 0 <= i - TAKE_LAG < units:
                        take_turned(i - TAKE_LAG)
                    if i < units:
                        exps(i)

            for idx, s in enumerate(PLAN):
                kind = s["kind"]
                act.drain().then_inc(act_settled, 1)
                act.wait_ge(act_settled, idx + 1)
                if kind == "gemm":
                    gemm(s, idx == LAST_GEMM)
                elif kind == "sumsq":
                    if s["src"] != "x":
                        act.wait_ge(bank_free, BANKS + s["at"]["o"])
                    squares(s, s["src"], s["src_at"], s["nch"])
                    if idx == 0:
                        for m in range(AHEAD):
                            split_hi(1, m, None)
                elif kind == "rstd":
                    act.wait_ge(aux_done, s["at"]["aux"])
                    act.activation(rstd[:, :], psum[:, AUX_BANK, :], ACT.Ln, bias=eps[s["eps"]][:, :])\
                       .then_inc(ln_done, 1)
                    act.wait_ge(ln_done, s["at"]["rstd"] + 1)
                    act.activation(rstd[:, :], rstd[:, :], ACT.Exp, scale=-0.5).then_inc(rstd_done, 1)
                elif kind == "norm":
                    norm(s)
                elif kind in ("final1", "update") and not s.get("last"):
                    squares(s, "x", 0, 8, x_from=s["at"]["xup"])
                elif kind == "vtrans":
                    base = 0 if s["at"]["n"] < 40 else 8
                    for v in range(DT):
                        act.wait_ge(vt_done, base + v + 1)
                        act.activation(vtok[:, v, :, :].rearrange("p a n -> p (a n)"), psum[:, PT_BANK + v % 2, :],
                                       ACT.Copy).then_inc(v_done, 1)
                elif kind == "forget1":
                    act.wait_ge(small_done, 1)
                    act.activation(lam_exp[:, :], lam_sum[:, :], ACT.Exp).then_inc(lam_done, 1)
                    act.wait_ge(fg_step, 1)
                    act.activation(fgate_a[:, :, :], fgate[:, :, :], ACT.Abs).then_inc(fg_exp, 1)
                    act.wait_ge(fg_exp, 1)
                    act.activation(fgate_b[:, :, :], fgate_a[:, :, :], ACT.Exp, scale=-1.0).then_inc(fg_exp, 1)
                    act.wait_ge(fg_exp, 2)
                    act.activation(fgate_a[:, :, :], fgate_b[:, :, :], ACT.Ln, bias=1.0).then_inc(fg_exp, 1)
                elif kind == "forget2":
                    act.wait_ge(rope_done, 8)
                    act.dma_start(con[:, ROPE_AT:CONSTS], rope2).then_inc(rope_loaded, 16)
                elif kind == "forget3":
                    for h in range(8):
                        act.wait_ge(nck_psum, h + 1)
                        act.activation(proj[:, bias_tile(h), :], psum[:, PT_BANK + h % 2, :], ACT.Copy).then_inc(nck_done, 1)
                elif kind == "attn":
                    attention(s)

        @block.vector
        def _(dve):
            for n, m in mean.items():
                dve.memset(m[:, :], 1.0 / n).then_inc(const_done, 1)
            dve.memset(ones_col[:, :], 1.0).then_inc(const_done, 1)
            for e, t in eps.items():
                dve.memset(t[:, :], e).then_inc(const_done, 1)
            dve.sem_inc(bank_free, BANKS)
            dve.sem_inc(acc_free, ACCS)

            def split_lo(m, slot):
                dve.wait_ge(whi_done, m + 1)
                dve.tensor_tensor(w_lo[:, slot, :], w_raw[:, slot, :], w_hi[:, slot, :].bitcast(F32),
                                  ALU.subtract).then_inc(wlo_done, 1)

            for c in range(DT):
                dve.wait_ge(x_loaded[c], 16)

            def gemm(s, last):
                at_ = s["at"]
                evac = s["evac"]
                lo_out, hi_out = operand("hid")[1], operand("hid")[0]
                if evac == "acc" and s["sq"]:
                    dve.memset(ss[:, :], 0.0).then_inc(ss_done, 1)

                if evac == "conv":
                    dve.memset(conv_u[:, 0:2], 0.0).then_inc(tap_done, 1)
                    dve.wait_ge(tap_done, 1)

                def lo_of(f):
                    dve.wait_ge(hi_done, at_["hi"] + f + 1)
                    dve.tensor_tensor(tile_of(lo_out, f), scratch[:, 8, :], tile_of(hi_out, f).bitcast(F32),
                                      ALU.subtract).then_inc(rhs_ready, 1)

                def step(t):
                    if not (last and isinstance(t.n, int) and t.n + AHEAD >= NB):
                        split_lo(t.n + AHEAD, (t.n0 + AHEAD) % SPLIT)
                    bank = psum[:, t.o0 % BANKS, :]
                    val = scratch[:, 8, :]
                    if evac == "store":
                        for q in range(s["nout"]):
                            dve.wait_ge(out_done, t.o + q + 1)
                            dve.tensor_copy(stored(s["dst"], s["dst_at"] + t.b * s["nout"] + q),
                                            psum[:, (t.o0 + q) % BANKS, :]).then_inc(bank_free, 1)
                    elif evac == "acc":
                        dst = stored(s["dst"], t.b)
                        dve.wait_ge(out_done, t.o + 1)
                        if s["first"]:
                            dve.tensor_copy(dst, bank).then_inc(bank_free, 1)
                        else:
                            dve.tensor_tensor(dst, dst, bank, ALU.add).then_inc(bank_free, 1)
                        if s["sq"]:
                            dve.wait_ge(bank_free, BANKS + t.o + 1)
                            dve.wait_ge(ss_done, at_["ss"] + t.b + 1)
                            dve.tensor_tensor(scratch[:, 4, :], dst, dst, ALU.mult).then_inc(sqv_done, 1)
                            dve.wait_ge(sqv_done, at_["sqv"] + t.b + 1)
                            dve.tensor_tensor(ss[:, :], ss[:, :], scratch[:, 4, :], ALU.add).then_inc(ss_done, 1)
                    elif evac == "gateup":
                        f = t.of(2)
                        if t.j % 2 == 0:
                            dve.wait_ge(gate_done, at_["gate"] + f + 1)
                            dve.sem_inc(bank_free, 1)
                        else:
                            dve.wait_ge(out_done, t.o + 1)
                            dve.wait_ge(rhs_ready, at_["rhs"] + f)
                            dve.tensor_tensor(val, scratch[:, 2 + t.j // 2 % 2, :], bank, ALU.mult)\
                               .then_inc(bank_free, 1)
                            lo_of(f)
                    elif evac == "relu2":
                        dve.wait_ge(gate_done, at_["gate"] + t.b + 1)
                        dve.wait_ge(rhs_ready, at_["rhs"] + t.b)
                        dve.tensor_tensor(val, scratch[:, 2 + t.j % 2, :], bank, ALU.mult).then_inc(bank_free, 1)
                        lo_of(t.b)
                    elif evac == "conv":
                        f = t.of(3)
                        if t.j % 3 == 0:
                            dve.wait_ge(gate_done, at_["gate"] + f + 1)
                            dve.sem_inc(bank_free, 1)
                        elif t.j % 3 == 1:
                            dve.wait_ge(out_done, t.o + 1)
                            dve.wait_ge(tap_done, at_["tap"] + 1 + 3 * f)
                            dve.tensor_tensor(conv_u[:, 2:S + 2], scratch[:, 2, :], bank, ALU.mult)\
                               .then_inc(bank_free, 1)
                            dve.wait_ge(bank_free, BANKS + t.o + 1)
                            w0 = COLS["conv_w"]
                            tap = at_["tap"] + 1 + 3 * f
                            dve.wait_ge(rhs_ready, at_["rhs"] + f)
                            dve.tensor_scalar(val, conv_u[:, 0:S], col_of(par, w0 + f), col_of(par, COLS["conv_b"] + f),
                                              ALU.mult, ALU.add).then_inc(tap_done, 1)
                            for k in (1, 2):
                                dve.wait_ge(tap_done, tap + k)
                                dve.scalar_tensor_tensor(out=val, in0=conv_u[:, k:S + k],
                                                         scalar=col_of(par, w0 + 8 * k + f), in1=val,
                                                         op0=ALU.mult, op1=ALU.add).then_inc(tap_done, 1)
                        else:
                            dve.wait_ge(out_done, t.o + 1)
                            dve.wait_ge(tap_done, at_["tap"] + 3 * f + 4)
                            dve.tensor_tensor(val, val, bank, ALU.mult).then_inc(bank_free, 1)
                            lo_of(f)

                steps(dve, s, step, last)

            def norm(s):
                hi_out, lo_out = operand(s["dst"])
                at_ = s["at"]

                def value(c):
                    if c >= 3:
                        dve.wait_ge(rhs_ready, at_["rhs"] + c - 2)
                    dve.scalar_tensor_tensor(out=scratch[:, 7 + c % 3, :], in0=stored(s["src"], s["src_at"] + c),
                                             scalar=gain_of(s["gain"], c), in1=rstd[:, :], op0=ALU.mult,
                                             op1=ALU.mult).then_inc(val_done, 1)

                def low(c):
                    d = s["dst_at"] + c
                    dve.wait_ge(hi_done, at_["hi"] + c + 1)
                    val, hi = scratch[:, 7 + c % 3, :], hi_out[:, d, :].bitcast(F32)
                    if s["shift"] is None:
                        dve.tensor_tensor(lo_out[:, d, :], val, hi, ALU.subtract).then_inc(rhs_ready, 1)
                    else:
                        sh = s["shift"] + c
                        dve.scalar_tensor_tensor(out=lo_out[:, d, :], in0=val, scalar=mod[:, sh:sh + 1], in1=hi,
                                                 op0=ALU.add, op1=ALU.subtract).then_inc(rhs_ready, 1)

                for c in range(s["nch"] + 1):
                    if c < s["nch"]:
                        value(c)
                    if c >= 1:
                        low(c - 1)

            def update(s):
                for c in range(DT):
                    val = scratch[:, 8 + c % 2, :]
                    if c >= 2:
                        dve.wait_ge(x_done, s["at"]["xup"] + c - 1)
                    dve.scalar_tensor_tensor(out=val, in0=y[:, c, :], scalar=gain_of(s["gain"], c), in1=rstd[:, :],
                                             op0=ALU.mult, op1=ALU.mult).then_inc(val_done, 1)
                    dve.wait_ge(val_done, s["at"]["val"] + c + 1)
                    dve.tensor_tensor(x[:, c, :], x[:, c, :], val, ALU.add).then_inc(x_done, 1)

            def modulated(name, norm_col, scale_col, with_one, base):
                out = r_f1[:, :] if name == "r_f1" else gains[:, GAIN[name], :]
                g = par[:, norm_col:norm_col + 8]
                dve.scalar_tensor_tensor(out=out, in0=mod[:, scale_col:scale_col + 8], scalar=1.0 if with_one else 0.0,
                                         in1=g, op0=ALU.add, op1=ALU.mult).then_inc(gains_done, 1)

            def rope(tiles, base):
                dve.wait_ge(con_loaded, 16)
                for r, tile in enumerate(tiles):
                    t = proj[:, tile, :]
                    tmp = scratch[:, 8 + r % 2, :]
                    dve.wait_ge(rot_done, base + r + 1)
                    if r >= 2:
                        dve.wait_ge(rope_done, base + r - 1)
                    dve.tensor_tensor(tmp, psum[:, PT_BANK + r % 2, :], cst("sin", 512), ALU.mult)\
                       .then_inc(rope_mul, 1)
                    dve.tensor_tensor(t, t, cst("cos", 512), ALU.mult).then_inc(rope_mul, 1)
                    dve.wait_ge(rope_mul, 2 * (base + r + 1))
                    dve.tensor_tensor(t, t, tmp, ALU.add).then_inc(rope_done, 1)

            def attention(s):
                name = s["name"]
                a, e = ATTN[name], att[name]
                M, units = a["mats"], a["heads"] * QB
                upt = a["per_tile"] * QB
                mask = cst("causal_mask" if name == "fox" else "chunk_mask", 128)

                def unit(i, j):
                    W, Wj = (i % QB + 1) * P, (j % QB + 1) * P
                    new, old = i < units, 0 <= j < units
                    c, cj = M * (i % 4), M * (j % 4)
                    if new:
                        dve.wait_ge(e["scores"], i + 1)
                        rows = [psum[:, score_bank(name, i, m), :] for m in range(M)]
                        if name == "fox":
                            h = i // QB
                            rows = [exp_tile(name, i, 0)]
                            if i >= 6:
                                dve.wait_ge(e["turned"], i - 5)
                            dve.scalar_tensor_tensor(out=rows[0][:, 0:W], in0=psum[:, score_bank(name, i, 0), 0:W],
                                                     scalar=cum_tok[:, i % QB, h:h + 1],
                                                     in1=proj[:, bias_tile(h), 0:W],
                                                     op0=ALU.add, op1=ALU.add).then_inc(e["biased"], 1)
                    if old:
                        dve.wait_ge(e["exp"], M * (j + 1))
                        dve.reciprocal(row_inv[:, cj:cj + M], row_sum[:, cj:cj + M]).then_inc(e["inv"], 1)
                    if new:
                        if name == "fox":
                            dve.wait_ge(e["biased"], i + 1)
                        for m in range(M):
                            dve.tensor_tensor(rows[m][:, W - P:W], rows[m][:, W - P:W], mask, ALU.add)\
                               .then_inc(e["masked"], 1)
                    if old:
                        dve.wait_ge(e["inv"], j + 1)
                        if M == 2:
                            dve.tensor_tensor(lam_inv[:, j % 2:j % 2 + 1], row_inv[:, cj + 1:cj + 2], neg_lam[:, :],
                                              ALU.mult).then_inc(e["lam"], 1)
                        if name == "diff" and j >= 3:
                            dve.wait_ge(e["turned"], j - 2)
                        p = prob_tile(name, j)[:, 0:Wj]
                        dve.tensor_scalar(p, exp_tile(name, j, 0)[:, 0:Wj], row_inv[:, cj:cj + 1], None, ALU.mult)\
                           .then_inc(e["prob"], 1)
                    if new:
                        for m in range(M):
                            dve.wait_ge(e["masked"], M * i + m + 1)
                            dve.tensor_reduce(row_max[:, c + m:c + m + 1], rows[m][:, 0:W], AX_X, ALU.max)\
                               .then_inc(e["maxed"], 1)
                    if old and M == 2:
                        dve.wait_ge(e["prob"], 2 * j + 1)
                        dve.wait_ge(e["lam"], j + 1)
                        dve.scalar_tensor_tensor(out=p, in0=exp_tile(name, j, 1)[:, 0:Wj],
                                                 scalar=lam_inv[:, j % 2:j % 2 + 1], in1=p, op0=ALU.mult,
                                                 op1=ALU.add).then_inc(e["prob"], 1)
                    if new:
                        dve.wait_ge(e["maxed"], M * (i + 1))
                        dve.tensor_scalar(neg_max[:, c:c + M], row_max[:, c:c + M], -a["scale"], None, ALU.mult)\
                           .then_inc(e["negmax"], 1)

                def finish(t):
                    c = t + (4 if name == "fox" else 0)
                    dve.wait_ge(hi_done, s["at"]["hi"] + t + 1)
                    dve.tensor_tensor(h_lo[:, c, :], psum[:, out_bank(name, t), :], h_hi[:, c, :].bitcast(F32),
                                      ALU.subtract).then_inc(rhs_ready, 1)

                def value(t):
                    dve.wait_ge(e["o_rstd"], t + 1)
                    dve.wait_ge(rhs_ready, s["at"]["rhs"] + t)
                    dve.scalar_tensor_tensor(out=ss[:, :], in0=head_out, scalar=subln_gain[:, 0:1],
                                             in1=rstd[:, :], op0=ALU.mult, op1=ALU.mult).then_inc(e["o_val"], 1)

                def low(t):
                    dve.wait_ge(hi_done, s["at"]["hi"] + t + 1)
                    dve.tensor_tensor(h_lo[:, t, :], ss[:, :], h_hi[:, t, :].bitcast(F32),
                                      ALU.subtract).then_inc(rhs_ready, 1)

                def due(i, lag):
                    u = i - PV_LAG - lag
                    return u // upt if 0 <= u < units and u % upt == upt - 1 else None

                for i in range(units + PV_LAG + 4):
                    if name != "diff" and due(i, 1) is not None:
                        finish(due(i, 1))
                    if name == "diff" and due(i, 3) is not None:
                        low(due(i, 3))
                    unit(i, i - PROB_LAG)
                    if name == "diff" and due(i, 2) is not None:
                        value(due(i, 2))

            def lambdas():
                lam = col("lam", 0, 256).rearrange("p (a b n) -> p a b n", a=2, b=2)
                dve.tensor_tensor(lam_prod[:, :, :], lam[:, :, 0, :], lam[:, :, 1, :], ALU.mult)\
                   .then_inc(gains_done, 1)
                dve.wait_ge(gains_done, 1)
                dve.tensor_reduce(lam_sum[:, :], lam_prod[:, :, :], AX_X, ALU.add).then_inc(small_done, 1)
                dve.tensor_scalar(subln_gain[:, :], col("subln"), 1.0 - LAM_INIT, None, ALU.mult)\
                   .then_inc(gains_done, 1)
                dve.wait_ge(lam_done, 1)
                dve.tensor_tensor(lam_diff[:, :], lam_exp[:, 1:2], lam_exp[:, 0:1], ALU.subtract)\
                   .then_inc(gains_done, 1)
                dve.wait_ge(gains_done, 3)
                dve.tensor_scalar(neg_lam[:, :], lam_diff[:, :], -LAM_INIT, None, ALU.add).then_inc(gains_done, 1)

            dve.wait_ge(par_loaded, 16)
            NG2 = COLS["norm_g2"]
            for idx, s in enumerate(PLAN):
                kind = s["kind"]
                dve.drain().then_inc(dve_settled, 1)
                dve.wait_ge(dve_settled, idx + 1)
                if kind == "gemm":
                    gemm(s, idx == LAST_GEMM)
                elif kind == "rstd":
                    dve.wait_ge(rstd_done, s["at"]["rstd"] + 1)
                elif kind == "sumsq":
                    if idx == 0:
                        for m in range(AHEAD):
                            split_lo(m, m)
                elif kind == "norm":
                    norm(s)
                elif kind == "update":
                    update(s)
                elif kind == "final1":
                    for c in range(DT):
                        dve.scalar_tensor_tensor(out=x[:, c, :], in0=x[:, c, :], scalar=col("normf", c),
                                                 in1=rstd[:, :], op0=ALU.mult, op1=ALU.mult).then_inc(x_done, 1)
                    dve.wait_ge(x_done, s["at"]["xup"] + 8)
                elif kind == "take":
                    a, b = MOD_PER_GROUP * s["first"], MOD_PER_GROUP * s["upto"]
                    dve.wait_ge(acc_free, ACCS + s["upto"])
                    dve.tensor_tensor(mod[:, a:b], psum[:, O_BANK, a:b], col("ada_b", a, b - a), ALU.add)\
                       .then_inc(mod_done, 1)
                elif kind == "modcols0":
                    dve.wait_ge(mod_done, s["at"]["take"])
                    modulated("g_m0", NG2 + 0, 8, True, 4)
                    modulated("r_m0", NG2 + 8, 16, False, 5)
                    modulated("g_f0", NG2 + 16, 32, True, 6)
                    modulated("r_f0", NG2 + 24, 40, False, 7)
                    dve.wait_ge(gains_done, 8)
                elif kind == "modcols1":
                    dve.wait_ge(mod_done, s["at"]["take"])
                    modulated("g_kv", COLS["kv_norm"], 56, True, 8)
                    modulated("g_m1", NG2 + 32, 72, True, 9)
                    modulated("r_m1", NG2 + 40, 80, False, 10)
                    modulated("g_f1", NG2 + 48, 96, True, 11)
                    modulated("r_f1", NG2 + 56, 104, False, 12)
                    dve.wait_ge(gains_done, 13)
                elif kind == "rope1":
                    rope(range(8), 0)
                elif kind == "rope2":
                    dve.wait_ge(rope_loaded, 16)
                    rope(range(16, 21), 8)
                elif kind == "forget1":
                    lambdas()
                    dve.wait_ge(gains_done, 4)
                    dve.wait_ge(fg_turned, 1)
                    turned = psum[:, AUX_BANK, :].rearrange("p (a n) -> p a n", a=QB)
                    for q in range(QB):
                        z = dve.tensor_tensor(fgate[:, q, :], turned[:, q, P - 8:P], col("b_f", 0, 8), ALU.add)
                    z.then_inc(fg_step, 1)
                    dve.wait_ge(fg_exp, 3)
                    dve.scalar_tensor_tensor(out=log_f[:, :, :], in0=fgate[:, :, :], scalar=0.0,
                                             in1=fgate_a[:, :, :], op0=ALU.min, op1=ALU.subtract)\
                       .then_inc(logf_done, 1)
                elif kind == "forget2":
                    dve.wait_ge(cum_psum, 1)
                    dve.tensor_scalar(neg_cum, psum[0:8, AUX_BANK, :], -8.0, None, ALU.mult)\
                       .then_inc(cum_done, 1)
                    dve.wait_ge(cum_psum, 2)
                    dve.tensor_scalar(cum_tok[:, :, :].rearrange("p a n -> p (a n)"), psum[:, O_BANK, 0:8 * QB],
                                      8.0, None, ALU.mult).then_inc(cum_done, 1)
                elif kind == "forget3":
                    dve.wait_ge(nck_done, 8)
                    dve.wait_ge(cum_done, 2)
                elif kind == "vtrans":
                    pass
                elif kind == "attn":
                    attention(s)

        @block.tensor
        def _(pe):
            pe.wait_ge(const_done, 7)

            def gemm(s, last):
                hi, lo = operand(s["rhs"])
                nk, ra = s["nk"], s["rhs_at"]

                def step(t):
                    slot = t.n0 % SPLIT
                    pe.wait_ge(wlo_done, t.n + 1)
                    for q in range(s["nout"]):
                        bank = psum[:, (t.o0 + q) % BANKS, :]
                        pe.wait_ge(bank_free, t.o + q + 1)
                        for k in range(nk):
                            if t.j == 0 and q == 0:
                                pe.wait_ge(rhs_ready, s["r0"] + k + 1)
                            w = slice((q * nk + k) * P, (q * nk + k + 1) * P)
                            pe.matmul(bank, w_hi[:, slot, w], hi[:, ra + k, :], start=k == 0, stop=False)
                            pe.matmul(bank, w_hi[:, slot, w], lo[:, ra + k, :], start=False, stop=False)
                            mm = pe.matmul(bank, w_lo[:, slot, w], hi[:, ra + k, :], start=False,
                                           stop=k == nk - 1)
                        mm.then_inc(out_done, 1)

                if not s.get("kouter"):
                    steps(pe, s, step, last)
                    return
                blocks = [Step(s, b, b, 0, 4) for b in range(AHEAD)]
                for t in blocks:
                    pe.wait_ge(wlo_done, t.n + 1)
                    pe.wait_ge(bank_free, t.o + 1)
                for k in range(nk):
                    pe.wait_ge(rhs_ready, s["r0"] + k + 1)
                    for t in blocks:
                        slot, bank, w = t.n0 % SPLIT, psum[:, t.o0 % BANKS, :], slice(k * P, (k + 1) * P)
                        pe.matmul(bank, w_hi[:, slot, w], hi[:, ra + k, :], start=k == 0, stop=False)
                        pe.matmul(bank, w_hi[:, slot, w], lo[:, ra + k, :], start=False, stop=False)
                        mm = pe.matmul(bank, w_lo[:, slot, w], hi[:, ra + k, :], start=False, stop=k == nk - 1)
                        if k == nk - 1:
                            mm.then_inc(out_done, 1)
                steps(pe, s, step, last, done=AHEAD)

            def sum_squares(s, nch, n):
                pe.wait_ge(rstd_done, s["at"]["rstd"])
                for c in range(nch):
                    pe.wait_ge(sqa_done, s["at"]["sqa"] + c + 1)
                    pe.matmul(psum[:, AUX_BANK, :], mean[n][:, :], scratch[:, 5 + c % 2, :], start=c == 0,
                              stop=c == nch - 1).then_inc(aux_done, 1)

            def rope(tiles, base, stored_by):
                pe.wait_ge(bank_free, BANKS + stored_by)
                pe.wait_ge(con_loaded, 16)
                for r, tile in enumerate(tiles):
                    if r >= 2:
                        pe.wait_ge(rope_done, base + r - 1)
                    pe.matmul(psum[:, PT_BANK + r % 2, :], cst("rot", 128), proj[:, tile, :], start=True,
                              stop=True).then_inc(rot_done, 1)

            def attention(s):
                name = s["name"]
                a, e = ATTN[name], att[name]
                M, units = a["mats"], a["heads"] * QB
                upt = a["per_tile"] * QB

                def scores(i):
                    h, q = divmod(i, QB)
                    W = (q + 1) * P
                    rows = slice(q * P, (q + 1) * P)
                    ring = 2 if name == "diff" else 4
                    if i >= ring:
                        pe.wait_ge(e["exp"], M * (i - ring + 1))
                    for m in range(M):
                        out = psum[:, score_bank(name, i, m), 0:W]
                        if name == "diff":
                            half = slice(64 * m, 64 * m + 64)
                            mm = pe.matmul(out, proj[half, h, rows], proj[half, 4 + h, 0:W], start=True, stop=True)
                        elif name == "fox":
                            half = slice(64 * (h % 2), 64 * (h % 2) + 64)
                            mm = pe.matmul(out, proj[half, 8 + h // 2, rows], proj[half, 12 + h // 2, 0:W],
                                           start=True, stop=True)
                        else:
                            half = slice(64 * (h % 2), 64 * (h % 2) + 64)
                            pe.matmul(out, proj[:, 8 + h, rows], proj[:, h, 0:W], start=True, stop=False)
                            mm = pe.matmul(out, proj[half, 16 + h // 2, rows], proj[half, 20, 0:W], start=False,
                                           stop=True)
                    mm.then_inc(e["scores"], 1)

                def turn(i):
                    q = i % QB
                    pe.wait_ge(e["prob"], M * (i + 1))
                    if i >= 2:
                        pe.wait_ge(e["pt"], i - 1)
                    for kb in range(q + 1):
                        mm = pe.transpose(psum[:, PT_BANK + i % 2, kb * P:(kb + 1) * P],
                                          prob_tile(name, i)[:, kb * P:(kb + 1) * P], ident)
                    mm.then_inc(e["turned"], 1)

                def values(i):
                    h, q = divmod(i, QB)
                    pe.wait_ge(e["pt"], i + 1)
                    t = i // upt
                    if i % upt == 0 and name == "diff" and t >= 1:
                        pe.wait_ge(e["o_sq"], t)
                    if i % upt == 0 and name != "diff" and t >= 2:
                        pe.wait_ge(rhs_ready, s["at"]["rhs"] + t - 1)
                    for kb in range(q + 1):
                        if name == "fox":
                            c = 64 * (h % 2)
                            v, rows = vtok[:, 4 + h // 2, kb, c:c + 64], slice(c, c + 64)
                        else:
                            v, rows = vtok[:, h, kb, :], slice(0, P)
                        mm = pe.matmul(psum[rows, out_bank(name, t), q * P:(q + 1) * P], v,
                                       turned_tile(i)[:, kb * P:(kb + 1) * P], start=kb == 0, stop=kb == q)
                    mm.then_inc(e["pv"], 1)

                def head_square(t):
                    pe.wait_ge(e["o_sq"], t + 1)
                    if t >= 1:
                        pe.wait_ge(e["o_free"], t)
                    pe.matmul(psum[:, AUX_BANK, :], mean[128][:, :], head_sq, start=True,
                              stop=True).then_inc(e["o_ss"], 1)

                for i in range(units + PV_LAG + 3):
                    if i < units:
                        scores(i)
                    if 0 <= i - PV_LAG < units:
                        values(i - PV_LAG)
                    if 0 <= i - TURN_LAG < units:
                        turn(i - TURN_LAG)
                    u = i - PV_LAG - 1
                    if name == "diff" and 0 <= u < units and u % upt == upt - 1:
                        head_square(u // upt)

            for idx, s in enumerate(PLAN):
                kind = s["kind"]
                if kind == "gemm":
                    gemm(s, idx == LAST_GEMM)
                elif kind == "sumsq":
                    sum_squares(s, s["nch"], s["mean"])
                elif kind in ("final1", "update") and not s.get("last"):
                    sum_squares(s, 8, 1024)
                elif kind == "total":
                    pe.wait_ge(rstd_done, s["at"]["rstd"])
                    pe.wait_ge(ss_done, s["at"]["ss"])
                    pe.matmul(psum[:, AUX_BANK, :], mean[1024][:, :], ss[:, :], start=True, stop=True)\
                      .then_inc(aux_done, 1)
                elif kind == "mod":
                    if s["at"]["take"]:
                        pe.wait_ge(mod_done, s["at"]["take"])
                    if s["after"] == "attn":
                        pe.wait_ge(rhs_ready, s["at"]["rhs"])
                    for g in range(s["at"]["mod"], s["at"]["mod"] + s["groups"]):
                        pe.wait_ge(ada_used, DT * (g + 1))
                        for m in range(MOD_PER_GROUP):
                            c = g * MOD_PER_GROUP + m
                            mm = pe.matmul(psum[:, O_BANK, c:c + 1], ada_acc[:, g % ACCS, m * P:(m + 1) * P],
                                           ones_col[:, :], start=True, stop=True)
                        mm.then_inc(acc_free, 1)
                elif kind == "rope1":
                    rope(range(8), 0, s["at"]["o"])
                elif kind == "rope2":
                    pe.wait_ge(rope_loaded, 16)
                    pe.wait_ge(v_done, 16)
                    rope(range(16, 21), 8, s["at"]["o"])
                elif kind == "vtrans":
                    base = 0 if s["at"]["n"] < 40 else 8
                    pe.wait_ge(bank_free, BANKS + s["at"]["o"])
                    if base == 0:
                        pe.wait_ge(rope_done, 8)
                    for v in range(DT):
                        if v >= 2:
                            pe.wait_ge(v_done, base + v - 1)
                        for kb in range(QB):
                            mm = pe.transpose(psum[:, PT_BANK + v % 2, kb * P:(kb + 1) * P],
                                              scratch[:, v, kb * P:(kb + 1) * P], ident)
                        mm.then_inc(vt_done, 1)
                elif kind == "forget1":
                    for kb in range(QB):
                        mm = pe.transpose(psum[:, AUX_BANK, kb * P:(kb + 1) * P], proj[:, 16, kb * P:(kb + 1) * P],
                                          ident)
                    mm.then_inc(fg_turned, 1)
                elif kind == "forget2":
                    pe.wait_ge(logf_done, 1)
                    for kb in range(QB):
                        mm = pe.matmul(psum[0:8, AUX_BANK, kb * P:S], log_f[:, kb, :], cst("tri", S - kb * P),
                                       start=kb == 0, stop=kb == QB - 1)
                    mm.then_inc(cum_psum, 1)
                    pe.wait_ge(mod_done, s["at"]["take"])
                    for q in range(QB):
                        for kb in range(q + 1):
                            mm = pe.matmul(psum[:, O_BANK, 8 * q:8 * q + 8], cst("tri", P, (q - kb) * P),
                                           log_f[:, kb, :], start=kb == 0, stop=kb == q)
                    mm.then_inc(cum_psum, 1)
                elif kind == "forget3":
                    pe.wait_ge(cum_done, 2)
                    for h in range(8):
                        if h >= 2:
                            pe.wait_ge(nck_done, h - 1)
                        pe.matmul(psum[:, PT_BANK + h % 2, :], con[0:8, h:h + 1].broadcast_to([8, P]),
                                  neg_cum, start=True, stop=True).then_inc(nck_psum, 1)
                elif kind == "attn":
                    pe.wait_ge(v_done, 8 if s["name"] != "mla" else 16)
                    pe.wait_ge(rope_done, 8 if s["name"] != "mla" else 13)
                    pe.wait_ge(mod_done, s["at"]["take"])
                    pe.wait_ge(cum_done, 2)
                    if s["name"] == "fox":
                        pe.wait_ge(nck_done, 8)
                        pe.wait_ge(rhs_ready, s["at"]["rhs"])
                    attention(s)


def lay_out(inp):
    f = {k: np.asarray(v) for k, v in inp.items()}
    blocks = []

    def tiles(w):
        K, M = w.shape
        return w.reshape(K // P, P, M // P, P).transpose(2, 1, 0, 3).reshape(M // P, P, K)

    def push(t, per=1):
        n = t.shape[0] // per
        t = t.reshape(n, per, P, -1).transpose(0, 2, 1, 3).reshape(n, P, -1)
        full = np.zeros((n, P, D), np.float32)
        full[:, :, :t.shape[2]] = t
        blocks.append(full)

    w = f["w_in"][0]
    push(tiles(w[:, 0:1024]))
    push(tiles(w[:, 1536:2560]))
    push(tiles(w[:, w.shape[1] - P:]))
    push(tiles(w[:, 1024:1536]))
    push(tiles(w[:, 2560:3072]))
    push(tiles(f["w_out"][0]))
    gate, up = tiles(f["w_gate"][0]), tiles(f["w_up"][0])
    for c, nk in ((0, 8), (8, 8), (16, 6)):
        push(np.stack([gate[c:c + nk], up[c:c + nk]], 1).reshape(2 * nk, P, D))
        push(tiles(f["w_down"][0][c * P:(c + nk) * P]))
    b, c, xh = (tiles(f["conv_in_w_2"][0][:, i * D:(i + 1) * D]) for i in range(3))
    push(np.stack([c, xh, b], 1).reshape(24, P, D))
    push(tiles(f["conv_out_w_2"][0]))

    def mlp(l):
        for g in range(4):
            push(tiles(f["mlp_up_w_2"][l][:, g * D:(g + 1) * D]))
            push(tiles(f["mlp_down_w_2"][l][g * D:(g + 1) * D]))

    mlp(0)
    w = f["kv_a_w_2"]
    push(tiles(w[:, 0:256]))
    push(tiles(np.concatenate([w[:, 256:320], w[:, 256:320]], 1)))
    push(tiles(f["q_a_w_2"][0]))
    w = f["kv_b_w_2"].reshape(256, 8, 2, P)
    push(tiles(w[:, :, 0].reshape(256, D)), 4)
    push(tiles(w[:, :, 1].reshape(256, D)), 4)
    w = f["q_b_w_2"][0].reshape(384, 8, 192)
    push(tiles(np.concatenate([w[:, :, 0:P].reshape(384, D), w[:, :, P:].reshape(384, 512)], 1)), 2)
    push(tiles(f["attn_o_w_2"][0]))
    mlp(1)
    wstream = np.concatenate(blocks, 0)
    assert wstream.shape[0] == NB, (wstream.shape, NB)

    ada = np.concatenate([f["ada_w_2"][0], f["kv_ada_w_2"], f["ada_w_2"][1]], 1)
    ada = ada.reshape(DT, P, ADA_GROUPS, ADA_COLS)
    ada = ada.transpose(2, 0, 1, 3).reshape(ADA_GROUPS * DT // 2, 2, P, ADA_COLS).transpose(0, 2, 1, 3)
    ada = ada.reshape(ADA_GROUPS * DT // 2, P, 2 * ADA_COLS)

    def cols(v):
        return np.asarray(v).reshape(-1, P).T

    def rows(v):
        v = np.asarray(v).reshape(1, -1)
        return np.broadcast_to(v, (P, v.shape[1]))

    params = np.concatenate([
        cols(f["norm1_g"]), cols(f["norm2_g"]), cols(f["normf_g"]), cols(f["norm_g_2"]), cols(f["kv_norm_g_2"]),
        cols(f["kv_a_norm_g_2"]), cols(f["q_a_norm_g_2"]), cols(f["subln_g"]), cols(f["conv_w_2"]),
        cols(f["conv_b_2"]), cols(np.concatenate([f["ada_b_2"][0], f["kv_ada_b_2"], f["ada_b_2"][1]])),
        cols(f["c_2"]), rows(f["b_f"]), rows(np.concatenate([f["lam_q1"], f["lam_k1"], f["lam_q2"], f["lam_k2"]])),
    ], 1)
    xT = f["x"][0].T.reshape(DT, P, S)
    return xT, wstream, ada, params


def constants():
    q, k = np.arange(P)[:, None], np.arange(P)[None, :]
    ident = np.eye(P)
    tri = np.concatenate([(q <= k) * 1.0, np.ones((P, S - P))], 1)
    chunk_mask = np.where(k // 64 <= q // 64, 0.0, NEG)
    causal_mask = np.where(k <= q, 0.0, NEG)

    def rotary(dim, theta):
        half = dim // 2
        inv = np.float32(theta) ** (-np.arange(0, dim, 2, dtype=np.float32) / np.float32(dim))
        ang = np.arange(S, dtype=np.float32)[None, :] * inv.astype(np.float32)[:, None]
        cos, sin = np.ones((64, S)), np.zeros((64, S))
        rot = np.zeros((64, 64))
        for i in range(half):
            cos[i] = cos[i + half] = np.cos(ang[i])
            sin[i] = sin[i + half] = np.sin(ang[i])
            rot[i + half, i] = -1.0
            rot[i, i + half] = 1.0
        two = np.zeros((P, P))
        two[:64, :64] = two[64:, 64:] = rot
        return [two, np.tile(cos, (2, 1)), np.tile(sin, (2, 1))]

    first = np.concatenate([ident, tri, chunk_mask, causal_mask] + rotary(16, 500000.0), 1)
    return first.astype(np.float32), np.concatenate(rotary(64, 10000.0), 1).astype(np.float32)


def kernel(**inputs):
    import concourse.bacc as bacc
    from concourse.bass_utils import run_bass_kernel_spmd as run

    xT, wstream, ada, params = lay_out(inputs)
    consts, rope2 = constants()
    arrays = dict(xT=xT, wstream=wstream, ada=ada, params=params, consts=consts, rope2=rope2)
    arrays = {f"in_{k}": np.ascontiguousarray(v) for k, v in arrays.items()}
    nc = bacc.Bacc("TRN2", target_bir_lowering=False, num_devices=1)
    args = [nc.dram_tensor(k, v.shape, F32, kind="ExternalInput").ap() for k, v in arrays.items()]
    args.append(nc.dram_tensor("outT", (DT, P, S), F32, kind="ExternalOutput").ap())
    build(nc, *args)
    r = run(nc, [arrays], core_ids=[0])
    return np.asarray(r.results[0]["outT"]).reshape(D, S).T.reshape(1, S, D)
```

```python
from contextlib import ExitStack

import numpy as np

import concourse.bass as bass
from concourse import mybir

F32 = mybir.dt.float32
F32R = mybir.dt.float32r
ALU = mybir.AluOpType
ACT = mybir.ActivationFunctionType
AX_X = mybir.AxisListType.X

P = 128
S = 512
D = 1024
DT = D // P
QB = S // P
D_FF = 2816
EPS1, EPS2 = 1e-5, 1e-6
NEG = -1e30
LAM_INIT = 0.2

RAW = 4
SPLIT = 4
AHEAD = 3
BANKS = 4
PT_BANK, O_BANK, AUX_BANK = 4, 6, 7
ADA_COLS = 512
ADA_GROUPS = (6 + 2 + 6) * D // ADA_COLS
ADA_SLOTS = 4
WARM_START, WARM = 16, 9
WARM_UNIT = dict(diff=2, fox=0, mla=0)
ACCS = 3
MOD_PER_GROUP = ADA_COLS // P

COLS = {}
_at = 0
for _name, _n in (("norm1", 8), ("norm2", 8), ("normf", 8), ("norm_g2", 64), ("kv_norm", 8), ("kv_a_norm", 2),
                  ("q_a_norm", 3), ("subln", 1), ("conv_w", 24), ("conv_b", 8), ("ada_b", 112), ("c", 8),
                  ("b_f", 8), ("lam", 256)):
    COLS[_name] = _at
    _at += _n
PARAMS = _at
CONST = {}
_at = 0
for _name, _n in (("ident", 128), ("tri", 512), ("chunk_mask", 128), ("causal_mask", 128),
                  ("heads", 8), ("rot", 128), ("cos", 512), ("sin", 512)):
    CONST[_name] = _at
    _at += _n
CONSTS = _at
ROPE_AT = CONST["rot"]
ROPE_COLS = CONSTS - ROPE_AT


def make_plan():
    counts = dict(n=0, o=0, gate=0, tap=0, sqv=0, ss=0, val=0, hi=0, rhs=0, xup=0, sqa=0, aux=0, rstd=0,
                  mod=0, take=0, rope=0, vt=0, xpool=0)
    plan = []

    def add(kind, inc=None, **about):
        plan.append(dict(kind=kind, at=dict(counts), **about))
        for k, v in (inc or {}).items():
            counts[k] += v

    def gemm(evac, nblk, rhs, r0, nk=8, nout=1, rhs_at=0, **about):
        inc = dict(n=nblk, o=nblk * nout)
        if evac == "acc" and about.get("sq"):
            inc.update(sqv=nblk, ss=nblk + (0 if about.get("more") else 1) - (0 if about.get("go_on") else 1))
        if evac == "gateup":
            inc.update(gate=nblk // 2, hi=nblk // 2, rhs=nblk // 2)
        if evac == "relu2":
            inc.update(gate=nblk, hi=nblk, rhs=nblk)
        if evac == "conv":
            inc.update(gate=nblk // 3, tap=1 + nblk, hi=nblk // 3, rhs=nblk // 3)
        add("gemm", inc, evac=evac, nblk=nblk, rhs=rhs, r0=r0, nk=nk, nout=nout, rhs_at=rhs_at, **about)

    def sumsq(src, at, nch, mean, stored_by=0):
        add("sumsq", dict(sqa=nch, aux=nch), src=src, src_at=at, nch=nch, mean=mean, stored_by=stored_by)

    def total():
        add("total", dict(aux=1))

    def rstd(eps):
        add("rstd", dict(rstd=1), eps=eps)

    def norm(dst, src="x", src_at=0, nch=8, dst_at=0, gain=None, shift=None):
        r0 = counts["rhs"]
        add("norm", dict(val=nch, hi=nch, rhs=nch), dst=dst, src=src, src_at=src_at, nch=nch, dst_at=dst_at,
            gain=gain, shift=shift)
        return r0

    def update(gain, last=False, pool=True):
        add("update", dict(val=8, xup=4 if pool else 8, xpool=4 if pool else 0,
                           **({} if last else dict(sqa=8, aux=8))), gain=gain, last=last, pool=pool)

    def rope(tiles, stored_by):
        add("rope", dict(rope=len(tiles)), tiles=tiles, stored_by=stored_by)

    def vtrans(first, upto, stored_at):
        add("vtrans", dict(vt=upto - first), first=first, upto=upto, stored_by=stored_at + upto)

    def modulation(groups, after=None):
        add("mod", dict(mod=groups), groups=groups, after=after)

    taken = [0]

    def take():
        add("take", dict(take=1), first=taken[0], upto=counts["mod"])
        taken[0] = counts["mod"]

    sumsq("x", 0, 8, 1024)
    rstd(EPS1)
    h = norm("h", gain="norm1")
    gemm("store", 8, "h", h, dst="proj", dst_at=0, kouter=2)
    modulation(2)
    rotary = counts["o"]
    for i, nblk in enumerate((2, 2, 2, 3)):
        gemm("store", nblk, "h", h, dst="proj", dst_at=8 + 2 * i)
        rope((2 * i, 2 * i + 1), rotary)
    modulation(2)
    add("forget1")
    v_at = counts["o"]
    gemm("store", 2, "h", h, dst="scratch", dst_at=0)
    take()
    add("forget2")
    gemm("store", 2, "h", h, dst="scratch", dst_at=2)
    vtrans(0, 2, v_at)
    gemm("store", 2, "h", h, dst="scratch", dst_at=4)
    vtrans(2, 4, v_at)
    gemm("store", 1, "h", h, dst="scratch", dst_at=6)
    vtrans(4, 6, v_at)
    gemm("store", 1, "h", h, dst="scratch", dst_at=7)
    vtrans(6, 8, v_at)
    mix = counts["rhs"]
    add("attn", dict(hi=4, rhs=4), name="diff")
    add("attn", dict(hi=4, rhs=4), name="fox")
    gemm("acc", 4, "h", mix, dst="x", first=False, sq=True, go_on=True, kouter=AHEAD)
    modulation(3, "attn")
    gemm("acc", 4, "h", mix, dst="x", dst_at=4, first=False, sq=True, more=True)
    total()
    rstd(EPS1)
    h = norm("h", gain="norm2")
    for g, nk in enumerate((8, 8, 6)):
        hid = counts["rhs"]
        gemm("gateup", 2 * nk, "h", h, kouter=AHEAD if g == 0 else 0)
        modulation(2 if g < 2 else 1)
        gemm("acc", 8, "hid", hid, nk=nk, dst="x", first=False, sq=g == 2)
        if g < 2:
            modulation(2)
    take()
    add("modcols0")
    total()
    rstd(EPS1)
    add("final1", dict(xup=8, sqa=8, aux=8))
    rstd(EPS2)
    h = norm("h", gain="g_m0", shift=0)
    hid = counts["rhs"]
    gemm("conv", 24, "h", h, kouter=AHEAD)
    modulation(3)
    gemm("acc", 8, "hid", hid, dst="y", first=True, sq=True)
    modulation(1)
    total()
    rstd(EPS2)
    update("r_m0", pool=False)
    rstd(EPS2)
    h = norm("h", gain="g_f0", shift=24)

    def mlp(h):
        for g in range(4):
            hid = counts["rhs"]
            gemm("relu2", 8, "h", h, kouter=AHEAD if g == 0 else 0)
            if counts["mod"] < ADA_GROUPS:
                modulation(2)
            gemm("acc", 8, "hid", hid, dst="y", first=g == 0, sq=g == 3)

    mlp(h)
    take()
    add("modcols1")
    total()
    rstd(EPS2)
    update("r_f0")
    rstd(EPS2)
    hkv = norm("hid", gain="g_kv", shift=48)
    h = norm("h", gain="g_m1", shift=64)
    gemm("store", 3, "hid", hkv, dst="kv_a", dst_at=0)
    latent = counts["o"]
    gemm("store", 1, "h", h, dst="scratch", dst_at=0)
    sumsq("scratch", 3, 2, 256, latent)
    gemm("store", 1, "h", h, dst="scratch", dst_at=1)
    rstd(EPS2)
    c_kv = norm("latent", src="scratch", src_at=3, nch=2, gain="kv_a_norm")
    rope((20,), latent)
    gemm("store", 1, "h", h, dst="scratch", dst_at=2)
    latent = counts["o"]
    gemm("store", 1, "latent", c_kv, nk=2, nout=4, dst="proj", dst_at=0)
    sumsq("scratch", 0, 3, 384, latent)
    gemm("store", 1, "latent", c_kv, nk=2, nout=4, dst="proj", dst_at=4)
    rstd(EPS2)
    q_a = norm("h", src="scratch", src_at=0, nch=3, dst_at=0, gain="q_a_norm")
    v_at = counts["o"]
    gemm("store", 2, "latent", c_kv, nk=2, nout=4, dst="scratch", dst_at=0)
    gemm("store", 2, "h", q_a, nk=3, nout=2, dst="proj", dst_at=16)
    rotary = counts["o"]
    vtrans(0, 4, v_at)
    for i in range(4):
        gemm("store", 1, "h", q_a, nk=3, nout=2, dst="proj", dst_at=8 + 2 * i)
        if i == 1:
            vtrans(4, 8, v_at)
        if i in (0, 2):
            rope((16 + i, 17 + i), rotary)
    mix = counts["rhs"]
    add("attn", dict(hi=8, rhs=8), name="mla")
    gemm("acc", 8, "h", mix, dst="y", first=True, sq=True, kouter=AHEAD)
    total()
    rstd(EPS2)
    update("r_m1")
    rstd(EPS2)
    h = norm("h", gain="g_f1", shift=88)
    mlp(h)
    total()
    rstd(EPS2)
    update("r_f1", last=True)
    assert counts["mod"] == ADA_GROUPS, counts["mod"]
    return plan, counts


PLAN, TOTALS = make_plan()
NB = TOTALS["n"]
LAST_GEMM = max(i for i, s in enumerate(PLAN) if s["kind"] == "gemm")

ATTN = dict(
    diff=dict(heads=4, mats=2, scale=64 ** -0.5, per_tile=1, tiles=4),
    fox=dict(heads=8, mats=1, scale=64 ** -0.5, per_tile=2, tiles=4),
    mla=dict(heads=8, mats=1, scale=192 ** -0.5, per_tile=1, tiles=8),
)


PROB_LAG, TURN_LAG, TAKE_LAG, PV_LAG = 2, 3, 4, 5
ENDING = 3


class Step:

    def __init__(self, stage, b, j, turn, body):
        self.b, self.j = b, j
        self.n = stage["at"]["n"] + b
        self.n0 = stage["at"]["n"] + j
        self.turn, self.body = turn, body
        self.o = stage["at"]["o"] + b * stage["nout"]
        self.o0 = stage["at"]["o"] + j * stage["nout"]

    def rounds(self, ahead, ring):
        return (self.n0 + ahead) // ring + 1 + self.turn * (self.body // ring)

    def of(self, per):
        return self.j // per + self.turn * (self.body // per)


def steps(eng, stage, do, last=False, done=0):
    nblk = stage["nblk"]
    body = 12 if stage["evac"] == "conv" else 4
    turns = nblk // body
    first = 1 if stage["at"]["n"] == 0 or done else 0
    if last:
        turns -= 1
    if turns - first < 2 or stage.get("sq"):
        first = turns = 0
    for b in range(done, first * body):
        do(Step(stage, b, b, 0, body))
    if turns:
        with eng.Fori(first, turns) as i:
            for j in range(body):
                do(Step(stage, body * i + j, j, i, body))
    for b in range(max(done, turns * body), nblk):
        do(Step(stage, b, b, 0, body))


def tile_of(t, i):
    if isinstance(i, int):
        return t[:, i, :]
    return t[:, bass.ds(i, 1), :].rearrange("p a n -> p (a n)")


def col_of(t, i):
    if isinstance(i, int):
        return t[:, i:i + 1]
    return t[:, bass.ds(i, 1)]


def build(nc, xT, wstream, ada, params, consts, rope2, outT):
    ctx = ExitStack()
    with ctx:
        place = [nc.sbuf_base if not callable(nc.sbuf_base) else nc.sbuf_base()]
        place[0] = (place[0] + 63) // 64 * 64

        def at(name, shape, dtype, where):
            return nc.alloc_sbuf_tensor_at(name, shape, dtype, offset=where)

        def sb(name, shape, dtype=F32):
            where = place[0]
            place[0] += (int(np.prod(shape[1:])) * 4 + 63) // 64 * 64
            return at(name, shape, dtype, where)

        x = sb("x", [P, DT, S])
        y_at = place[0]
        y = sb("y", [P, DT, S])
        vtok = at("vtok", [P, DT, QB, P], F32, y_at)
        latent_hi = at("latent_hi", [P, 2, S], F32R, y_at + 4 * S * 4)
        latent_lo = at("latent_lo", [P, 2, S], F32R, y_at + 6 * S * 4)
        h_hi = sb("h_hi", [P, DT, S], F32R)
        h_lo = sb("h_lo", [P, DT, S], F32R)
        proj_at = place[0]
        proj = sb("proj", [P, 21, S])
        hid_hi = at("hid_hi", [P, DT, S], F32R, proj_at)
        hid_lo = at("hid_lo", [P, DT, S], F32R, proj_at + DT * S * 4)
        w_raw = sb("w_raw", [P, RAW, D])
        w_hi = sb("w_hi", [P, SPLIT, D], F32R)
        w_lo = sb("w_lo", [P, SPLIT, D], F32R)
        conv_u = at("conv_u", [P, S + 2], F32, place[0])
        scratch = sb("scratch", [P, 10, S])
        ss = sb("ss", [P, S])
        rstd = sb("rstd", [P, S])
        ada_raw = sb("ada_raw", [P, ADA_SLOTS, ADA_COLS])
        ada_acc = sb("ada_acc", [P, ACCS, ADA_COLS])
        par = sb("par", [P, PARAMS])
        con = sb("con", [P, CONSTS])
        mean = {n: sb(f"mean{n}", [P, P]) for n in (1024, 256, 384, 128)}
        ones_col = sb("ones_col", [P, 1])
        eps = {e: sb(f"eps{n}", [P, 1]) for n, e in enumerate((EPS1, EPS2))}
        c_act = sb("c_act", [P, 8])
        c_exp = sb("c_exp", [P, 8])
        mod = sb("mod", [P, ADA_GROUPS * MOD_PER_GROUP])
        gains = sb("gains", [P, 8, DT])
        subln_gain = sb("subln_gain", [P, 1])
        lam_prod = sb("lam_prod", [P, 2, 64])
        lam_sum = sb("lam_sum", [P, 2])
        lam_exp = sb("lam_exp", [P, 2])
        neg_lam = sb("neg_lam", [P, 1])
        lam_diff = sb("lam_diff", [P, 1])
        fgate = sb("fgate", [P, QB, 8])
        fgate_a = sb("fgate_a", [P, QB, 8])
        fgate_b = sb("fgate_b", [P, QB, 8])
        log_f = sb("log_f", [P, QB, 8])
        cum_tok = sb("cum_tok", [P, QB, 8])
        neg_cum = at("neg_cum", [P, S], F32R, proj_at + 17 * S * 4)
        small_r = at("small_r", [P, S], F32R, proj_at + 20 * S * 4)
        ident_r, heads_r = small_r[:, 0:P], small_r[:, 3 * P:3 * P + 8]
        mask_r = dict(diff=small_r[:, P:2 * P], fox=small_r[:, 2 * P:3 * P])
        row_max = sb("row_max", [P, 8])
        neg_max = sb("neg_max", [P, 8])
        neg_cum_max = sb("neg_cum_max", [P, 8])
        row_sum = sb("row_sum", [P, 8])
        row_inv = sb("row_inv", [P, 8])
        lam_inv = sb("lam_inv", [P, 2])

        psum = ctx.enter_context(nc.psum_tensor("psum", [P, 8, S], F32))

        def sem(name):
            return ctx.enter_context(nc.semaphore(name))

        raw_loaded = [sem(f"raw_loaded{i}") for i in range(RAW)]
        whi_done = sem("whi_done")
        wlo_done = sem("wlo_done")
        out_done = sem("out_done")
        bank_free = sem("bank_free")
        gate_done = sem("gate_done")
        tap_done = sem("tap_done")
        sqv_done = sem("sqv_done")
        ss_done = sem("ss_done")
        val_done = sem("val_done")
        hi_done = sem("hi_done")
        rhs_ready = sem("rhs_ready")
        x_done = sem("x_done")
        x_pool = sem("x_pool")
        sqa_done = sem("sqa_done")
        aux_done = sem("aux_done")
        ln_done = sem("ln_done")
        rstd_done = sem("rstd_done")
        ada_loaded = [sem(f"ada_loaded{i}") for i in range(2)]
        ada_scaled = sem("ada_scaled")
        ada_used = sem("ada_used")
        acc_free = sem("acc_free")
        mod_done = sem("mod_done")
        gains_done = sem("gains_done")
        c_step = sem("c_step")
        c_done = sem("c_done")
        act_settled = sem("act_settled")
        dve_settled = sem("dve_settled")
        x_loaded = [sem(f"x_loaded{c}") for c in range(DT)]
        par_loaded = sem("par_loaded")
        con_loaded = sem("con_loaded")
        rope_loaded = sem("rope_loaded")
        const_done = sem("const_done")
        small_done = sem("small_done")
        lam_done = sem("lam_done")
        out_stored = sem("out_stored")
        rot_done = sem("rot_done")
        rope_mul = sem("rope_mul")
        rope_done = sem("rope_done")
        vt_done = sem("vt_done")
        v_done = sem("v_done")
        fg_turned = sem("fg_turned")
        fg_step = sem("fg_step")
        fg_exp = sem("fg_exp")
        logf_done = sem("logf_done")
        cum_psum = sem("cum_psum")
        cum_done = sem("cum_done")
        names = ("scores", "masked", "maxed", "negmax", "exp", "inv", "prob", "turned", "pt", "pv", "o_copied",
                 "o_sq", "o_ss", "o_free", "o_rstd", "o_val", "shifted", "lam")
        att = {a: {n: sem(f"{a}_{n}") for n in names} for a in ATTN}

        def col(name, i=0, n=1):
            return par[:, COLS[name] + i:COLS[name] + i + n]

        def cst(name, n, i=0, rows=P):
            return con[0:rows, CONST[name] + i:CONST[name] + i + n]

        ident = cst("ident", 128)
        GAIN = dict(g_m0=0, r_m0=1, g_f0=2, r_f0=3, g_kv=4, g_m1=5, r_m1=6, g_f1=7)
        r_f1 = sb("r_f1", [P, DT])

        def gain_of(name, c):
            if name == "r_f1":
                return r_f1[:, c:c + 1]
            if name in GAIN:
                return gains[:, GAIN[name], c:c + 1]
            return col(name, c)

        def operand(name):
            return dict(h=(h_hi, h_lo), hid=(hid_hi, hid_lo), latent=(latent_hi, latent_lo))[name]

        def stored(name, i):
            if name == "kv_a":
                return scratch[:, 3 + i, :] if i < 2 else proj[:, 20, :]
            return tile_of(dict(proj=proj, scratch=scratch, x=x, y=y)[name], i)

        def score_bank(name, i, m):
            return 2 * (i % 2) + m if name == "diff" else i % 4

        def exp_tile(name, i, m):
            return scratch[:, 2 * (i % 2) + m if name == "diff" else i % 6, :]

        def prob_tile(name, i):
            return scratch[:, (4, 5, 9)[i % 3], :] if name == "diff" else exp_tile(name, i, 0)

        def turned_tile(i):
            return scratch[:, 6 + i % 3, :]

        def out_bank(name, t):
            return O_BANK if name == "diff" else (O_BANK, AUX_BANK)[t % 2]

        head_out, head_sq = proj[:, 18, :], proj[:, 19, :]

        def square_tiles(s):
            return [scratch[:, i, :] for i in ((5, 6) if s["kind"] == "sumsq" else (5, 6, 7, 8))]

        def wait_x(eng, s, c):
            if not s.get("pool"):
                eng.wait_ge(x_done, s["at"]["xup"] + c + 1)
            elif c % 2 == 0:
                eng.wait_ge(x_pool, s["at"]["xpool"] + c // 2 + 1)
            else:
                eng.wait_ge(x_done, s["at"]["xup"] + c // 2 + 1)

        block = ctx.enter_context(nc.Block())

        @block.sync
        def _(sp):
            for c in range(DT):
                sp.dma_start(x[:, c, :], xT[c]).then_inc(x_loaded[c], 16)
                if c == 1:
                    sp.dma_start(par[:, :], params).then_inc(par_loaded, 16)
            for n in range(RAW):
                sp.dma_start(w_raw[:, n, :], wstream[n]).then_inc(raw_loaded[n], 16)
            sp.dma_start(con[:, :], consts).then_inc(con_loaded, 16)

            def load(n, slot):
                sp.wait_ge(wlo_done, n + 1 - RAW)
                src = wstream[n] if isinstance(n, int) else wstream[bass.ds(n, 1)].rearrange("a p m -> (a p) m")
                sp.dma_start(w_raw[:, slot, :], src).then_inc(raw_loaded[slot], 16)

            with sp.Fori(1, NB // RAW) as i:
                for j in range(RAW):
                    load(RAW * i + j, j)
            for n in range(NB // RAW * RAW, NB):
                load(n, n % RAW)
            for s in PLAN:
                if s["kind"] == "update" and s["last"]:
                    for c in range(DT):
                        wait_x(sp, s, c)
                        sp.dma_start(outT[c], x[:, c, :]).then_inc(out_stored, 16)
            sp.wait_ge(out_stored, 16 * DT)

        @block.gpsimd
        def _(pool):
            def load(v, half):
                src = ada[v] if isinstance(v, int) else ada[bass.ds(v, 1)].rearrange("a p m -> (a p) m")
                pool.dma_start(ada_raw[:, 2 * half:2 * half + 2, :].rearrange("p a n -> p (a n)"), src)\
                    .then_inc(ada_loaded[half], 16)

            load(0, 0)
            load(1, 1)
            pool.wait_ge(c_done, 1)

            def groups(i, n, last):
                for v in range(4 * n):
                    g, acc = v // 4, ada_acc[:, v // 4, :]
                    if v % 4 == 0:
                        pool.wait_ge(acc_free, ACCS * i + g + 1)
                    pool.wait_ge(ada_loaded[v % 2], 16 * (2 * ACCS * i + v // 2 + 1))
                    for u in range(2 * v, 2 * v + 2):
                        k = u % DT
                        row = ada_raw[:, u % ADA_SLOTS, :]
                        c_k = c_act[:, k:k + 1].broadcast_to([P, ADA_COLS])
                        if k == 0:
                            pool.tensor_tensor(acc, row, c_k, ALU.mult).then_inc(ada_used, 1)
                        else:
                            pool.tensor_tensor(row, row, c_k, ALU.mult).then_inc(ada_scaled, 1)
                            pool.wait_ge(ada_scaled, (DT - 1) * (ACCS * i + g) + k)
                            pool.wait_ge(ada_used, ACCS * DT * i + u)
                            pool.tensor_tensor(acc, acc, row, ALU.add).then_inc(ada_used, 1)
                    if not (last and v >= 4 * n - 2):
                        pool.wait_ge(ada_used, ACCS * DT * i + 2 * v + 2)
                        pool.wait_ge(c_done, 1)
                        load(4 * ACCS * i + (v + 2), v % 2)

            with pool.Fori(0, ADA_GROUPS // ACCS) as i:
                groups(i, ACCS, False)
            assert ADA_GROUPS % ACCS == 1
            groups(ADA_GROUPS // ACCS, 1, True)
            for s in PLAN:
                if s["kind"] == "update" and s["pool"]:
                    for c in range(0, DT, 2):
                        pool.wait_ge(val_done, s["at"]["val"] + c + 1)
                        pool.tensor_tensor(x[:, c, :], x[:, c, :], y[:, c, :], ALU.add).then_inc(x_pool, 1)

        @block.scalar
        def _(act):
            act.preload_act_table_set("natural_log_exp_and_others")
            act.wait_ge(const_done, 7)

            def split_hi(m_rounds, slot, out_wait):
                if out_wait is not None:
                    act.wait_ge(out_done, out_wait)
                act.wait_ge(raw_loaded[slot], 16 * m_rounds)
                act.activation(w_hi[:, slot, :], w_raw[:, slot, :], ACT.Copy).then_inc(whi_done, 1)

            def gemm(s, last):
                at_ = s["at"]
                evac = s["evac"]
                hi_out = operand("hid")[0]
                if evac == "acc" and s["sq"]:
                    act.preload_act_table_set("natural_log_exp_and_others")

                def step(t):
                    if not (last and isinstance(t.n, int) and t.n + AHEAD >= NB):
                        split_hi(t.rounds(AHEAD, RAW), (t.n0 + AHEAD) % SPLIT,
                                 None if isinstance(t.o, int) and t.o == 0 else t.o)
                    bank = psum[:, t.o0 % BANKS, :]
                    if evac == "gateup" and t.j % 2 == 0:
                        f = t.of(2)
                        act.wait_ge(out_done, t.o + 1)
                        act.wait_ge(bank_free, BANKS + t.o - 2)
                        act.activation(scratch[:, 2 + t.j // 2 % 2, :], bank, ACT.Silu).then_inc(gate_done, 1)
                    if evac == "gateup" and t.j % 2 == 1:
                        act.wait_ge(bank_free, BANKS + t.o + 1)
                        act.activation(tile_of(hi_out, t.of(2)), scratch[:, 8, :], ACT.Copy).then_inc(hi_done, 1)
                    if evac == "relu2":
                        act.wait_ge(out_done, t.o + 1)
                        act.wait_ge(bank_free, BANKS + t.o - 1)
                        act.activation(scratch[:, 2 + t.j % 2, :], bank, ACT.Relu).then_inc(gate_done, 1)
                        act.wait_ge(bank_free, BANKS + t.o + 1)
                        act.activation(tile_of(hi_out, t.b), scratch[:, 8, :], ACT.Copy).then_inc(hi_done, 1)
                    if evac == "conv" and t.j % 3 == 0:
                        act.wait_ge(out_done, t.o + 1)
                        act.wait_ge(bank_free, BANKS + t.o - 1)
                        act.activation(scratch[:, 2, :], bank, ACT.Copy).then_inc(gate_done, 1)
                    if evac == "conv" and t.j % 3 == 2:
                        act.wait_ge(bank_free, BANKS + t.o + 1)
                        act.activation(tile_of(hi_out, t.of(3)), scratch[:, 8, :], ACT.Copy).then_inc(hi_done, 1)

                steps(act, s, step, last)

            def squares(s, src, src_at, nch, of_x=False):
                for c in range(nch):
                    if s is PLAN[0] and c == 2:
                        act.wait_ge(par_loaded, 16)
                        act.activation(c_exp[:, :], col("c", 0, 8), ACT.Exp, scale=-1.0).then_inc(c_step, 1)
                    if of_x:
                        wait_x(act, s, c)
                    ring = len(square_tiles(s))
                    if c >= ring:
                        act.wait_ge(aux_done, s["at"]["aux"] + c - ring + 1)
                    if s["at"]["sqa"] == 0:
                        act.wait_ge(x_loaded[c], 16)
                    act.activation(square_tiles(s)[c % ring], stored(src, src_at + c), ACT.Square)\
                       .then_inc(sqa_done, 1)

            def norm(s):
                hi_out = operand(s["dst"])[0]
                for c in range(s["nch"]):
                    act.wait_ge(val_done, s["at"]["val"] + c + 1)
                    val = scratch[:, 7 + c % 3, :]
                    if s["shift"] is None:
                        act.activation(hi_out[:, s["dst_at"] + c, :], val, ACT.Copy).then_inc(hi_done, 1)
                    else:
                        act.activation(hi_out[:, s["dst_at"] + c, :], val, ACT.Identity,
                                       bias=mod[:, s["shift"] + c:s["shift"] + c + 1]).then_inc(hi_done, 1)

            def attention(s, ending=None):
                name = s["name"]
                a, e = ATTN[name], att[name]
                M, units = a["mats"], a["heads"] * QB
                upt = a["per_tile"] * QB

                def exps(i):
                    W = (i % QB + 1) * P
                    act.wait_ge(e["negmax"], i + 1)
                    for m in range(M):
                        dst = exp_tile(name, i, m)[:, 0:W]
                        src = psum[:, score_bank(name, i, m), 0:W]
                        c = M * (i % 4) + m
                        act.activation(dst, src, ACT.Exp, bias=neg_max[:, c:c + 1], scale=a["scale"],
                                       accum_out=row_sum[:, c:c + 1]).then_inc(e["exp"], 1)

                def take_turned(i):
                    W = (i % QB + 1) * P
                    act.wait_ge(e["turned"], i + 1)
                    if i >= 3:
                        act.wait_ge(e["pv"], i - 2)
                    act.activation(turned_tile(i)[:, 0:W], psum[:, PT_BANK + i % 2, 0:W], ACT.Copy)\
                       .then_inc(e["pt"], 1)

                def finish(t):
                    act.wait_ge(e["pv"], upt * (t + 1))
                    O = psum[:, out_bank(name, t), :]
                    if name != "diff":
                        c = t + (4 if name == "fox" else 0)
                        act.activation(h_hi[:, c, :], O, ACT.Copy).then_inc(hi_done, 1)
                    else:
                        if t >= 1:
                            act.wait_ge(e["o_val"], t)
                        act.activation(head_out, O, ACT.Copy).then_inc(e["o_copied"], 1)
                        act.activation(head_sq, O, ACT.Square).then_inc(e["o_sq"], 1)

                def root(t):
                    act.wait_ge(e["o_ss"], t + 1)
                    act.activation(rstd[:, :], psum[:, AUX_BANK, :], ACT.Ln, bias=eps[EPS1][:, :])\
                       .then_inc(e["o_free"], 1)
                    act.wait_ge(e["o_free"], t + 1)
                    act.activation(rstd[:, :], rstd[:, :], ACT.Exp, scale=-0.5).then_inc(e["o_rstd"], 1)

                def high(t):
                    act.wait_ge(e["o_val"], t + 1)
                    act.activation(h_hi[:, t, :], ss[:, :], ACT.Copy).then_inc(hi_done, 1)

                def due(i, lag):
                    u = i - PV_LAG - lag
                    return u // upt if 0 <= u < units and u % upt == upt - 1 else None

                def outputs(i):
                    if due(i, 1) is not None:
                        finish(due(i, 1))
                    if name == "diff" and due(i, 2) is not None:
                        root(due(i, 2))
                    if name == "diff" and due(i, 3) is not None:
                        high(due(i, 3))

                for i in range(units + PV_LAG + (0 if name == "diff" else 1)):
                    if ending and i < ENDING:
                        ending(i)
                    outputs(i)
                    if 0 <= i - TAKE_LAG < units:
                        take_turned(i - TAKE_LAG)
                    if i < units:
                        exps(i)
                return (lambda i: outputs(units + PV_LAG + i)) if name == "diff" else None

            ending = None
            for idx, s in enumerate(PLAN):
                kind = s["kind"]
                act.drain().then_inc(act_settled, 1)
                act.wait_ge(act_settled, idx + 1)
                if kind == "gemm":
                    gemm(s, idx == LAST_GEMM)
                elif kind == "sumsq":
                    if s["src"] != "x":
                        act.wait_ge(bank_free, BANKS + s["stored_by"])
                    squares(s, s["src"], s["src_at"], s["nch"])
                    if idx == 0:
                        split_hi(1, 0, None)
                elif kind == "rstd":
                    act.wait_ge(aux_done, s["at"]["aux"])
                    act.activation(rstd[:, :], psum[:, AUX_BANK, :], ACT.Ln, bias=eps[s["eps"]][:, :])\
                       .then_inc(ln_done, 1)
                    act.wait_ge(ln_done, s["at"]["rstd"] + 1)
                    act.activation(rstd[:, :], rstd[:, :], ACT.Exp, scale=-0.5).then_inc(rstd_done, 1)
                elif kind == "norm":
                    if s["at"]["rhs"] == 0:
                        split_hi(1, 1, None)
                    norm(s)
                    if s["at"]["rhs"] == 0:
                        split_hi(1, 2, None)
                elif kind in ("final1", "update") and not s.get("last"):
                    squares(s, "x", 0, 8, of_x=True)
                elif kind == "vtrans":
                    base = s["at"]["vt"] - s["first"]
                    for v in range(s["first"], s["upto"]):
                        act.wait_ge(vt_done, base + v + 1)
                        act.activation(vtok[:, v, :, :].rearrange("p a n -> p (a n)"), psum[:, PT_BANK + v % 2, :],
                                       ACT.Copy).then_inc(v_done, 1)
                elif kind == "forget1":
                    act.wait_ge(small_done, 1)
                    act.activation(lam_exp[:, :], lam_sum[:, :], ACT.Exp).then_inc(lam_done, 1)
                    act.wait_ge(fg_step, 1)
                    act.activation(fgate_a[:, :, :], fgate[:, :, :], ACT.Abs).then_inc(fg_exp, 1)
                    act.wait_ge(fg_exp, 1)
                    act.activation(fgate_b[:, :, :], fgate_a[:, :, :], ACT.Exp, scale=-1.0).then_inc(fg_exp, 1)
                    act.wait_ge(fg_exp, 2)
                    act.activation(fgate_a[:, :, :], fgate_b[:, :, :], ACT.Ln, bias=1.0).then_inc(fg_exp, 1)
                elif kind == "forget2":
                    act.wait_ge(rope_done, 8)
                    act.dma_start(con[:, ROPE_AT:CONSTS], rope2).then_inc(rope_loaded, 16)
                elif kind == "attn":
                    ending = attention(s, ending)

        @block.vector
        def _(dve):
            for n, m in mean.items():
                dve.memset(m[:, :], 1.0 / n).then_inc(const_done, 1)
            dve.memset(ones_col[:, :], 1.0).then_inc(const_done, 1)
            for e, t in eps.items():
                dve.memset(t[:, :], e).then_inc(const_done, 1)
            dve.sem_inc(bank_free, BANKS)
            dve.sem_inc(acc_free, ACCS)

            def split_lo(m, slot):
                dve.wait_ge(whi_done, m + 1)
                dve.tensor_tensor(w_lo[:, slot, :], w_raw[:, slot, :], w_hi[:, slot, :].bitcast(F32),
                                  ALU.subtract).then_inc(wlo_done, 1)

            dve.wait_ge(par_loaded, 16)
            dve.wait_ge(c_step, 1)
            dve.tensor_scalar(c_exp[:, :], c_exp[:, :], 1.0, None, ALU.add).then_inc(c_step, 1)
            dve.wait_ge(c_step, 2)
            dve.reciprocal(c_exp[:, :], c_exp[:, :]).then_inc(c_step, 1)
            dve.wait_ge(c_step, 3)
            dve.tensor_tensor(c_act[:, :], col("c", 0, 8), c_exp[:, :], ALU.mult).then_inc(c_done, 1)
            for c in range(DT):
                dve.wait_ge(x_loaded[c], 16)

            def gemm(s, last):
                at_ = s["at"]
                evac = s["evac"]
                lo_out, hi_out = operand("hid")[1], operand("hid")[0]
                more = s.get("more", False)
                if evac == "acc" and s["sq"] and not more:
                    dve.memset(ss[:, :], 0.0).then_inc(ss_done, 1)

                if evac == "conv":
                    dve.memset(conv_u[:, 0:2], 0.0).then_inc(tap_done, 1)
                    dve.wait_ge(tap_done, 1)

                def lo_of(f):
                    dve.wait_ge(hi_done, at_["hi"] + f + 1)
                    dve.tensor_tensor(tile_of(lo_out, f), scratch[:, 8, :], tile_of(hi_out, f).bitcast(F32),
                                      ALU.subtract).then_inc(rhs_ready, 1)

                def step(t):
                    if not (last and isinstance(t.n, int) and t.n + AHEAD >= NB):
                        split_lo(t.n + AHEAD, (t.n0 + AHEAD) % SPLIT)
                    bank = psum[:, t.o0 % BANKS, :]
                    val = scratch[:, 8, :]
                    if evac == "store":
                        for q in range(s["nout"]):
                            dve.wait_ge(out_done, t.o + q + 1)
                            dve.tensor_copy(stored(s["dst"], s["dst_at"] + t.b * s["nout"] + q),
                                            psum[:, (t.o0 + q) % BANKS, :]).then_inc(bank_free, 1)
                    elif evac == "acc":
                        dst = stored(s["dst"], t.b + s.get("dst_at", 0))
                        dve.wait_ge(out_done, t.o + 1)
                        if s["first"]:
                            dve.tensor_copy(dst, bank).then_inc(bank_free, 1)
                        else:
                            dve.tensor_tensor(dst, dst, bank, ALU.add).then_inc(bank_free, 1)
                        if s["sq"]:
                            dve.wait_ge(bank_free, BANKS + t.o + 1)
                            dve.wait_ge(ss_done, at_["ss"] + t.b + (0 if more else 1))
                            dve.tensor_tensor(scratch[:, 4, :], dst, dst, ALU.mult).then_inc(sqv_done, 1)
                            if isinstance(t.b, int) and t.b == s["nblk"] - 1 and not s.get("go_on"):
                                return
                            dve.wait_ge(sqv_done, at_["sqv"] + t.b + 1)
                            dve.tensor_tensor(ss[:, :], ss[:, :], scratch[:, 4, :], ALU.add).then_inc(ss_done, 1)
                    elif evac == "gateup":
                        f = t.of(2)
                        if t.j % 2 == 0:
                            dve.wait_ge(gate_done, at_["gate"] + f + 1)
                            dve.sem_inc(bank_free, 1)
                        else:
                            dve.wait_ge(out_done, t.o + 1)
                            dve.wait_ge(rhs_ready, at_["rhs"] + f)
                            dve.tensor_tensor(val, scratch[:, 2 + t.j // 2 % 2, :], bank, ALU.mult)\
                               .then_inc(bank_free, 1)
                            lo_of(f)
                    elif evac == "relu2":
                        dve.wait_ge(gate_done, at_["gate"] + t.b + 1)
                        dve.wait_ge(rhs_ready, at_["rhs"] + t.b)
                        dve.tensor_tensor(val, scratch[:, 2 + t.j % 2, :], bank, ALU.mult).then_inc(bank_free, 1)
                        lo_of(t.b)
                    elif evac == "conv":
                        f = t.of(3)
                        if t.j % 3 == 0:
                            dve.wait_ge(gate_done, at_["gate"] + f + 1)
                            dve.sem_inc(bank_free, 1)
                        elif t.j % 3 == 1:
                            dve.wait_ge(out_done, t.o + 1)
                            dve.wait_ge(tap_done, at_["tap"] + 1 + 3 * f)
                            dve.tensor_tensor(conv_u[:, 2:S + 2], scratch[:, 2, :], bank, ALU.mult)\
                               .then_inc(bank_free, 1)
                            dve.wait_ge(bank_free, BANKS + t.o + 1)
                            w0 = COLS["conv_w"]
                            tap = at_["tap"] + 1 + 3 * f
                            dve.wait_ge(rhs_ready, at_["rhs"] + f)
                            dve.tensor_scalar(val, conv_u[:, 0:S], col_of(par, w0 + f), col_of(par, COLS["conv_b"] + f),
                                              ALU.mult, ALU.add).then_inc(tap_done, 1)
                            for k in (1, 2):
                                dve.wait_ge(tap_done, tap + k)
                                dve.scalar_tensor_tensor(out=val, in0=conv_u[:, k:S + k],
                                                         scalar=col_of(par, w0 + 8 * k + f), in1=val,
                                                         op0=ALU.mult, op1=ALU.add).then_inc(tap_done, 1)
                        else:
                            dve.wait_ge(out_done, t.o + 1)
                            dve.wait_ge(tap_done, at_["tap"] + 3 * f + 4)
                            dve.tensor_tensor(val, val, bank, ALU.mult).then_inc(bank_free, 1)
                            lo_of(f)

                steps(dve, s, step, last)

            def norm(s):
                hi_out, lo_out = operand(s["dst"])
                at_ = s["at"]

                def value(c):
                    if c >= 3:
                        dve.wait_ge(rhs_ready, at_["rhs"] + c - 2)
                    dve.scalar_tensor_tensor(out=scratch[:, 7 + c % 3, :], in0=stored(s["src"], s["src_at"] + c),
                                             scalar=gain_of(s["gain"], c), in1=rstd[:, :], op0=ALU.mult,
                                             op1=ALU.mult).then_inc(val_done, 1)

                def low(c):
                    d = s["dst_at"] + c
                    dve.wait_ge(hi_done, at_["hi"] + c + 1)
                    val, hi = scratch[:, 7 + c % 3, :], hi_out[:, d, :].bitcast(F32)
                    if s["shift"] is None:
                        dve.tensor_tensor(lo_out[:, d, :], val, hi, ALU.subtract).then_inc(rhs_ready, 1)
                    else:
                        sh = s["shift"] + c
                        dve.scalar_tensor_tensor(out=lo_out[:, d, :], in0=val, scalar=mod[:, sh:sh + 1], in1=hi,
                                                 op0=ALU.add, op1=ALU.subtract).then_inc(rhs_ready, 1)

                for c in range(s["nch"] + 1):
                    if c < s["nch"]:
                        value(c)
                    if c == 1 and at_["rhs"] == 0:
                        split_lo(1, 1)
                    if c >= 1:
                        low(c - 1)

            def update(s):
                def value(c):
                    dve.scalar_tensor_tensor(out=y[:, c, :], in0=y[:, c, :], scalar=gain_of(s["gain"], c),
                                             in1=rstd[:, :], op0=ALU.mult, op1=ALU.mult).then_inc(val_done, 1)

                def plus(c):
                    dve.wait_ge(val_done, s["at"]["val"] + c + 1)
                    dve.tensor_tensor(x[:, c, :], x[:, c, :], y[:, c, :], ALU.add).then_inc(x_done, 1)

                for c in range(DT + 1):
                    if c < DT:
                        value(c)
                    if c >= 1 and not (s["pool"] and (c - 1) % 2 == 0):
                        plus(c - 1)

            def modulated(name, norm_col, scale_col, with_one):
                out = r_f1[:, :] if name == "r_f1" else gains[:, GAIN[name], :]
                g = par[:, norm_col:norm_col + 8]
                dve.scalar_tensor_tensor(out=out, in0=mod[:, scale_col:scale_col + 8], scalar=1.0 if with_one else 0.0,
                                         in1=g, op0=ALU.add, op1=ALU.mult).then_inc(gains_done, 1)

            def rope(s):
                dve.wait_ge(rope_loaded if s["at"]["rope"] >= 8 else con_loaded, 16)
                for r, tile in enumerate(s["tiles"], s["at"]["rope"]):
                    t = proj[:, tile, :]
                    tmp = scratch[:, 8 + r % 2, :]
                    dve.wait_ge(rot_done, r + 1)
                    dve.tensor_tensor(tmp, psum[:, PT_BANK + r % 2, :], cst("sin", 512), ALU.mult)\
                       .then_inc(rope_mul, 1)
                    dve.tensor_tensor(t, t, cst("cos", 512), ALU.mult).then_inc(rope_mul, 1)
                    dve.wait_ge(rope_mul, 2 * (r + 1))
                    dve.tensor_tensor(t, t, tmp, ALU.add).then_inc(rope_done, 1)

            def attention(s, ending=None):
                name = s["name"]
                a, e = ATTN[name], att[name]
                M, units = a["mats"], a["heads"] * QB
                upt = a["per_tile"] * QB
                mask = cst("chunk_mask", 128)

                def unit(i, j):
                    W, Wj = (i % QB + 1) * P, (j % QB + 1) * P
                    new, old = i < units, 0 <= j < units
                    c, cj = M * (i % 4), M * (j % 4)
                    if new:
                        dve.wait_ge(e["scores"], i + 1)
                        rows = [psum[:, score_bank(name, i, m), :] for m in range(M)]
                    if old:
                        dve.wait_ge(e["exp"], M * (j + 1))
                        dve.reciprocal(row_inv[:, cj:cj + M], row_sum[:, cj:cj + M]).then_inc(e["inv"], 1)
                    if new and name == "mla":
                        dve.tensor_tensor(rows[0][:, W - P:W], rows[0][:, W - P:W], mask, ALU.add)\
                           .then_inc(e["masked"], 1)
                    if old:
                        dve.wait_ge(e["inv"], j + 1)
                        if M == 2:
                            dve.tensor_tensor(lam_inv[:, j % 2:j % 2 + 1], row_inv[:, cj + 1:cj + 2], neg_lam[:, :],
                                              ALU.mult).then_inc(e["lam"], 1)
                        if name == "diff" and j >= 3:
                            dve.wait_ge(e["turned"], j - 2)
                        p = prob_tile(name, j)[:, 0:Wj]
                        dve.tensor_scalar(p, exp_tile(name, j, 0)[:, 0:Wj], row_inv[:, cj:cj + 1], None, ALU.mult)\
                           .then_inc(e["prob"], 1)
                    if new:
                        for m in range(M):
                            if name == "mla":
                                dve.wait_ge(e["masked"], i + 1)
                            dve.tensor_reduce(row_max[:, c + m:c + m + 1], rows[m][:, 0:W], AX_X, ALU.max)\
                               .then_inc(e["maxed"], 1)
                    if old and M == 2:
                        dve.wait_ge(e["prob"], 2 * j + 1)
                        dve.wait_ge(e["lam"], j + 1)
                        dve.scalar_tensor_tensor(out=p, in0=exp_tile(name, j, 1)[:, 0:Wj],
                                                 scalar=lam_inv[:, j % 2:j % 2 + 1], in1=p, op0=ALU.mult,
                                                 op1=ALU.add).then_inc(e["prob"], 1)
                    if new:
                        dve.wait_ge(e["maxed"], M * (i + 1))
                        if name == "fox":
                            cum_q = cum_tok[:, i % QB, i // QB:i // QB + 1]
                            dve.tensor_scalar(neg_cum_max[:, c:c + 1], row_max[:, c:c + 1], cum_q, -a["scale"],
                                              ALU.add, ALU.mult).then_inc(e["shifted"], 1)
                            dve.wait_ge(e["shifted"], i + 1)
                            dve.scalar_tensor_tensor(out=neg_max[:, c:c + 1], in0=cum_q, scalar=a["scale"],
                                                     in1=neg_cum_max[:, c:c + 1], op0=ALU.mult, op1=ALU.add)\
                               .then_inc(e["negmax"], 1)
                        else:
                            dve.tensor_scalar(neg_max[:, c:c + M], row_max[:, c:c + M], -a["scale"], None,
                                              ALU.mult).then_inc(e["negmax"], 1)

                def finish(t):
                    c = t + (4 if name == "fox" else 0)
                    dve.wait_ge(hi_done, s["at"]["hi"] + t + 1)
                    dve.tensor_tensor(h_lo[:, c, :], psum[:, out_bank(name, t), :], h_hi[:, c, :].bitcast(F32),
                                      ALU.subtract).then_inc(rhs_ready, 1)

                def value(t):
                    dve.wait_ge(e["o_rstd"], t + 1)
                    dve.wait_ge(rhs_ready, s["at"]["rhs"] + t)
                    dve.scalar_tensor_tensor(out=ss[:, :], in0=head_out, scalar=subln_gain[:, 0:1],
                                             in1=rstd[:, :], op0=ALU.mult, op1=ALU.mult).then_inc(e["o_val"], 1)

                def low(t):
                    dve.wait_ge(hi_done, s["at"]["hi"] + t + 1)
                    dve.tensor_tensor(h_lo[:, t, :], ss[:, :], h_hi[:, t, :].bitcast(F32),
                                      ALU.subtract).then_inc(rhs_ready, 1)

                def due(i, lag):
                    u = i - PV_LAG - lag
                    return u // upt if 0 <= u < units and u % upt == upt - 1 else None

                def outputs(i):
                    if name != "diff" and due(i, 1) is not None:
                        finish(due(i, 1))
                    if name == "diff" and due(i, 3) is not None:
                        low(due(i, 3))
                    if name == "diff" and due(i, 2) is not None:
                        value(due(i, 2))

                for i in range(units + PV_LAG + (0 if name == "diff" else 1)):
                    unit(i, i - PROB_LAG)
                    outputs(i)
                    if ending and i < ENDING:
                        ending(i)
                return (lambda i: outputs(units + PV_LAG + i)) if name == "diff" else None

            def lambdas():
                lam = col("lam", 0, 256).rearrange("p (a b n) -> p a b n", a=2, b=2)
                dve.tensor_tensor(lam_prod[:, :, :], lam[:, :, 0, :], lam[:, :, 1, :], ALU.mult)\
                   .then_inc(gains_done, 1)
                dve.wait_ge(gains_done, 1)
                dve.tensor_reduce(lam_sum[:, :], lam_prod[:, :, :], AX_X, ALU.add).then_inc(small_done, 1)
                dve.tensor_scalar(subln_gain[:, :], col("subln"), 1.0 - LAM_INIT, None, ALU.mult)\
                   .then_inc(gains_done, 1)
                dve.wait_ge(lam_done, 1)
                dve.tensor_tensor(lam_diff[:, :], lam_exp[:, 1:2], lam_exp[:, 0:1], ALU.subtract)\
                   .then_inc(gains_done, 1)
                dve.wait_ge(gains_done, 3)
                dve.tensor_scalar(neg_lam[:, :], lam_diff[:, :], -LAM_INIT, None, ALU.add).then_inc(gains_done, 1)

            NG2 = COLS["norm_g2"]
            ending = None
            for idx, s in enumerate(PLAN):
                kind = s["kind"]
                dve.drain().then_inc(dve_settled, 1)
                dve.wait_ge(dve_settled, idx + 1)
                if kind == "gemm":
                    gemm(s, idx == LAST_GEMM)
                elif kind == "rstd":
                    dve.wait_ge(rstd_done, s["at"]["rstd"] + 1)
                elif kind == "sumsq":
                    if idx == 0:
                        split_lo(0, 0)
                elif kind == "norm":
                    norm(s)
                    if s["at"]["rhs"] == 0:
                        split_lo(2, 2)
                elif kind == "update":
                    update(s)
                elif kind == "final1":
                    for c in range(DT):
                        dve.scalar_tensor_tensor(out=x[:, c, :], in0=x[:, c, :], scalar=col("normf", c),
                                                 in1=rstd[:, :], op0=ALU.mult, op1=ALU.mult).then_inc(x_done, 1)
                    dve.wait_ge(x_done, s["at"]["xup"] + 8)
                elif kind == "take":
                    a, b = MOD_PER_GROUP * s["first"], MOD_PER_GROUP * s["upto"]
                    dve.wait_ge(acc_free, ACCS + s["upto"])
                    dve.tensor_tensor(mod[:, a:b], psum[:, O_BANK, a:b], col("ada_b", a, b - a), ALU.add)\
                       .then_inc(mod_done, 1)
                elif kind == "modcols0":
                    dve.wait_ge(mod_done, s["at"]["take"])
                    modulated("g_m0", NG2 + 0, 8, True)
                    modulated("r_m0", NG2 + 8, 16, False)
                    modulated("g_f0", NG2 + 16, 32, True)
                    modulated("r_f0", NG2 + 24, 40, False)
                    dve.wait_ge(gains_done, 8)
                elif kind == "modcols1":
                    dve.wait_ge(mod_done, s["at"]["take"])
                    modulated("g_kv", COLS["kv_norm"], 56, True)
                    modulated("g_m1", NG2 + 32, 72, True)
                    modulated("r_m1", NG2 + 40, 80, False)
                    modulated("g_f1", NG2 + 48, 96, True)
                    modulated("r_f1", NG2 + 56, 104, False)
                    dve.wait_ge(gains_done, 13)
                elif kind == "rope":
                    rope(s)
                elif kind == "forget1":
                    lambdas()
                    dve.wait_ge(gains_done, 4)
                    dve.wait_ge(fg_turned, 1)
                    turned = psum[:, AUX_BANK, :].rearrange("p (a n) -> p a n", a=QB)
                    for q in range(QB):
                        z = dve.tensor_tensor(fgate[:, q, :], turned[:, q, P - 8:P], col("b_f", 0, 8), ALU.add)
                    z.then_inc(fg_step, 1)
                    dve.wait_ge(fg_exp, 3)
                    dve.scalar_tensor_tensor(out=log_f[:, :, :], in0=fgate[:, :, :], scalar=0.0,
                                             in1=fgate_a[:, :, :], op0=ALU.min, op1=ALU.subtract)\
                       .then_inc(logf_done, 1)
                elif kind == "forget2":
                    for dst, src in ((ident_r, ident), (mask_r["diff"], cst("chunk_mask", P)),
                                     (mask_r["fox"], cst("causal_mask", P)), (heads_r, cst("heads", 8))):
                        dve.tensor_copy(dst, src).then_inc(cum_done, 1)
                    dve.memset(neg_cum[:, :].bitcast(F32), 0.0).then_inc(cum_done, 1)
                    dve.wait_ge(cum_psum, 1)
                    dve.wait_ge(cum_done, 5)
                    dve.tensor_scalar(neg_cum[0:8, :], psum[0:8, AUX_BANK, :], -8.0, None, ALU.mult)\
                       .then_inc(cum_done, 1)
                    dve.wait_ge(cum_done, 6)
                    dve.scalar_tensor_tensor(out=neg_cum[32:40, :], in0=psum[0:8, AUX_BANK, :], scalar=-8.0,
                                             in1=neg_cum[0:8, :].bitcast(F32), op0=ALU.mult, op1=ALU.subtract)\
                       .then_inc(cum_done, 1)
                    dve.wait_ge(cum_psum, 2)
                    dve.tensor_scalar(cum_tok[:, :, :].rearrange("p a n -> p (a n)"), psum[:, O_BANK, 0:8 * QB],
                                      8.0, None, ALU.mult).then_inc(cum_done, 1)
                elif kind == "attn":
                    if s["name"] == "fox":
                        dve.wait_ge(cum_done, 8)
                    ending = attention(s, ending)

        @block.tensor
        def _(pe):
            pe.wait_ge(const_done, 7)

            def keep_warm(n, bank=PT_BANK):
                for _ in range(n):
                    pe.matmul(psum[:, bank, 0:P], mean[128][:, :], mean[128][:, :], start=True, stop=True)

            keep_warm(WARM_START)

            def gemm(s, last):
                hi, lo = operand(s["rhs"])
                nk, ra = s["nk"], s["rhs_at"]

                def step(t):
                    slot = t.n0 % SPLIT
                    pe.wait_ge(wlo_done, t.n + 1)
                    for q in range(s["nout"]):
                        bank = psum[:, (t.o0 + q) % BANKS, :]
                        pe.wait_ge(bank_free, t.o + q + 1)
                        for k in range(nk):
                            if t.j == 0 and q == 0:
                                pe.wait_ge(rhs_ready, s["r0"] + k + 1)
                            w = slice((q * nk + k) * P, (q * nk + k + 1) * P)
                            pe.matmul(bank, w_hi[:, slot, w], hi[:, ra + k, :], start=k == 0, stop=False)
                            pe.matmul(bank, w_hi[:, slot, w], lo[:, ra + k, :], start=False, stop=False)
                            mm = pe.matmul(bank, w_lo[:, slot, w], hi[:, ra + k, :], start=False,
                                           stop=k == nk - 1)
                        mm.then_inc(out_done, 1)

                if not s.get("kouter"):
                    steps(pe, s, step, last)
                    return
                blocks = [Step(s, b, b, 0, 4) for b in range(s["kouter"])]
                for t in blocks:
                    pe.wait_ge(wlo_done, t.n + 1)
                    pe.wait_ge(bank_free, t.o + 1)
                for k in range(nk):
                    pe.wait_ge(rhs_ready, s["r0"] + k + 1)
                    for t in blocks:
                        slot, bank, w = t.n0 % SPLIT, psum[:, t.o0 % BANKS, :], slice(k * P, (k + 1) * P)
                        pe.matmul(bank, w_hi[:, slot, w], hi[:, ra + k, :], start=k == 0, stop=False)
                        pe.matmul(bank, w_hi[:, slot, w], lo[:, ra + k, :], start=False, stop=False)
                        mm = pe.matmul(bank, w_lo[:, slot, w], hi[:, ra + k, :], start=False, stop=k == nk - 1)
                        if k == nk - 1:
                            mm.then_inc(out_done, 1)
                steps(pe, s, step, last, done=s["kouter"])

            def sum_squares(s, nch, n):
                pe.wait_ge(rstd_done, s["at"]["rstd"])
                tiles = square_tiles(s)
                for c in range(nch):
                    pe.wait_ge(sqa_done, s["at"]["sqa"] + c + 1)
                    pe.matmul(psum[:, AUX_BANK, :], mean[n][:, :], tiles[c % len(tiles)], start=c == 0,
                              stop=c == nch - 1).then_inc(aux_done, 1)

            def rope(s):
                pe.wait_ge(bank_free, BANKS + s["stored_by"])
                pe.wait_ge(rope_loaded if s["at"]["rope"] >= 8 else con_loaded, 16)
                if s["at"]["vt"]:
                    pe.wait_ge(v_done, s["at"]["vt"])
                for r, tile in enumerate(s["tiles"], s["at"]["rope"]):
                    if r >= 2:
                        pe.wait_ge(rope_done, r - 1)
                    pe.matmul(psum[:, PT_BANK + r % 2, :], cst("rot", 128), proj[:, tile, :], start=True,
                              stop=True).then_inc(rot_done, 1)

            def attention(s, ending=None):
                name = s["name"]
                a, e = ATTN[name], att[name]
                M, units = a["mats"], a["heads"] * QB
                upt = a["per_tile"] * QB

                def scores(i):
                    h, q = divmod(i, QB)
                    W = (q + 1) * P
                    rows = slice(q * P, (q + 1) * P)
                    ring = 2 if name == "diff" else 4
                    if i >= ring:
                        pe.wait_ge(e["exp"], M * (i - ring + 1))
                    keep_warm(WARM_UNIT[name], score_bank(name, i, 0))
                    for m in range(M):
                        out = psum[:, score_bank(name, i, m), 0:W]
                        if name == "diff":
                            half = slice(64 * m, 64 * m + 64)
                            pe.matmul(out, proj[half, h, rows], proj[half, 4 + h, 0:W], start=True, stop=False)
                            mm = pe.matmul(psum[:, score_bank(name, i, m), W - P:W], ident_r, mask_r[name],
                                           start=False, stop=True)
                        elif name == "fox":
                            half = slice(64 * (h % 2), 64 * (h % 2) + 64)
                            pe.matmul(out, proj[half, 8 + h // 2, rows], proj[half, 12 + h // 2, 0:W],
                                      start=True, stop=False)
                            pe.matmul(out, heads_r[:, h:h + 1].broadcast_to([P, P]), neg_cum[:, 0:W],
                                      start=False, stop=False)
                            mm = pe.matmul(psum[:, score_bank(name, i, m), W - P:W], ident_r, mask_r[name],
                                           start=False, stop=True)
                        else:
                            half = slice(64 * (h % 2), 64 * (h % 2) + 64)
                            pe.matmul(out, proj[:, 8 + h, rows], proj[:, h, 0:W], start=True, stop=False)
                            mm = pe.matmul(out, proj[half, 16 + h // 2, rows], proj[half, 20, 0:W], start=False,
                                           stop=True)
                    mm.then_inc(e["scores"], 1)

                def turn(i):
                    q = i % QB
                    pe.wait_ge(e["prob"], M * (i + 1))
                    if i >= 2:
                        pe.wait_ge(e["pt"], i - 1)
                    for kb in range(q + 1):
                        mm = pe.transpose(psum[:, PT_BANK + i % 2, kb * P:(kb + 1) * P],
                                          prob_tile(name, i)[:, kb * P:(kb + 1) * P], ident)
                    mm.then_inc(e["turned"], 1)

                def values(i):
                    h, q = divmod(i, QB)
                    pe.wait_ge(e["pt"], i + 1)
                    t = i // upt
                    if i == 0 and name == "fox":
                        pe.wait_ge(att["diff"]["o_sq"], 4)
                    if i == upt and name == "fox":
                        pe.wait_ge(att["diff"]["o_free"], 4)
                    if i % upt == 0 and name == "diff" and t >= 1:
                        pe.wait_ge(e["o_sq"], t)
                    if i % upt == 0 and name != "diff" and t >= 2:
                        pe.wait_ge(rhs_ready, s["at"]["rhs"] + t - 1)
                    for kb in range(q + 1):
                        if name == "fox":
                            c = 64 * (h % 2)
                            v, rows = vtok[:, 4 + h // 2, kb, c:c + 64], slice(c, c + 64)
                        else:
                            v, rows = vtok[:, h, kb, :], slice(0, P)
                        mm = pe.matmul(psum[rows, out_bank(name, t), q * P:(q + 1) * P], v,
                                       turned_tile(i)[:, kb * P:(kb + 1) * P], start=kb == 0, stop=kb == q)
                    mm.then_inc(e["pv"], 1)

                def head_square(t):
                    pe.wait_ge(e["o_sq"], t + 1)
                    if t >= 1:
                        pe.wait_ge(e["o_free"], t)
                    pe.matmul(psum[:, AUX_BANK, :], mean[128][:, :], head_sq, start=True,
                              stop=True).then_inc(e["o_ss"], 1)

                def outputs(i):
                    u = i - PV_LAG - 1
                    if name == "diff" and 0 <= u < units and u % upt == upt - 1:
                        head_square(u // upt)

                for i in range(units + PV_LAG):
                    if i < units:
                        scores(i)
                    if 0 <= i - PV_LAG < units:
                        values(i - PV_LAG)
                    if 0 <= i - TURN_LAG < units:
                        turn(i - TURN_LAG)
                    outputs(i)
                    if ending and i < ENDING:
                        ending(i)
                return (lambda i: outputs(units + PV_LAG + i)) if name == "diff" else None

            ending = None
            for idx, s in enumerate(PLAN):
                kind = s["kind"]
                if kind == "gemm":
                    gemm(s, idx == LAST_GEMM)
                elif kind == "sumsq":
                    sum_squares(s, s["nch"], s["mean"])
                    keep_warm(WARM if idx == 0 else 0)
                elif kind in ("final1", "update") and not s.get("last"):
                    sum_squares(s, 8, 1024)
                    keep_warm(WARM)
                elif kind == "total":
                    pe.wait_ge(rstd_done, s["at"]["rstd"])
                    pe.wait_ge(ss_done, s["at"]["ss"])
                    pe.matmul(psum[:, AUX_BANK, :], mean[1024][:, :], ss[:, :], start=True, stop=False)
                    pe.wait_ge(sqv_done, s["at"]["sqv"])
                    pe.matmul(psum[:, AUX_BANK, :], mean[1024][:, :], scratch[:, 4, :], start=False, stop=True)\
                      .then_inc(aux_done, 1)
                    keep_warm(WARM if idx + 2 < len(PLAN) else 0)
                elif kind == "mod":
                    if s["at"]["take"]:
                        pe.wait_ge(mod_done, s["at"]["take"])
                    if s["after"] == "attn":
                        pe.wait_ge(rhs_ready, s["at"]["rhs"])
                    for g in range(s["at"]["mod"], s["at"]["mod"] + s["groups"]):
                        pe.wait_ge(ada_used, DT * (g + 1))
                        for m in range(MOD_PER_GROUP):
                            c = g * MOD_PER_GROUP + m
                            mm = pe.matmul(psum[:, O_BANK, c:c + 1], ada_acc[:, g % ACCS, m * P:(m + 1) * P],
                                           ones_col[:, :], start=True, stop=True)
                        mm.then_inc(acc_free, 1)
                elif kind == "rope":
                    rope(s)
                elif kind == "vtrans":
                    pe.wait_ge(bank_free, BANKS + s["stored_by"])
                    pe.wait_ge(rope_done, s["at"]["rope"])
                    base = s["at"]["vt"] - s["first"]
                    for v in range(s["first"], s["upto"]):
                        if base + v >= 2:
                            pe.wait_ge(v_done, base + v - 1)
                        for kb in range(QB):
                            mm = pe.transpose(psum[:, PT_BANK + v % 2, kb * P:(kb + 1) * P],
                                              scratch[:, v, kb * P:(kb + 1) * P], ident)
                        mm.then_inc(vt_done, 1)
                elif kind == "forget1":
                    pe.wait_ge(bank_free, BANKS + s["at"]["o"])
                    for kb in range(QB):
                        mm = pe.transpose(psum[:, AUX_BANK, kb * P:(kb + 1) * P], proj[:, 16, kb * P:(kb + 1) * P],
                                          ident)
                    mm.then_inc(fg_turned, 1)
                elif kind == "forget2":
                    pe.wait_ge(logf_done, 1)
                    for kb in range(QB):
                        mm = pe.matmul(psum[0:8, AUX_BANK, kb * P:S], log_f[:, kb, :], cst("tri", S - kb * P),
                                       start=kb == 0, stop=kb == QB - 1)
                    mm.then_inc(cum_psum, 1)
                    pe.wait_ge(mod_done, s["at"]["take"])
                    for q in range(QB):
                        for kb in range(q + 1):
                            mm = pe.matmul(psum[:, O_BANK, 8 * q:8 * q + 8], cst("tri", P, (q - kb) * P),
                                           log_f[:, kb, :], start=kb == 0, stop=kb == q)
                    mm.then_inc(cum_psum, 1)
                elif kind == "attn":
                    pe.wait_ge(bank_free, BANKS + s["at"]["o"])
                    pe.wait_ge(v_done, s["at"]["vt"])
                    pe.wait_ge(rope_done, s["at"]["rope"])
                    pe.wait_ge(mod_done, s["at"]["take"])
                    pe.wait_ge(cum_done, 8)
                    ending = attention(s, ending)


def lay_out(inp):
    f = {k: np.asarray(v) for k, v in inp.items()}
    blocks = []

    def tiles(w):
        K, M = w.shape
        return w.reshape(K // P, P, M // P, P).transpose(2, 1, 0, 3).reshape(M // P, P, K)

    def push(t, per=1):
        n = t.shape[0] // per
        t = t.reshape(n, per, P, -1).transpose(0, 2, 1, 3).reshape(n, P, -1)
        full = np.zeros((n, P, D), np.float32)
        full[:, :, :t.shape[2]] = t
        blocks.append(full)

    w = f["w_in"][0]
    push(tiles(w[:, 0:1024]))
    push(tiles(w[:, 1536:2560]))
    push(tiles(w[:, w.shape[1] - P:]))
    push(tiles(w[:, 1024:1536]))
    push(tiles(w[:, 2560:3072]))
    push(tiles(f["w_out"][0]))
    gate, up = tiles(f["w_gate"][0]), tiles(f["w_up"][0])
    for c, nk in ((0, 8), (8, 8), (16, 6)):
        push(np.stack([gate[c:c + nk], up[c:c + nk]], 1).reshape(2 * nk, P, D))
        push(tiles(f["w_down"][0][c * P:(c + nk) * P]))
    b, c, xh = (tiles(f["conv_in_w_2"][0][:, i * D:(i + 1) * D]) for i in range(3))
    push(np.stack([c, xh, b], 1).reshape(24, P, D))
    push(tiles(f["conv_out_w_2"][0]))

    def mlp(l):
        for g in range(4):
            push(tiles(f["mlp_up_w_2"][l][:, g * D:(g + 1) * D]))
            push(tiles(f["mlp_down_w_2"][l][g * D:(g + 1) * D]))

    mlp(0)
    w = f["kv_a_w_2"]
    push(tiles(w[:, 0:256]))
    push(tiles(np.concatenate([w[:, 256:320], w[:, 256:320]], 1)))
    push(tiles(f["q_a_w_2"][0]))
    w = f["kv_b_w_2"].reshape(256, 8, 2, P)
    push(tiles(w[:, :, 0].reshape(256, D)), 4)
    push(tiles(w[:, :, 1].reshape(256, D)), 4)
    w = f["q_b_w_2"][0].reshape(384, 8, 192)
    push(tiles(np.concatenate([w[:, :, P:].reshape(384, 512), w[:, :, 0:P].reshape(384, D)], 1)), 2)
    push(tiles(f["attn_o_w_2"][0]))
    mlp(1)
    wstream = np.concatenate(blocks, 0)
    assert wstream.shape[0] == NB, (wstream.shape, NB)

    ada = np.concatenate([f["ada_w_2"][0], f["kv_ada_w_2"], f["ada_w_2"][1]], 1)
    ada = ada.reshape(DT, P, ADA_GROUPS, ADA_COLS)
    ada = ada.transpose(2, 0, 1, 3).reshape(ADA_GROUPS * DT // 2, 2, P, ADA_COLS).transpose(0, 2, 1, 3)
    ada = ada.reshape(ADA_GROUPS * DT // 2, P, 2 * ADA_COLS)

    def cols(v):
        return np.asarray(v).reshape(-1, P).T

    def rows(v):
        v = np.asarray(v).reshape(1, -1)
        return np.broadcast_to(v, (P, v.shape[1]))

    params = np.concatenate([
        cols(f["norm1_g"]), cols(f["norm2_g"]), cols(f["normf_g"]), cols(f["norm_g_2"]), cols(f["kv_norm_g_2"]),
        cols(f["kv_a_norm_g_2"]), cols(f["q_a_norm_g_2"]), cols(f["subln_g"]), cols(f["conv_w_2"]),
        cols(f["conv_b_2"]), cols(np.concatenate([f["ada_b_2"][0], f["kv_ada_b_2"], f["ada_b_2"][1]])),
        cols(f["c_2"]), rows(f["b_f"]), rows(np.concatenate([f["lam_q1"], f["lam_k1"], f["lam_q2"], f["lam_k2"]])),
    ], 1)
    xT = f["x"][0].T.reshape(DT, P, S)
    return xT, wstream, ada, params


def constants():
    q, k = np.arange(P)[:, None], np.arange(P)[None, :]
    ident = np.eye(P)
    tri = np.concatenate([(q <= k) * 1.0, np.ones((P, S - P))], 1)
    chunk_mask = np.where(k // 64 <= q // 64, 0.0, NEG)
    causal_mask = np.where(k <= q, 0.0, NEG)

    def rotary(dim, theta):
        half = dim // 2
        inv = np.float32(theta) ** (-np.arange(0, dim, 2, dtype=np.float32) / np.float32(dim))
        ang = np.arange(S, dtype=np.float32)[None, :] * inv.astype(np.float32)[:, None]
        cos, sin = np.ones((64, S)), np.zeros((64, S))
        rot = np.zeros((64, 64))
        for i in range(half):
            cos[i] = cos[i + half] = np.cos(ang[i])
            sin[i] = sin[i + half] = np.sin(ang[i])
            rot[i + half, i] = -1.0
            rot[i, i + half] = 1.0
        two = np.zeros((P, P))
        two[:64, :64] = two[64:, 64:] = rot
        return [two, np.tile(cos, (2, 1)), np.tile(sin, (2, 1))]

    heads = (q % 32 == np.arange(8)[None, :]) * (q < 64) * 1.0
    first = np.concatenate([ident, tri, chunk_mask, causal_mask, heads] + rotary(16, 500000.0), 1)
    return first.astype(np.float32), np.concatenate(rotary(64, 10000.0), 1).astype(np.float32)


def kernel(**inputs):
    import concourse.bacc as bacc
    from concourse.bass_utils import run_bass_kernel_spmd as run

    xT, wstream, ada, params = lay_out(inputs)
    consts, rope2 = constants()
    arrays = dict(xT=xT, wstream=wstream, ada=ada, params=params, consts=consts, rope2=rope2)
    arrays = {f"in_{k}": np.ascontiguousarray(v) for k, v in arrays.items()}
    nc = bacc.Bacc("TRN2", target_bir_lowering=False, num_devices=1)
    args = [nc.dram_tensor(k, v.shape, F32, kind="ExternalInput").ap() for k, v in arrays.items()]
    args.append(nc.dram_tensor("outT", (DT, P, S), F32, kind="ExternalOutput").ap())
    build(nc, *args)
    r = run(nc, [arrays], core_ids=[0])
    return np.asarray(r.results[0]["outT"]).reshape(D, S).T.reshape(1, S, D)
```
